# Optimizing a Trainium2 kernel written in Bass

```python
import math
import jax
import jax.numpy as jnp
from jax import lax
import numpy as np

D_MODEL = 1024
BATCH = 1
SEQ = 256
DEPTH = 2

CHUNK = 64
Q_BLOCK = 128
HEAD_DIM = 64
ROPE_THETA = 10000.0
EPS = 1e-6
A_HEADS = 4
A_VDIM = 2 * HEAD_DIM
B_HEADS = 8
C_CHANNELS = 512
CONV_WIDTH = 31
D_HEADS = 8
LEFT_CHUNKS = 8
BAND_CHUNKS = LEFT_CHUNKS + 1
BAND = BAND_CHUNKS * CHUNK
MAX_REL = 128
D_FF = 2816
N_EXPERTS = 8
TOP_K = 2
D_FF_EXPERT = 3584
N_PAIR = DEPTH // 2

A_QK = A_HEADS * 2 * HEAD_DIM
A_V = A_HEADS * A_VDIM
B_W = B_HEADS * HEAD_DIM
D_W = D_HEADS * HEAD_DIM
EVEN_SPLITS = (A_QK, A_QK, A_V, B_W, B_W, B_W)
ODD_SPLITS = (C_CHANNELS, C_CHANNELS, D_W, D_W, D_W)
EVEN_IN = sum(EVEN_SPLITS)
ODD_IN = sum(ODD_SPLITS)
EVEN_MIX = A_V + B_W
ODD_MIX = C_CHANNELS + D_W

kernel_name = 'hybrid_streaming_diff_stickbreak_conformer_moe'

def _split(a, widths):
    cuts = [int(c) for c in np.cumsum(widths)[:-1]]
    return jnp.split(a, cuts, axis=-1)

def rmsnorm(x, g):
    xf = x.astype(jnp.float32)
    y = xf * lax.rsqrt(jnp.mean(xf * xf, axis=-1, keepdims=True) + EPS)
    return (y * g.astype(jnp.float32)).astype(x.dtype)

def layernorm(x, g, b):
    xf = x.astype(jnp.float32)
    mu = jnp.mean(xf, axis=-1, keepdims=True)
    xc = xf - mu
    var = jnp.mean(xc * xc, axis=-1, keepdims=True)
    return (xc * lax.rsqrt(var + EPS) * g.astype(jnp.float32) + b.astype(jnp.float32)).astype(x.dtype)

def rope(x):
    s, d = x.shape[1], x.shape[-1]
    half = d // 2
    inv_freq = ROPE_THETA ** (-jnp.arange(half, dtype=jnp.float32) * 2.0 / d)
    ang = jnp.arange(s, dtype=jnp.float32)[:, None] * inv_freq[None, :]
    cos = jnp.cos(ang)[None, :, None, :]
    sin = jnp.sin(ang)[None, :, None, :]
    xf = x.astype(jnp.float32)
    x1, x2 = xf[..., :half], xf[..., half:]
    return jnp.concatenate([x1 * cos - x2 * sin, x2 * cos + x1 * sin], axis=-1).astype(x.dtype)

def _block_split(a):
    b, s = a.shape[:2]
    return a.reshape(b, s // Q_BLOCK, Q_BLOCK, *a.shape[2:]).swapaxes(0, 1)

def _block_merge(a):
    nb, b, qb = a.shape[:3]
    return a.swapaxes(0, 1).reshape(b, nb * qb, *a.shape[3:])

def diff_attention(q, k, v, lam):
    b, s = q.shape[:2]
    scale = HEAD_DIM ** -0.5
    key_chunk = jnp.arange(s) // CHUNK

    def block(args):
        qb, start = args
        q_chunk = (start + jnp.arange(Q_BLOCK)) // CHUNK
        mask = key_chunk[None, :] <= q_chunk[:, None]
        scores = jnp.einsum('bqhd,bkhd->bhqk', qb, k, preferred_element_type=jnp.float32) * scale
        p = jax.nn.softmax(jnp.where(mask, scores, -jnp.inf), axis=-1)
        p = p.reshape(b, A_HEADS, 2, Q_BLOCK, s)
        p_diff = p[:, :, 0] - lam * p[:, :, 1]
        return jnp.einsum('bhqk,bkhd->bqhd', p_diff, v).astype(v.dtype)

    starts = jnp.arange(s // Q_BLOCK) * Q_BLOCK
    return _block_merge(lax.map(block, (_block_split(q), starts)))

def stick_breaking(q, k, v):
    b, s = q.shape[:2]
    scale = HEAD_DIM ** -0.5
    key_pos = jnp.arange(s)

    def block(args):
        qb, start = args
        q_pos = start + jnp.arange(Q_BLOCK)
        mask = key_pos[None, :] < q_pos[:, None]
        z = jnp.einsum('bqhd,bkhd->bhqk', qb, k, preferred_element_type=jnp.float32) * scale
        log_1m_beta = jnp.where(mask, jax.nn.log_sigmoid(-z), 0.0)
        rev = lax.cumsum(log_1m_beta, axis=3, reverse=True)
        after = jnp.pad(rev[..., 1:], ((0, 0), (0, 0), (0, 0), (0, 1)))
        weights = jnp.where(mask, jnp.exp(jax.nn.log_sigmoid(z) + after), 0.0)
        return jnp.einsum('bhqk,bkhd->bqhd', weights, v).astype(v.dtype)

    starts = jnp.arange(s // Q_BLOCK) * Q_BLOCK
    return _block_merge(lax.map(block, (_block_split(q), starts)))

def _rel_index():
    iq = np.arange(CHUNK)[:, None]
    key_off = np.arange(BAND)[None, :] - LEFT_CHUNKS * CHUNK
    return np.clip(iq - key_off, -MAX_REL, MAX_REL) + MAX_REL

def chunk_rel_attention(q, k, v, rel_table):
    b, s, h, dh = q.shape
    nc = s // CHUNK

    def band(a):
        a = a.reshape(b, nc, CHUNK, h, dh)
        a = jnp.pad(a, ((0, 0), (LEFT_CHUNKS, 0), (0, 0), (0, 0), (0, 0)))
        return jnp.stack([a[:, i:i + nc] for i in range(BAND_CHUNKS)], axis=2).reshape(b, nc, BAND, h, dh)

    k_band, v_band = band(k), band(v)
    qc = q.reshape(b, nc, CHUNK, h, dh)
    scores = jnp.einsum('bcqhd,bckhd->bhcqk', qc, k_band, preferred_element_type=jnp.float32) * (dh ** -0.5)
    bias = rel_table.astype(jnp.float32)[:, _rel_index()]
    scores = scores + bias[None, :, None]
    key_chunk = jnp.arange(nc)[:, None] - LEFT_CHUNKS + (jnp.arange(BAND) // CHUNK)[None, :]
    valid = (key_chunk >= 0)[:, None, :]
    p = jax.nn.softmax(jnp.where(valid, scores, -jnp.inf), axis=-1)
    out = jnp.einsum('bhcqk,bckhd->bcqhd', p, v_band)
    return out.reshape(b, s, h, dh).astype(q.dtype)

def even_mixer(h, w_in, lq1, lk1, lq2, lk2, subln_g, w_out, lambda_init):
    b, s, _ = h.shape
    qa, ka, va, qb, kb, vb = _split(h @ w_in, EVEN_SPLITS)
    qa = rope(qa.reshape(b, s, 2 * A_HEADS, HEAD_DIM))
    ka = rope(ka.reshape(b, s, 2 * A_HEADS, HEAD_DIM))
    va = va.reshape(b, s, A_HEADS, A_VDIM)
    f32 = jnp.float32
    lam = (jnp.exp(jnp.sum(lq1.astype(f32) * lk1.astype(f32)))
           - jnp.exp(jnp.sum(lq2.astype(f32) * lk2.astype(f32))) + lambda_init)
    oa = diff_attention(qa, ka, va, lam)
    oa = rmsnorm(oa, subln_g) * (1.0 - lambda_init)
    heads_b = lambda a: a.reshape(b, s, B_HEADS, HEAD_DIM)
    ob = stick_breaking(heads_b(qb), heads_b(kb), heads_b(vb))
    mixed = jnp.concatenate([oa.reshape(b, s, A_V), ob.reshape(b, s, B_W)], axis=-1)
    return mixed @ w_out

def odd_mixer(h, w_in, conv_w, conv_b, ln_g, ln_b, rel_table, w_out):
    b, s, _ = h.shape
    c_val, c_gate, qd, kd, vd = _split(h @ w_in, ODD_SPLITS)
    u = c_val * jax.nn.sigmoid(c_gate)
    c = lax.conv_general_dilated(
        u, conv_w.astype(u.dtype)[:, None, :], window_strides=(1,),
        padding=[(CONV_WIDTH - 1, 0)], dimension_numbers=('NWC', 'WIO', 'NWC'),
        feature_group_count=C_CHANNELS) + conv_b
    c = jax.nn.silu(layernorm(c, ln_g, ln_b))
    heads_d = lambda a: a.reshape(b, s, D_HEADS, HEAD_DIM)
    od = chunk_rel_attention(heads_d(qd), heads_d(kd), heads_d(vd), rel_table)
    mixed = jnp.concatenate([c, od.reshape(b, s, D_W)], axis=-1)
    return mixed @ w_out

def swiglu(h, w_gate, w_up, w_down):
    return (jax.nn.silu(h @ w_gate) * (h @ w_up)) @ w_down

def moe_swiglu(h, w_router, w_gate, w_up, w_down):
    b, s, d = h.shape
    t = h.reshape(b * s, d)
    logits = (t @ w_router).astype(jnp.float32)
    top_vals, top_idx = lax.top_k(logits, TOP_K)
    gates = jax.nn.softmax(top_vals, axis=-1)
    combine = jnp.sum(jax.nn.one_hot(top_idx, N_EXPERTS, dtype=jnp.float32) * gates[..., None], axis=1)
    combine = combine.astype(t.dtype)
    out = jnp.zeros_like(t)
    for e in range(N_EXPERTS):
        out = out + combine[:, e:e + 1] * swiglu(t, w_gate[e], w_up[e], w_down[e])
    return out.reshape(b, s, d)

def setup_inputs(seed: int = 0) -> dict:
    key = jax.random.key(seed)
    ks = iter(jax.random.split(key, 32))
    nrm = lambda shape, scale: jax.random.normal(next(ks), shape, jnp.float32) * scale
    gain = lambda shape: 1.0 + nrm(shape, 0.02)
    P = N_PAIR
    return {
        'x': nrm((BATCH, SEQ, D_MODEL), 1.0),
        'ev_norm_mix': gain((P, D_MODEL)),
        'ev_w_in': nrm((P, D_MODEL, EVEN_IN), D_MODEL ** -0.5),
        'ev_lambda_q1': nrm((P, HEAD_DIM), 0.1),
        'ev_lambda_k1': nrm((P, HEAD_DIM), 0.1),
        'ev_lambda_q2': nrm((P, HEAD_DIM), 0.1),
        'ev_lambda_k2': nrm((P, HEAD_DIM), 0.1),
        'ev_subln': gain((P, A_VDIM)),
        'ev_w_out': nrm((P, EVEN_MIX, D_MODEL), EVEN_MIX ** -0.5),
        'ev_norm_ffn': gain((P, D_MODEL)),
        'ev_ffn_gate': nrm((P, D_MODEL, D_FF), D_MODEL ** -0.5),
        'ev_ffn_up': nrm((P, D_MODEL, D_FF), D_MODEL ** -0.5),
        'ev_ffn_down': nrm((P, D_FF, D_MODEL), D_FF ** -0.5),
        'od_norm_mix': gain((P, D_MODEL)),
        'od_w_in': nrm((P, D_MODEL, ODD_IN), D_MODEL ** -0.5),
        'od_conv_w': nrm((P, CONV_WIDTH, C_CHANNELS), CONV_WIDTH ** -0.5),
        'od_conv_b': nrm((P, C_CHANNELS), 0.02),
        'od_conv_ln_g': gain((P, C_CHANNELS)),
        'od_conv_ln_b': nrm((P, C_CHANNELS), 0.02),
        'od_rel_bias': nrm((P, D_HEADS, 2 * MAX_REL + 1), 0.2),
        'od_w_out': nrm((P, ODD_MIX, D_MODEL), ODD_MIX ** -0.5),
        'od_norm_ffn': gain((P, D_MODEL)),
        'od_router': nrm((P, D_MODEL, N_EXPERTS), D_MODEL ** -0.5),
        'od_exp_gate': nrm((P, N_EXPERTS, D_MODEL, D_FF_EXPERT), D_MODEL ** -0.5),
        'od_exp_up': nrm((P, N_EXPERTS, D_MODEL, D_FF_EXPERT), D_MODEL ** -0.5),
        'od_exp_down': nrm((P, N_EXPERTS, D_FF_EXPERT, D_MODEL), D_FF_EXPERT ** -0.5),
        'final_norm': gain((D_MODEL,)),
    }

def reference(x, ev_norm_mix, ev_w_in, ev_lambda_q1, ev_lambda_k1, ev_lambda_q2, ev_lambda_k2,
              ev_subln, ev_w_out, ev_norm_ffn, ev_ffn_gate, ev_ffn_up, ev_ffn_down,
              od_norm_mix, od_w_in, od_conv_w, od_conv_b, od_conv_ln_g, od_conv_ln_b, od_rel_bias,
              od_w_out, od_norm_ffn, od_router, od_exp_gate, od_exp_up, od_exp_down, final_norm):
    for layer in range(DEPTH):
        i = layer // 2
        if layer % 2 == 0:
            lambda_init = 0.8 - 0.6 * math.exp(-0.3 * layer)
            x = x + even_mixer(rmsnorm(x, ev_norm_mix[i]), ev_w_in[i], ev_lambda_q1[i], ev_lambda_k1[i],
                               ev_lambda_q2[i], ev_lambda_k2[i], ev_subln[i], ev_w_out[i], lambda_init)
            x = x + swiglu(rmsnorm(x, ev_norm_ffn[i]), ev_ffn_gate[i], ev_ffn_up[i], ev_ffn_down[i])
        else:
            x = x + odd_mixer(rmsnorm(x, od_norm_mix[i]), od_w_in[i], od_conv_w[i], od_conv_b[i],
                              od_conv_ln_g[i], od_conv_ln_b[i], od_rel_bias[i], od_w_out[i])
            x = x + moe_swiglu(rmsnorm(x, od_norm_ffn[i]), od_router[i], od_exp_gate[i],
                               od_exp_up[i], od_exp_down[i])
    return rmsnorm(x, final_norm)


_drawn_inputs = setup_inputs


def setup_inputs(seed=0):
    import zlib

    import numpy as np

    out = dict(_drawn_inputs(seed))
    spreads = {}
    factors = {'ev_lambda_q2': 200.0,
     'od_conv_ln_g': 27.496,
     'od_conv_ln_b': 28.6,
     'final_norm': 21.896,
     'ev_subln': 3.483,
     'ev_norm_ffn': 2.814,
     'od_rel_bias': 16.579,
     'od_norm_mix': 6.865,
     'od_conv_b': 4.141,
     'od_norm_ffn': 8.0}
    for name, (base, spread) in spreads.items():
        noise = np.random.default_rng([zlib.crc32(name.encode()), seed]).standard_normal(out[name].shape)
        drawn = base * np.exp(spread * noise) if base else spread * noise
        out[name] = jnp.asarray(drawn.astype(out[name].dtype))
    for name, factor in factors.items():
        out[name] = (out[name] * factor).astype(out[name].dtype)
    return out
```

```python
from contextlib import ExitStack

import numpy as np

import concourse.bass as bass
from concourse import mybir

ALU = mybir.AluOpType
ACT = mybir.ActivationFunctionType
AX = mybir.AxisListType.X
F32 = mybir.dt.float32
F32R = mybir.dt.float32r
I32 = mybir.dt.int32
U32 = mybir.dt.uint32

P = 128
SEQ = 256
T = SEQ // P
D = 1024
KD = D // P
C = 512
HD = 64
A_HEADS = 4
HEADS = 8
PLACED = [0, 2, 4, 6, 1, 3, 5, 7]
D_FF = 2816
E_FF = 3584
N_EXP = 8
TAPS = 31
CONV_C = 512
CHUNK = 64
MAX_REL = 128
REL = 2 * MAX_REL + 1
EPS = 1e-6
LAMBDA_INIT = 0.2
NEG = -1e30

RAW = 6
RING = 3
HALF = 2048
FFC = D_FF // C
EC = E_FF // C
G_IN = 0
G_OUT = G_IN + 12
G_FFN = G_OUT + 4
G_DOWN = G_FFN + 4 * FFC + 2
G_OIN = G_DOWN + D_FF // 256
G_OOUT = G_OIN + 10
G_MOE = G_OOUT + 4
JOB = 6 * EC
assert JOB % RAW == 0 and JOB % RING == 0 and G_MOE % RING == 0
OVERFLOW = 3
JOBS = N_EXP + OVERFLOW

K_IDENT, K_NTRI, K_DMASK, K_LEXC, K_ONES, K_IOTA, K_NONES = (P * i for i in range(7))
K_IOTA8 = P * 7
K_COS = K_IOTA8 + 8
K_SIN = K_COS + T * 32
K_ROW = K_SIN + T * 32
K_COL = K_ROW + P
K_FLIP = K_COL + SEQ
K_ALL = K_FLIP + P


def constants():
    c = np.zeros((P, K_ALL), np.float32)
    p, i = np.arange(P)[:, None], np.arange(P)[None, :]
    c[:, K_IDENT:K_IDENT + P] = p == i
    c[:, K_NTRI:K_NTRI + P] = np.where(p >= i, -1.0, 0.0)
    c[:, K_DMASK:K_DMASK + P] = np.where(p >= i, NEG, 0.0)
    c[:, K_LEXC:K_LEXC + P] = p < i
    c[:, K_ONES:K_ONES + P] = 1.0
    c[:, K_IOTA:K_IOTA + P] = i
    c[:, K_NONES:K_NONES + P] = -1.0
    c[:, K_IOTA8:K_IOTA8 + 8] = np.arange(8)
    half = HD // 2
    freq = (np.float32(10000.0) ** (-np.arange(half, dtype=np.float32) * np.float32(2.0) / np.float32(HD)))
    ang = np.arange(SEQ, dtype=np.float32)[:, None] * freq.astype(np.float32)[None, :]
    ang = ang.reshape(T, P, half).transpose(1, 0, 2).reshape(P, T * half)
    c[:, K_COS:K_COS + T * half] = np.cos(ang)
    c[:, K_SIN:K_SIN + T * half] = np.sin(ang)
    c[:, K_ROW:K_ROW + P] = i < CHUNK
    c[:, K_COL:K_COL + SEQ] = np.where(np.arange(SEQ) >= SEQ - CHUNK, NEG, 0.0)
    c[:, K_FLIP:K_FLIP + P] = p + i == P - 1
    return c


def trunk(nc, w, out):
    ctx = ExitStack()
    with ctx:
        def sb(name, shape, dt=F32, at=ctx):
            return at.enter_context(nc.sbuf_tensor(name, shape, dt))

        def sem(name):
            return ctx.enter_context(nc.semaphore(name))

        raw = sb("raw", [P, RAW, HALF])
        whi = sb("whi", [P, RING, HALF], F32R)
        wlo = sb("wlo", [P, RING, HALF], F32R)
        x = sb("x", [P, T, D])
        cst = sb("cst", [P, K_ALL])
        gains_row = sb("gains_row", [4 * KD, P])
        gains = sb("gains", [P, 4, KD])
        ss = sb("ss", [P, 5, T])
        std = sb("std", [P, 5, T])
        rstd = sb("rstd", [P, 5, T])
        eps = sb("eps", [P, 1])
        ident = cst[:, K_IDENT:K_IDENT + P]
        ones = cst[:, K_ONES:K_ONES + P]

        with ExitStack() as even:
            e_hi = sb("e_hi", [P, KD, SEQ], F32R, even)
            e_lo = sb("e_lo", [P, KD, SEQ], F32R, even)
            with ExitStack() as tmp:
                e_xn = sb("e_xn", [P, T, D], F32, tmp)
                e_full = sb("e_full", [P, 2 * T, C], F32, tmp)
                rope_a = sb("rope_a", [P, C], F32, tmp)
                rope_b = sb("rope_b", [P, C], F32, tmp)
            with ExitStack() as tmp:
                pa = sb("pa", [P, HEADS * 3 * P], F32, tmp)
                pd = sb("pd", [P, A_HEADS * 3 * P], F32, tmp)
                pdT = sb("pdT", [P, A_HEADS * 3 * P], F32, tmp)
            with ExitStack() as tmp:
                sp = sb("sp", [P, 3, D], F32, tmp)
                wt = sb("wt", [P, 3, D], F32, tmp)
            sb("even_tmp", [P, 6 * D], F32, even)
            proj = sb("proj", [P, T, 6 * C], F32, even)
            qkT = sb("qkT", [P, 16, SEQ], F32, even)
            mixed = sb("mixed", [P, T, D], F32, even)
            lam_in = sb("lam_in", [P, 4, HD], F32, even)
            lam_j = sb("lam_j", [P, HD], F32, even)
            lam_s = sb("lam_s", [P, 4], F32, even)
            subln = sb("subln", [P, P], F32, even)
            a_nm = sb("a_nm", [P, T, HEADS], F32, even)
            a_sum = sb("a_sum", [P, T, HEADS], F32, even)
            a_r = sb("a_r", [P, T, HEADS], F32, even)
            a_ms = sb("a_ms", [P, T, A_HEADS], F32, even)
            a_sd = sb("a_sd", [P, T, A_HEADS], F32, even)
            a_rs = sb("a_rs", [P, T, A_HEADS], F32, even)
        with ExitStack() as ffn:
            f_hi = sb("f_hi", [P, KD, SEQ], F32R, ffn)
            f_lo = sb("f_lo", [P, KD, SEQ], F32R, ffn)
            f_xn = sb("f_xn", [P, T, D], F32, ffn)
            f_full = sb("f_full", [P, 2 * T, C], F32, ffn)
            fa_hi = sb("fa_hi", [P, D_FF // P, SEQ], F32R, ffn)
            fa_lo = sb("fa_lo", [P, D_FF // P, SEQ], F32R, ffn)
            f_s = sb("f_s", [P, T, C], F32, ffn)
            f_a = sb("f_a", [P, T, C], F32, ffn)
        with ExitStack() as odd:
            o_hi = sb("o_hi", [P, KD, SEQ], F32R, odd)
            o_lo = sb("o_lo", [P, KD, SEQ], F32R, odd)
            with ExitStack() as tmp:
                o_xn = sb("o_xn", [P, T, D], F32, tmp)
                o_full = sb("o_full", [P, 2 * T, C], F32, tmp)
            with ExitStack() as tmp:
                po = sb("po", [P, HEADS * 3 * P], F32, tmp)
                poT = sb("poT", [P, HEADS * 3 * P], F32, tmp)
            sb("odd_tmp", [P, 6 * D], F32, odd)
            oproj = sb("oproj", [P, T, 5 * C], F32, odd)
            oqkT = sb("oqkT", [P, 8, SEQ], F32, odd)
            uT = sb("uT", [P, 4, TAPS - 1 + SEQ], F32, odd)
            cv = sb("cv", [P, 4, SEQ], F32, odd)
            cn = oproj[:, :, 0:C]
            od = oproj[:, :, C:2 * C]
            conv_row = sb("conv_row", [TAPS + 3, CONV_C], F32, odd)
            conv = sb("conv", [P, 4, TAPS + 3], F32, odd)
            rel_in = sb("rel_in", [HEADS, REL], F32, odd)
            rel_rev = sb("rel_rev", [HEADS, 3 * P], F32, odd)
            bias = sb("bias", [P, HEADS, SEQ], F32, odd)
            o_nm = sb("o_nm", [P, T, HEADS], F32, odd)
            o_sum = sb("o_sum", [P, T, HEADS], F32, odd)
            o_r = sb("o_r", [P, T, HEADS], F32, odd)
            bn6 = sb("bn6", [P, T, 6], F32, odd)
            bn2 = sb("bn2", [P, T, 2], F32, odd)
            bsd = sb("bsd", [P, T], F32, odd)
            brs = sb("brs", [P, T], F32, odd)
        with ExitStack() as moe:
            with ExitStack() as tmp:
                m_hi = sb("m_hi", [P, KD, SEQ], F32R, tmp)
                m_lo = sb("m_lo", [P, KD, SEQ], F32R, tmp)
            with ExitStack() as tmp:
                ea_hi = sb("ea_hi", [P, E_FF // P, P], F32R, tmp)
                ea_lo = sb("ea_lo", [P, E_FF // P, P], F32R, tmp)
            sb("moe_tmp", [P, 2 * E_FF], F32, moe)
            with ExitStack() as tmp:
                m_full = sb("m_full", [P, 2 * T, C], F32, tmp)
            with ExitStack() as tmp:
                y_hi = sb("y_hi", [P, D], F32R, tmp)
                y_lo = sb("y_lo", [P, D], F32R, tmp)
            sb("moe_tmp2", [P, 2 * D], F32, moe)
            m_xn = sb("m_xn", [P, T, D], F32, moe)
            h_hi = sb("h_hi", [P, T, D], F32R, moe)
            h_lo = sb("h_lo", [P, T, D], F32R, moe)
            g_hi = sb("g_hi", [P, KD, P], F32R, moe)
            g_lo = sb("g_lo", [P, KD, P], F32R, moe)
            e_s = sb("e_s", [P, C], F32, moe)
            e_a = sb("e_a", [P, C], F32, moe)
            gain_row = sb("gain_row", [P, D], F32, moe)
            router = sb("router", [P, KD, N_EXP], F32, moe)
            r_hi = sb("r_hi", [P, KD, N_EXP], F32R, moe)
            r_lo = sb("r_lo", [P, KD, N_EXP], F32R, moe)
            pick = sb("pick", [P, T, P], F32, moe)
            pick_r = sb("pick_r", [P, T, P], F32R, moe)
            put_r = sb("put_r", [P, T, P], F32R, moe)
            logit = sb("logit", [P, T, N_EXP], F32, moe)
            top = sb("top", [P, T, 8], F32, moe)
            topi = sb("topi", [P, T, 8], U32, moe)
            topf = sb("topf", [P, T, 8], F32, moe)
            gate = sb("gate", [P, T, 4], F32, moe)
            hot = sb("hot", [P, T, 2, N_EXP], F32, moe)
            sel = sb("sel", [P, T, N_EXP], F32, moe)
            comb = sb("comb", [P, T, JOBS + 1], F32, moe)
            slot = sb("slot", [P, T, JOBS + 1], F32, moe)
            over = sb("over", [P, 4, N_EXP], F32, moe)
            over_w = sb("over_w", [P, OVERFLOW, N_EXP], F32, moe)
            over_t = sb("over_t", [P, OVERFLOW, 6, N_EXP], F32, moe)
            jobs_f = sb("jobs_f", [P, 16], F32, moe)
            jobs_i = sb("jobs_i", [P, 16], I32, moe)

        ps = ctx.enter_context(nc.psum_tensor("ps", [P, 8, C], F32))
        rel_dram = nc.dram_tensor("rel_scratch", (HEADS, 3 * P), F32, kind="Internal")

        raw_in = [sem(f"raw_in{s}") for s in range(RAW)]
        hi_done = sem("hi_done")
        lo_done = sem("lo_done")
        pe_half = sem("pe_half")
        S = {n: sem(n) for n in (
            "x_in cst_in row_in lam_ld sub_in crow_in rel_ld rel_st bias_in router_in grow_in fin_in out_st "
            "eps_set gains_tr gains_ev "
            "ip_ev roped at_tr at_ev_a at_ev_d a_sc a_mx a_ex a_pd a_tr a_tev a_pv a_oev a_msq a_sqrt a_done "
            "lam_sum lam_exp b_z b_ln b_sp b_cum b_w b_pv b_ev mx_tr mx_hi mx_lo op_add "
            "f_silu f_gfree f_ufree f_tr f_hi f_lo f_add "
            "oi_ev u_mul u_tr u_ev cw_tr cw_ev conv_step conv_done ct_tr ct_bn ct_sd cn_done cb_tr c_act c_hi c_lo "
            "rel_rv ot_tr ot_ev o_sc o_mx o_ex o_tr o_tev o_pv o_norm od_tr od_hi od_lo oo_add uz "
            "h_full h_hi_s h_lo_s r_hi_s r_lo_s r_mm cnt_mm sel_s route g_exp pk pk_r ga_mm ga_hi ga_lo pt_mm pt_ev "
            "e_silu e_ufree e_tr e_hi e_lo y_hi_s y_lo_s sc_mm sc_add fin_n load_turn dve_chain act_chain final_ok "
        ).split()}
        NORMS = 4
        n_ss = [sem(f"n_ss{i}") for i in range(NORMS + 1)]
        n_std = [sem(f"n_std{i}") for i in range(NORMS + 1)]
        n_xn = [sem(f"n_xn{i}") for i in range(NORMS)]
        n_tr = [sem(f"n_tr{i}") for i in range(NORMS)]
        n_full = [sem(f"n_full{i}") for i in range(NORMS)]
        n_hi = [sem(f"n_hi{i}") for i in range(NORMS)]
        n_lo = [sem(f"n_lo{i}") for i in range(NORMS)]

        XN = [e_xn, f_xn, o_xn, m_xn]
        FULL = [e_full, f_full, o_full, m_full]
        HI = [e_hi, f_hi, o_hi, m_hi]
        LO = [e_lo, f_lo, o_lo, m_lo]

        def cols_view(ap, k=4):
            return ap.rearrange("p (k n) -> p k n", k=k)

        def cols_src(m, k0, kn, c0, cn_):
            return m.rearrange("(k p) n -> p k n", p=P)[:, k0:k0 + kn, c0:c0 + cn_]

        def rows_src(m, b0, bn):
            return m[b0 * P:(b0 + bn) * P, :].rearrange("(b p) n -> p b n", p=P)

        W_IN, W_OUT = w["ev_w_in"][0], w["ev_w_out"][0]
        W_G, W_U, W_D = w["ev_ffn_gate"][0], w["ev_ffn_up"][0], w["ev_ffn_down"][0]
        O_IN, O_OUT = w["od_w_in"][0], w["od_w_out"][0]

        def static_src(g):
            if g < G_OUT:
                return cols_src(W_IN, g % 2 * 4, 4, g // 2 * C, C), 4
            if g < G_FFN:
                g -= G_OUT
                return cols_src(W_OUT, g % 2 * 4, 4, g // 2 * C, C), 4
            if g < G_DOWN:
                g -= G_FFN
                if g >= 4 * FFC:
                    return cols_src((W_G, W_U)[g - 4 * FFC], 0, KD, FFC * C, D_FF - FFC * C), KD
                return cols_src((W_G, W_U)[g // 2 % 2], g % 2 * 4, 4, g // 4 * C, C), 4
            if g < G_OIN:
                return rows_src(W_D, 2 * (g - G_DOWN), 2), 2
            if g < G_OOUT:
                g -= G_OIN
                return cols_src(O_IN, g % 2 * 4, 4, g // 2 * C, C), 4
            g -= G_OOUT
            return cols_src(O_OUT, g % 2 * 4, 4, g // 2 * C, C), 4

        EG = w["od_exp_gate"][0].rearrange("e (k p) n -> p e k n", p=P)
        EU = w["od_exp_up"][0].rearrange("e (k p) n -> p e k n", p=P)
        ED = w["od_exp_down"][0].rearrange("e (b p) n -> p e b n", p=P)

        def expert_src(e, u):
            one = bass.ds(e, 1)
            if u < 4 * EC:
                m, c0, k0 = (EG, EU)[u // 2 % 2], u // 4 * C, u % 2 * 4
                return m[:, one, k0:k0 + 4, c0:c0 + C].rearrange("p e k n -> p (e k) n"), 4
            b0 = 2 * (u - 4 * EC)
            return ED[:, one, b0:b0 + 2, :].rearrange("p e b n -> p (e b) n"), 2

        def gm(j, u):
            return j * JOB + (G_MOE + u)

        block = ctx.enter_context(nc.Block())

        @block.sync
        def _(sp_):
            def load_half(g, s, src, k):
                if not isinstance(g, int) or g >= RAW:
                    sp_.wait_ge(lo_done, g - (RAW - 1))
                    if not isinstance(g, int):
                        sp_.sem_inc(S["load_turn"], 1)
                sp_.dma_start(cols_view(raw[:, s, :], k), src).then_inc(raw_in[s], 16)

            sp_.dma_start(x[:], w["x"][0].rearrange("(t p) d -> p t d", p=P)).then_inc(S["x_in"], 16)
            sp_.dma_start(cst[:], w["cst"]).then_inc(S["cst_in"], 16)
            for i, name in enumerate(("ev_norm_mix", "ev_norm_ffn", "od_norm_mix", "od_norm_ffn")):
                sp_.dma_start(gains_row[i * KD:(i + 1) * KD, :],
                              w[name][0].rearrange("(k p) -> k p", p=P)).then_inc(S["row_in"], 16)
            for g in range(RAW):
                load_half(g, g % RAW, *static_src(g))
            for i, name in enumerate(("ev_lambda_q1", "ev_lambda_k1", "ev_lambda_q2", "ev_lambda_k2")):
                sp_.dma_start(lam_in[:, i, :], w[name].broadcast_to([P, HD])).then_inc(S["lam_ld"], 16)
            sp_.dma_start(subln[:], w["ev_subln"].broadcast_to([P, P])).then_inc(S["sub_in"], 16)
            for g in range(RAW, G_OIN + RAW):
                load_half(g, g % RAW, *static_src(g))
            sp_.wait_ge(S["f_add"], 4)
            for r0, rn, name in ((0, TAPS, "od_conv_w"), (TAPS, 1, "od_conv_b"),
                                 (TAPS + 1, 1, "od_conv_ln_g"), (TAPS + 2, 1, "od_conv_ln_b")):
                src = w[name][0] if rn > 1 else w[name]
                sp_.dma_start(conv_row[r0:r0 + rn, :], src).then_inc(S["crow_in"], 16)
            sp_.dma_start(rel_in[:], w["od_rel_bias"][0]).then_inc(S["rel_ld"], 16)
            sp_.wait_ge(S["rel_rv"], 2)
            sp_.dma_start(rel_dram.ap(), rel_rev[:]).then_inc(S["rel_st"], 16)
            sp_.wait_ge(S["rel_st"], 16)
            hankel = bass.AP(rel_dram, 0, [[1, P], [3 * P, HEADS], [1, SEQ]])
            sp_.dma_start(bias[:], hankel).then_inc(S["bias_in"], 16)
            for g in range(G_OIN + RAW, G_MOE):
                load_half(g, g % RAW, *static_src(g))
            for u in range(RAW):
                load_half(G_MOE + u, (G_MOE + u) % RAW, *expert_src(0, u))
            sp_.wait_ge(S["oo_add"], 4)
            sp_.dma_start(gain_row[:], w["od_norm_ffn"].broadcast_to([P, D])).then_inc(S["grow_in"], 16)
            sp_.dma_start(router[:], w["od_router"][0].rearrange("(k p) e -> p k e", p=P)).then_inc(S["router_in"], 16)
            sp_.wait_ge(S["h_full"], 2)
            sp_.dma_start(gain_row[:], w["final_norm"].rearrange("(a d) -> a d", a=1).broadcast_to([P, D])).then_inc(S["fin_in"], 16)
            sp_.wait_ge(S["route"], 1)
            njobs = sp_.value_load(jobs_i[0:1, JOBS + 1:JOBS + 2], min_val=N_EXP, max_val=JOBS)
            with sp_.Fori(0, njobs) as j:
                e = sp_.value_load(jobs_i[0:1, bass.ds(j, 1)], min_val=0, max_val=N_EXP - 1)
                for u in range(RAW, JOB):
                    load_half(gm(j, u), (G_MOE + u) % RAW, *expert_src(e, u))
                e2 = sp_.value_load(jobs_i[0:1, bass.ds(j + 1, 1)], min_val=0, max_val=N_EXP - 1)
                for u in range(RAW):
                    load_half(gm(j, JOB + u), (G_MOE + u) % RAW, *expert_src(e2, u))
            sp_.wait_ge(S["final_ok"], 2)
            sp_.dma_start(out[0].rearrange("(t p) d -> p t d", p=P), m_xn[:]).then_inc(S["out_st"], 16)
            sp_.wait_ge(S["out_st"], 16)

        @block.scalar
        def _(act):
            chain = [0]

            def link(ins):
                chain[0] += 1
                ins.then_inc(S["act_chain"], 1)
                act.wait_ge(S["act_chain"], chain[0])

            def hi(g, s, landed):
                act.wait_ge(raw_in[s], landed)
                if not isinstance(g, int) or g >= RING:
                    act.wait_ge(pe_half, g - (RING - 1))
                r = (s % RING)
                act.copy(whi[:, r, :], raw[:, s, :]).then_inc(hi_done, 1)

            def hi_static(g):
                hi(g, g % RAW, 16 * (g // RAW + 1))

            def norm_std(n):
                act.wait_ge(n_ss[n], T)
                act.activation(std[:, n, :], ss[:, n, :], ACT.Sqrt, bias=eps[:], scale=1.0 / D).then_inc(n_std[n], 1)

            def norm_hi(n):
                for b in range(2 * T):
                    act.wait_ge(n_full[n], b + 1)
                    t, h = b // 2, b % 2
                    act.copy(HI[n][:, 4 * h:4 * h + 4, t * P:(t + 1) * P],
                             FULL[n][:, b, :].rearrange("p (k s) -> p k s", k=4)).then_inc(n_hi[n], 1)

            act.wait_ge(S["eps_set"], 1)
            for g in range(RING):
                hi_static(g)
            norm_std(0)
            norm_hi(0)
            for g in range(G_IN, G_OUT):
                hi_static(g + RING)
                if g % 2:
                    n = g // 2
                    act.wait_ge(pe_half, g + 1)
                    for t in range(T):
                        act.activation(proj[:, t, n * C:(n + 1) * C], ps[:, 2 * (n % 2) + t, :], ACT.Copy,
                                       scale=HD ** -0.5 if n in (0, 3) else 1.0).then_inc(S["ip_ev"], 1)
            for i in range(0, 8, 2):
                act.wait_ge(S["at_tr"], i + 1)
                part, t = i // 2, i % 2
                act.copy(qkT[:, 4 * part:4 * part + 4, t * P:(t + 1) * P],
                         ps[:, 4 + i % 4, :].rearrange("p (k s) -> p k s", k=4)).then_inc(S["at_ev_a"], 1)
            act.wait_ge(S["lam_sum"], 2)
            act.activation(lam_s[:, 2:4], lam_s[:, 0:2], ACT.Exp).then_inc(S["lam_exp"], 1)
            for t in range(T):
                act.wait_ge(S["a_mx"], t + 1)
                n_k = P * (t + 1)
                off = t * HEADS * P
                for s in range(HEADS):
                    src = ps[:, 0 if t == 0 else 2:, :].rearrange("p b c -> p (b c)")[:, s * n_k:(s + 1) * n_k]
                    act.activation(pa[:, off + s * n_k:off + (s + 1) * n_k], src, ACT.Exp,
                                   bias=a_nm[:, t, s:s + 1], accum_out=a_sum[:, t, s:s + 1]).then_inc(S["a_ex"], 1)
            for i, (bank, off) in enumerate(((6, 0), (7, C), (0, 2 * C))):
                act.wait_ge(S["a_tr"], i + 1)
                act.copy(pdT[:, off:off + C], ps[:, bank, :]).then_inc(S["a_tev"], 1)
            for t in range(T):
                act.wait_ge(S["a_pv"], t + 1)
                act.copy(mixed[:, t, 0:C], ps[:, 1 + t, :]).then_inc(S["a_oev"], 1)
            act.wait_ge(S["a_msq"], 1)
            act.activation(a_sd[:], a_ms[:], ACT.Sqrt, bias=eps[:], scale=1.0 / P).then_inc(S["a_sqrt"], 1)
            for i in range(3):
                act.wait_ge(S["b_z"], i + 1)
                if i == 0:
                    act.wait_ge(S["a_tr"], 3)
                    act.wait_ge(S["a_pv"], 2)
                link(act.activation(sp[:, i, :], ps[:, 2 * i:2 * i + 2, :].rearrange("p b c -> p (b c)"), ACT.Abs))
                link(act.activation(sp[:, i, :], sp[:, i, :], ACT.Exp, scale=-1.0))
                act.activation(sp[:, i, :], sp[:, i, :], ACT.Ln, bias=1.0).then_inc(S["b_ln"], 1)
            for i in range(3):
                act.wait_ge(S["b_cum"], i + 1)
                act.activation(wt[:, i, :], ps[:, 2 * i:2 * i + 2, :].rearrange("p b c -> p (b c)"),
                               ACT.Exp).then_inc(S["b_w"], 1)
            for t in range(T):
                act.wait_ge(S["b_pv"], t + 1)
                act.copy(mixed[:, t, C:D], ps[:, 6 + t, :]).then_inc(S["b_ev"], 1)
            for b in range(2 * T):
                act.wait_ge(S["mx_tr"], b + 1)
                t, h = b // 2, b % 2
                act.copy(e_hi[:, 4 * h:4 * h + 4, t * P:(t + 1) * P],
                         ps[:, 4 + b, :].rearrange("p (k s) -> p k s", k=4)).then_inc(S["mx_hi"], 1)
            for g in range(G_OUT, G_FFN):
                hi_static(g + RING)
            norm_std(1)
            norm_hi(1)

            def f_hi_evac(c):
                nb = min(4, D_FF // P - 4 * c)
                for t in range(T):
                    act.wait_ge(S["f_tr"], T * c + t + 1)
                    act.copy(fa_hi[:, 4 * c:4 * c + nb, t * P:(t + 1) * P],
                             ps[:, 4 + t, 0:nb * P].rearrange("p (k s) -> p k s", k=nb)).then_inc(S["f_hi"], 1)

            for g in range(G_FFN, G_DOWN + D_FF // 256):
                hi_static(g + RING)
                q = g - G_FFN
                c = q // 4
                last = q >= 4 * FFC
                if (not last and q % 4 == 1) or q == 4 * FFC:
                    act.wait_ge(pe_half, g + 1)
                    if c >= 1:
                        act.wait_ge(S["f_ufree"], T * c)
                    wd = C if c < FFC else D_FF - FFC * C
                    for t in range(T):
                        act.activation(f_s[:, t, 0:wd], ps[:, t, 0:wd], ACT.Silu).then_inc(S["f_silu"], 1)
                    if c >= 1:
                        f_hi_evac(c - 1)
                if q == 4 * FFC + 2:
                    f_hi_evac(FFC)
            norm_std(2)
            norm_hi(2)
            for g in range(G_OIN, G_OOUT):
                hi_static(g + RING)
                if (g - G_OIN) % 2:
                    n = (g - G_OIN) // 2
                    act.wait_ge(pe_half, g + 1)
                    for t in range(T):
                        if n == 1:
                            act.activation(oproj[:, t, n * C:(n + 1) * C], ps[:, 2 * (n % 2) + t, :],
                                           ACT.Sigmoid).then_inc(S["oi_ev"], 1)
                        else:
                            act.activation(oproj[:, t, n * C:(n + 1) * C], ps[:, 2 * (n % 2) + t, :], ACT.Copy,
                                           scale=HD ** -0.5 if n == 2 else 1.0).then_inc(S["oi_ev"], 1)
            for i in range(4):
                act.wait_ge(S["ot_tr"], i + 1)
                part, t = i // 2, i % 2
                act.copy(oqkT[:, 4 * part:4 * part + 4, t * P:(t + 1) * P],
                         ps[:, 4 + i, :].rearrange("p (k s) -> p k s", k=4)).then_inc(S["ot_ev"], 1)
            for t in range(T):
                act.wait_ge(S["o_mx"], t + 1)
                n_k = P * (t + 1)
                off = t * HEADS * P
                for s in range(HEADS):
                    src = ps[:, 0 if t == 0 else 2:, :].rearrange("p b c -> p (b c)")[:, s * n_k:(s + 1) * n_k]
                    act.activation(po[:, off + s * n_k:off + (s + 1) * n_k], src, ACT.Exp,
                                   bias=o_nm[:, t, s:s + 1], accum_out=o_sum[:, t, s:s + 1]).then_inc(S["o_ex"], 1)
            for i in range(6):
                act.wait_ge(S["o_tr"], i + 1)
                act.copy(poT[:, i * C:(i + 1) * C], ps[:, i, :]).then_inc(S["o_tev"], 1)
            act.wait_ge(S["ct_bn"], T)
            act.activation(bsd[:], bn2[:, :, 1], ACT.Sqrt, bias=eps[:]).then_inc(S["ct_sd"], 1)
            for b in range(4):
                act.wait_ge(S["cb_tr"], b // 2 + 1)
                act.activation(cv[:, b, :], ps[:, 2 + b // 2, (b % 2) * SEQ:(b % 2 + 1) * SEQ], ACT.Silu,
                               bias=conv[:, b, TAPS + 2:TAPS + 3],
                               scale=conv[:, b, TAPS + 1:TAPS + 2]).then_inc(S["c_act"], 1)
            act.wait_ge(S["c_act"], 4)
            act.copy(o_hi[:, 0:4, :], cv[:]).then_inc(S["c_hi"], 1)
            for t in range(T):
                act.wait_ge(S["od_tr"], t + 1)
                act.copy(o_hi[:, 4:8, t * P:(t + 1) * P],
                         ps[:, 4 + t, :].rearrange("p (k s) -> p k s", k=4)).then_inc(S["od_hi"], 1)
            for g in range(G_OOUT, G_MOE):
                hi_static(g + RING)
            norm_std(3)
            norm_hi(3)
            for t in range(T):
                act.wait_ge(S["h_full"], t + 1)
                act.copy(h_hi[:, t, :], m_xn[:, t, :]).then_inc(S["h_hi_s"], 1)
            act.wait_ge(S["router_in"], 16)
            act.copy(r_hi[:], router[:]).then_inc(S["r_hi_s"], 1)
            act.wait_ge(S["g_exp"], 1)
            act.activation(gate[:, :, 1], gate[:, :, 0], ACT.Exp).then_inc(S["g_exp"], 1)

            def pick_round(i):
                act.wait_ge(S["pk"], i + 1)
                act.copy(pick_r[:], pick[:]).then_inc(S["pk_r"], 1)

            def gather_hi(i):
                for h in range(2):
                    act.wait_ge(S["ga_mm"], 2 * i + (h + 1))
                    act.copy(g_hi[:, 4 * h:4 * h + 4, :],
                             ps[:, 7 - 2 * h, :].rearrange("p (k s) -> p k s", k=4)).then_inc(S["ga_hi"], 1)

            pick_round(0)
            gather_hi(0)
            act.wait_ge(S["route"], 1)
            njobs = act.value_load(jobs_i[0:1, JOBS + 1:JOBS + 2], min_val=N_EXP, max_val=JOBS)
            with act.Fori(0, njobs) as j:
                def e_hi_evac(c):
                    act.wait_ge(S["e_tr"], EC * j + (c + 1))
                    act.copy(ea_hi[:, 4 * c:4 * c + 4, :],
                             ps[:, 2, :].rearrange("p (k s) -> p k s", k=4)).then_inc(S["e_hi"], 1)

                for u in range(JOB):
                    g = gm(j, u + RING)
                    hi(g, (G_MOE + u + RING) % RAW, 16 * (JOB // RAW) * j + 16 * ((G_MOE + u + RING) // RAW + 1))
                    if u == 2:
                        act.wait_ge(S["pt_mm"], j + 1)
                        act.copy(put_r[:], ps[:, 7, 0:SEQ].rearrange("p (t s) -> p t s", t=T)).then_inc(S["pt_ev"], 1)
                    if u < 4 * EC and u % 4 == 1:
                        c = u // 4
                        act.wait_ge(pe_half, gm(j, u + 1))
                        if c:
                            act.wait_ge(S["e_ufree"], EC * j + c)
                        act.activation(e_s[:], ps[:, 0, :], ACT.Silu).then_inc(S["e_silu"], 1)
                        if c:
                            e_hi_evac(c - 1)
                    if u == 4 * EC + 1:
                        e_hi_evac(EC - 1)
                    if u == 4 * EC + 2:
                        pick_round(j + 1)
                    if u == 4 * EC + 5:
                        gather_hi(j + 1)
                act.wait_ge(pe_half, gm(j, JOB))
                act.copy(y_hi[:], ps[:, 3:5, :].rearrange("p b c -> p (b c)")).then_inc(S["y_hi_s"], 1)
            norm_std(4)

        @block.vector
        def _(dve):
            chain = [0]

            def link(ins):
                chain[0] += 1
                ins.then_inc(S["dve_chain"], 1)
                dve.wait_ge(S["dve_chain"], chain[0])

            def lo(g, s):
                dve.wait_ge(hi_done, g + 1)
                r = s % RING
                dve.tensor_tensor(wlo[:, r, :], raw[:, s, :], whi[:, r, :].bitcast(F32),
                                  ALU.subtract).then_inc(lo_done, 1)

            def lo_static(g):
                lo(g, g % RAW)

            def norm_rstd(n, junk):
                for t in range(T):
                    dve.tensor_tensor_reduce(out=junk[:, t, :], in0=x[:, t, :], in1=x[:, t, :], scale=1.0,
                                             scalar=0.0, op0=ALU.mult, op1=ALU.add,
                                             accum_out=ss[:, n, t:t + 1]).then_inc(n_ss[n], 1)
                dve.wait_ge(n_std[n], 1)
                link(dve.reciprocal(rstd[:, n, :], std[:, n, :]))

            def norm(n):
                norm_rstd(n, XN[n])
                for t in range(T):
                    dve.tensor_scalar(XN[n][:, t, :], x[:, t, :], rstd[:, n, t:t + 1], None,
                                      ALU.mult).then_inc(n_xn[n], 1)
                if n == 0:
                    dve.wait_ge(S["gains_tr"], 1)
                    dve.tensor_copy(gains[:].rearrange("p n k -> p (n k)"), ps[:, 0, 0:4 * KD]).then_inc(S["gains_ev"], 1)
                    dve.wait_ge(S["gains_ev"], 1)
                for b in range(2 * T):
                    dve.wait_ge(n_tr[n], b + 1)
                    h = b % 2
                    dve.tensor_tensor(FULL[n][:, b, :].rearrange("p (k s) -> p k s", k=4),
                                      ps[:, 4 + b, :].rearrange("p (k s) -> p k s", k=4),
                                      gains[:, n, 4 * h:4 * h + 4].unsqueeze(2).broadcast_to([P, 4, P]),
                                      ALU.mult).then_inc(n_full[n], 1)
                for b in range(2 * T):
                    dve.wait_ge(n_hi[n], b + 1)
                    t, h = b // 2, b % 2
                    tt = slice(t * P, (t + 1) * P)
                    dve.tensor_tensor(LO[n][:, 4 * h:4 * h + 4, tt], FULL[n][:, b, :].rearrange("p (k s) -> p k s", k=4),
                                      HI[n][:, 4 * h:4 * h + 4, tt].bitcast(F32), ALU.subtract).then_inc(n_lo[n], 1)

            dve.memset(eps[:], EPS).then_inc(S["eps_set"], 1)
            for g in range(RING):
                lo_static(g)
            dve.wait_ge(S["x_in"], 16)
            norm(0)
            dve.wait_ge(S["lam_ld"], 64)
            for i in range(2):
                if i:
                    dve.wait_ge(S["lam_sum"], i)
                dve.tensor_tensor_reduce(out=lam_j[:], in0=lam_in[:, 2 * i, :], in1=lam_in[:, 2 * i + 1, :],
                                         scale=1.0, scalar=0.0, op0=ALU.mult, op1=ALU.add,
                                         accum_out=lam_s[:, i:i + 1]).then_inc(S["lam_sum"], 1)

            def rope(part, t):
                v = proj[:, t, part * C:(part + 1) * C].rearrange("p (h a d) -> p h a d", a=2, d=HD // 2)
                a = rope_a[:].rearrange("p (h a d) -> p h a d", a=2, d=HD // 2)
                b = rope_b[:].rearrange("p (h a d) -> p h a d", a=2, d=HD // 2)
                cos = cst[:, K_COS + 32 * t:K_COS + 32 * (t + 1)].unsqueeze(1).broadcast_to([P, HEADS, 32])
                sin = cst[:, K_SIN + 32 * t:K_SIN + 32 * (t + 1)].unsqueeze(1).broadcast_to([P, HEADS, 32])
                dve.wait_ge(S["ip_ev"], T * part + t + 1)
                for i in range(2):
                    dve.tensor_tensor(a[:, :, i, :], v[:, :, i, :], cos, ALU.mult)
                    last = dve.tensor_tensor(b[:, :, i, :], v[:, :, 1 - i, :], sin, ALU.mult)
                link(last)
                dve.tensor_tensor(v[:, :, 0, :], a[:, :, 0, :], b[:, :, 0, :], ALU.subtract)
                last = dve.tensor_tensor(v[:, :, 1, :], a[:, :, 1, :], b[:, :, 1, :], ALU.add)
                link(last)

            for g in range(G_IN, G_OUT):
                lo_static(g + RING)
                if 4 <= g < 8:
                    rope(g % 2, (g - 4) // 2)
            dve.nop().then_inc(S["roped"], 1)
            for i in range(1, 8, 2):
                dve.wait_ge(S["at_tr"], i + 1)
                part, t = i // 2, i % 2
                dve.tensor_copy(qkT[:, 4 * part:4 * part + 4, t * P:(t + 1) * P],
                                ps[:, 4 + i % 4, :].rearrange("p (k s) -> p k s", k=4)).then_inc(S["at_ev_d"], 1)
            for t in range(T):
                dve.wait_ge(S["a_sc"], t + 1)
                n_k = P * (t + 1)
                src = ps[:, 0:2, :] if t == 0 else ps[:, 2:6, :]
                dve.tensor_reduce(a_nm[:, t, :], src.rearrange("p b (h k) -> p (b h) k", k=n_k), AX, ALU.max,
                                  negate=True).then_inc(S["a_mx"], 1)
            dve.wait_ge(S["lam_exp"], 1)
            link(dve.tensor_tensor(lam_s[:, 0:1], lam_s[:, 2:3], lam_s[:, 3:4], ALU.subtract))
            link(dve.tensor_scalar(lam_s[:, 1:2], lam_s[:, 0:1], LAMBDA_INIT, None, ALU.add))
            for t in range(T):
                n_k = P * (t + 1)
                off, offd = t * HEADS * P, t * A_HEADS * P
                dve.wait_ge(S["a_ex"], HEADS * (t + 1))
                link(dve.reciprocal(a_r[:, t, :], a_sum[:, t, :]))
                odd_r = a_r[:, t, A_HEADS:HEADS]
                link(dve.tensor_scalar(odd_r, odd_r, lam_s[:, 1:2], None, ALU.mult))
                p_of = lambda s: pa[:, off + s * n_k:off + (s + 1) * n_k]
                for h in range(A_HEADS):
                    last = dve.tensor_scalar(p_of(A_HEADS + h), p_of(A_HEADS + h), a_r[:, t, A_HEADS + h:A_HEADS + h + 1],
                                             None, ALU.mult)
                link(last)
                for h in range(A_HEADS):
                    dve.scalar_tensor_tensor(out=pd[:, offd + h * n_k:offd + (h + 1) * n_k], in0=p_of(h),
                                             scalar=a_r[:, t, h:h + 1], in1=p_of(A_HEADS + h),
                                             op0=ALU.mult, op1=ALU.subtract).then_inc(S["a_pd"], 1)
            dve.wait_ge(S["sub_in"], 16)
            link(dve.tensor_scalar(subln[:], subln[:], 1.0 - LAMBDA_INIT, None, ALU.mult))
            dve.wait_ge(S["a_oev"], T)
            dve.wait_ge(S["a_tr"], 3)
            sq = pa[:, 0:T * C].rearrange("p (t h d) -> p t h d", t=T, h=A_HEADS)
            mv = mixed[:, :, 0:C].rearrange("p t (h d) -> p t h d", h=A_HEADS)
            for t in range(T):
                last = dve.tensor_tensor(sq[:, t], mv[:, t], mv[:, t], ALU.mult)
            link(last)
            for t in range(T):
                last = dve.tensor_reduce(a_ms[:, t, :], sq[:, t], AX, ALU.add)
            last.then_inc(S["a_msq"], 1)
            dve.wait_ge(S["a_sqrt"], 1)
            link(dve.reciprocal(a_rs[:], a_sd[:]))
            for t in range(T):
                for h in range(A_HEADS):
                    last = dve.scalar_tensor_tensor(out=mv[:, t, h, :], in0=mv[:, t, h, :], scalar=a_rs[:, t, h:h + 1],
                                                    in1=subln[:], op0=ALU.mult, op1=ALU.mult)
            last.then_inc(S["a_done"], 1)
            for i in range(3):
                dve.wait_ge(S["b_ln"], i + 1)
                dve.scalar_tensor_tensor(out=sp[:, i, :], in0=ps[:, 2 * i:2 * i + 2, :].rearrange("p b c -> p (b c)"),
                                         scalar=0.0, in1=sp[:, i, :], op0=ALU.max, op1=ALU.add).then_inc(S["b_sp"], 1)
            for b in range(2 * T):
                dve.wait_ge(S["mx_hi"], b + 1)
                t, h = b // 2, b % 2
                tt = slice(t * P, (t + 1) * P)
                dve.tensor_tensor(e_lo[:, 4 * h:4 * h + 4, tt], ps[:, 4 + b, :].rearrange("p (k s) -> p k s", k=4),
                                  e_hi[:, 4 * h:4 * h + 4, tt].bitcast(F32), ALU.subtract).then_inc(S["mx_lo"], 1)

            def residual(n, banks, done):
                for t in range(T):
                    dve.tensor_tensor(x[:, t, n * C:(n + 1) * C], x[:, t, n * C:(n + 1) * C],
                                      ps[:, banks[t], :], ALU.add).then_inc(done, 1)

            for g in range(G_OUT, G_FFN):
                lo_static(g + RING)
                if g % 2:
                    n = (g - G_OUT) // 2
                    dve.wait_ge(pe_half, g + 1)
                    residual(n, (2 * n, 2 * n + 1), S["op_add"])
            dve.wait_ge(S["op_add"], 4)
            norm(1)

            def f_lo_evac(c):
                nb = min(4, D_FF // P - 4 * c)
                for t in range(T):
                    dve.wait_ge(S["f_hi"], T * c + t + 1)
                    dst = (slice(4 * c, 4 * c + nb), slice(t * P, (t + 1) * P))
                    dve.tensor_tensor(fa_lo[:, dst[0], dst[1]],
                                      ps[:, 4 + t, 0:nb * P].rearrange("p (k s) -> p k s", k=nb),
                                      fa_hi[:, dst[0], dst[1]].bitcast(F32), ALU.subtract).then_inc(S["f_lo"], 1)

            for g in range(G_FFN, G_OIN):
                lo_static(g + RING)
                q = g - G_FFN
                if (q < 4 * FFC and q % 4 == 1) or q == 4 * FFC:
                    c = q // 4
                    if c >= 1:
                        f_lo_evac(c - 1)
                if (q < 4 * FFC and q % 4 == 3) or q == 4 * FFC + 1:
                    c = q // 4
                    wd = C if c < FFC else D_FF - FFC * C
                    dve.wait_ge(pe_half, g + 1)
                    dve.wait_ge(S["f_silu"], T * (c + 1))
                    for t in range(T):
                        if c >= 1:
                            dve.wait_ge(S["f_tr"], T * (c - 1) + t + 1)
                        dve.tensor_tensor(f_a[:, t, 0:wd], ps[:, 2 + t, 0:wd], f_s[:, t, 0:wd],
                                          ALU.mult).then_inc(S["f_ufree"], 1)
                if q == 4 * FFC + 2:
                    f_lo_evac(FFC)
            dve.wait_ge(pe_half, G_OIN)
            for n in range(2):
                residual(n, ((0, 6), (1, 7))[n], S["f_add"])
            dve.wait_ge(S["f_add"], 4)
            norm(2)
            dve.wait_ge(S["rel_ld"], 16)
            dve.tensor_copy(rel_rev[:, 0:P - 1], rel_in[:, REL - 1:REL].broadcast_to([HEADS, P - 1])).then_inc(S["rel_rv"], 1)
            dve.tensor_copy(rel_rev[:, P - 1:P - 1 + REL], rel_in[:, ::-1]).then_inc(S["rel_rv"], 1)

            for g in range(G_OIN, G_OOUT):
                lo_static(g + RING)
                q = g - G_OIN
                if q == 3:
                    dve.memset(uT[:, :, 0:TAPS - 1], 0.0).then_inc(S["uz"], 1)
                    for t in range(T):
                        dve.wait_ge(S["oi_ev"], T + t + 1)
                        dve.tensor_tensor(oproj[:, t, 0:C], oproj[:, t, 0:C], oproj[:, t, C:2 * C],
                                          ALU.mult).then_inc(S["u_mul"], 1)
                if q == 6:
                    dve.wait_ge(S["cw_tr"], 1)
                    link(dve.tensor_copy(conv[:], ps[:, 6, 0:4 * (TAPS + 3)].rearrange("p (b n) -> p b n", b=4)))
                    for t in range(T):
                        dve.wait_ge(S["u_tr"], t + 1)
                        last = dve.tensor_copy(uT[:, :, TAPS - 1 + t * P:TAPS - 1 + (t + 1) * P],
                                               ps[:, 4 + t, :].rearrange("p (b s) -> p b s", b=4))
                        last.then_inc(S["u_ev"], 1)
            for t in range(T):
                dve.wait_ge(S["o_sc"], t + 1)
                n_k = P * (t + 1)
                src = ps[:, 0:2, :] if t == 0 else ps[:, 2:6, :]
                dve.tensor_reduce(o_nm[:, t, :], src.rearrange("p b (h k) -> p (b h) k", k=n_k), AX, ALU.max,
                                  negate=True).then_inc(S["o_mx"], 1)
            dve.wait_ge(S["u_ev"], T)
            dve.wait_ge(S["uz"], 1)
            for b in range(4):
                dve.tensor_scalar(cv[:, b, :], uT[:, b, 0:SEQ], conv[:, b, 0:1], conv[:, b, TAPS:TAPS + 1],
                                  ALU.mult, ALU.add).then_inc(S["conv_step"], 1)
            with dve.Fori(1, TAPS) as k:
                for b in range(4):
                    dve.wait_ge(S["conv_step"], k * 4 + (b - 3))
                    dve.scalar_tensor_tensor(out=cv[:, b, :], in0=uT[:, b, bass.ds(k, SEQ)],
                                             scalar=conv[:, b, bass.ds(k, 1)], in1=cv[:, b, :],
                                             op0=ALU.mult, op1=ALU.add).then_inc(S["conv_step"], 1)
            for t in range(T):
                dve.wait_ge(S["ct_tr"], t + 1)
                link(dve.bn_stats(bn6[:, t, :], ps[:, 6 + t, :]))
                dve.bn_aggr(bn2[:, t, :], bn6[:, t, :]).then_inc(S["ct_bn"], 1)
            dve.wait_ge(S["ct_sd"], 1)
            link(dve.reciprocal(brs[:], bsd[:]))
            for t in range(T):
                dve.tensor_scalar(cn[:, t, :], ps[:, 6 + t, :], bn2[:, t, 0:1], brs[:, t:t + 1],
                                  ALU.subtract, ALU.mult).then_inc(S["cn_done"], 1)
            dve.wait_ge(S["o_ex"], HEADS * T)
            link(dve.reciprocal(o_r[:], o_sum[:]))
            for t in range(T):
                dve.wait_ge(S["o_pv"], t + 1)
                for a in range(2):
                    last = dve.tensor_tensor(od[:, t, :].rearrange("p (h a d) -> p a h d", a=2, d=HD)[:, a],
                                             ps[:, t, :].rearrange("p (a h d) -> p a h d", a=2, d=HD)[:, a],
                                             o_r[:, t, 4 * a:4 * a + 4].unsqueeze(2).broadcast_to([P, 4, HD]),
                                             ALU.mult)
                last.then_inc(S["o_norm"], 1)
            dve.wait_ge(S["c_hi"], 1)
            dve.tensor_tensor(o_lo[:, 0:4, :], cv[:], o_hi[:, 0:4, :].bitcast(F32), ALU.subtract).then_inc(S["c_lo"], 1)
            for t in range(T):
                dve.wait_ge(S["od_hi"], t + 1)
                tt = slice(t * P, (t + 1) * P)
                dve.tensor_tensor(o_lo[:, 4:8, tt], ps[:, 4 + t, :].rearrange("p (k s) -> p k s", k=4),
                                  o_hi[:, 4:8, tt].bitcast(F32), ALU.subtract).then_inc(S["od_lo"], 1)
            for g in range(G_OOUT, G_MOE):
                lo_static(g + RING)
                q = g - G_OOUT
                if q % 2:
                    n = q // 2
                    dve.wait_ge(pe_half, g + 1)
                    residual(n, (2 * n, 2 * n + 1), S["oo_add"])
            dve.wait_ge(S["oo_add"], 4)
            norm(3)
            dve.wait_ge(S["grow_in"], 16)
            dve.wait_ge(n_tr[3], 2 * T)
            for t in range(T):
                dve.tensor_tensor(m_xn[:, t, :], m_xn[:, t, :], gain_row[:], ALU.mult).then_inc(S["h_full"], 1)
            for t in range(T):
                dve.wait_ge(S["h_hi_s"], t + 1)
                dve.tensor_tensor(h_lo[:, t, :], m_xn[:, t, :], h_hi[:, t, :].bitcast(F32),
                                  ALU.subtract).then_inc(S["h_lo_s"], 1)
            dve.wait_ge(S["r_hi_s"], 1)
            dve.tensor_tensor(r_lo[:], router[:], r_hi[:].bitcast(F32), ALU.subtract).then_inc(S["r_lo_s"], 1)
            dve.wait_ge(S["r_mm"], 1)
            link(dve.tensor_copy(logit[:], ps[:, 0:T, 0:N_EXP]))
            for t in range(T):
                last = dve.max(top[:, t, :], logit[:, t, :])
            link(last)
            for t in range(T):
                last = dve.max_index(topi[:, t, :], top[:, t, :], logit[:, t, :])
            link(last)
            link(dve.tensor_copy(topf[:], topi[:]))
            dve.tensor_tensor(gate[:, :, 0], top[:, :, 1], top[:, :, 0], ALU.subtract).then_inc(S["g_exp"], 1)
            iota8 = cst[:, K_IOTA8:K_IOTA8 + 8]
            for t in range(T):
                for c in range(2):
                    last = dve.tensor_scalar(hot[:, t, c, :], iota8, topf[:, t, c:c + 1], None, ALU.is_equal)
            link(last)
            dve.tensor_tensor(sel[:], hot[:, :, 0, :], hot[:, :, 1, :], ALU.add).then_inc(S["sel_s"], 1)
            dve.wait_ge(S["g_exp"], 2)
            link(dve.tensor_scalar(gate[:, :, 2], gate[:, :, 1], 1.0, None, ALU.add))
            link(dve.reciprocal(gate[:, :, 3], gate[:, :, 2]))
            link(dve.tensor_tensor(gate[:, :, 2], gate[:, :, 1], gate[:, :, 3], ALU.mult))
            link(dve.memset(comb[:], 0.0))
            for t in range(T):
                last = dve.tensor_scalar(comb[:, t, 0:N_EXP], hot[:, t, 0, :], gate[:, t, 3:4], None, ALU.mult)
            link(last)
            for t in range(T):
                last = dve.scalar_tensor_tensor(out=comb[:, t, 0:N_EXP], in0=hot[:, t, 1, :], scalar=gate[:, t, 2:3],
                                                in1=comb[:, t, 0:N_EXP], op0=ALU.mult, op1=ALU.add)
            link(last)
            link(dve.memset(slot[:], -1.0))
            dve.wait_ge(S["cnt_mm"], 1)
            for t in range(T):
                last = dve.scalar_tensor_tensor(out=slot[:, t, 0:N_EXP], in0=ps[:, 2 + t, 0:N_EXP], scalar=1.0,
                                                in1=sel[:, t, :], op0=ALU.add, op1=ALU.mult)
            link(last)
            link(dve.tensor_scalar(slot[:, :, 0:N_EXP], slot[:, :, 0:N_EXP], -1.0, None, ALU.add))
            link(dve.tensor_scalar(over[:, 0, :], ps[:, 4, 0:N_EXP], float(P), None, ALU.is_gt))
            link(dve.memset(over[:, 2, :], 0.0))
            link(dve.tensor_tensor_scan(over[:, 1, :], over[:, 0, :], over[:, 2, :], 0.0, ALU.add, ALU.add))
            link(dve.tensor_tensor(over[:, 3, :], over[:, 1, :], over[:, 0, :], ALU.mult))
            link(dve.memset(jobs_f[:], 0.0))
            link(dve.tensor_copy(jobs_f[:, 0:N_EXP], iota8))
            link(dve.tensor_scalar(jobs_f[:, JOBS + 1:JOBS + 2], over[:, 1, N_EXP - 1:N_EXP], float(N_EXP), None, ALU.add))
            for k in range(OVERFLOW):
                link(dve.tensor_scalar(over_w[:, k, :], over[:, 3, :], float(k + 1), None, ALU.is_equal))
                for i in range(5):
                    src = (iota8, comb[:, 0, 0:N_EXP], comb[:, 1, 0:N_EXP], slot[:, 0, 0:N_EXP], slot[:, 1, 0:N_EXP])[i]
                    last = dve.tensor_tensor(over_t[:, k, i, :], src, over_w[:, k, :], ALU.mult)
                link(last)
                dve.tensor_reduce(jobs_f[:, N_EXP + k:N_EXP + k + 1], over_t[:, k, 0, :], AX, ALU.add)
                dve.tensor_reduce(comb[:, :, N_EXP + k], over_t[:, k, 1:3, :], AX, ALU.add)
                link(dve.tensor_reduce(slot[:, :, N_EXP + k], over_t[:, k, 3:5, :], AX, ALU.add))
            link(dve.tensor_scalar(slot[:, :, N_EXP:JOBS], slot[:, :, N_EXP:JOBS], -float(P), None, ALU.add))

            def make_pick(i):
                for t in range(T):
                    last = dve.tensor_scalar(pick[:, t, :], cst[:, K_IOTA:K_IOTA + P], slot[:, t, bass.ds(i, 1)],
                                             None, ALU.is_equal)
                last.then_inc(S["pk"], 1)

            def gather_lo(i):
                for h in range(2):
                    dve.wait_ge(S["ga_hi"], 2 * i + (h + 1))
                    dve.tensor_tensor(g_lo[:, 4 * h:4 * h + 4, :], ps[:, 7 - 2 * h, :].rearrange("p (k s) -> p k s", k=4),
                                      g_hi[:, 4 * h:4 * h + 4, :].bitcast(F32), ALU.subtract).then_inc(S["ga_lo"], 1)

            dve.tensor_copy(jobs_i[:], jobs_f[:]).then_inc(S["route"], 1)
            make_pick(0)
            gather_lo(0)
            dve.wait_ge(S["route"], 1)
            njobs = dve.value_load(jobs_i[0:1, JOBS + 1:JOBS + 2], min_val=N_EXP, max_val=JOBS)
            with dve.Fori(0, njobs) as j:
                def e_lo_evac(c):
                    dve.wait_ge(S["e_hi"], EC * j + (c + 1))
                    dve.tensor_tensor(ea_lo[:, 4 * c:4 * c + 4, :], ps[:, 2, :].rearrange("p (k s) -> p k s", k=4),
                                      ea_hi[:, 4 * c:4 * c + 4, :].bitcast(F32), ALU.subtract).then_inc(S["e_lo"], 1)

                for u in range(JOB):
                    lo(gm(j, u + RING), (G_MOE + u + RING) % RAW)
                    if u < 4 * EC and u % 4 == 1 and u > 1:
                        e_lo_evac(u // 4 - 1)
                    if u < 4 * EC and u % 4 == 3:
                        c = u // 4
                        dve.wait_ge(pe_half, gm(j, u + 1))
                        dve.wait_ge(S["e_silu"], EC * j + (c + 1))
                        if c:
                            dve.wait_ge(S["e_tr"], EC * j + c)
                        dve.tensor_tensor(e_a[:], ps[:, 1, :], e_s[:], ALU.mult).then_inc(S["e_ufree"], 1)
                    if u == 4 * EC + 1:
                        e_lo_evac(EC - 1)
                        dve.wait_ge(S["pk_r"], j + 1)
                        make_pick(j + 1)
                    if u == 4 * EC + 5:
                        gather_lo(j + 1)
                dve.wait_ge(S["y_hi_s"], j + 1)
                dve.tensor_tensor(y_lo[:], ps[:, 3:5, :].rearrange("p b c -> p (b c)"), y_hi[:].bitcast(F32),
                                  ALU.subtract).then_inc(S["y_lo_s"], 1)
                for i in range(4):
                    t, h = i // 2, i % 2
                    dve.wait_ge(S["sc_mm"], 4 * j + (i + 1))
                    dve.scalar_tensor_tensor(out=x[:, t, h * C:(h + 1) * C], in0=ps[:, 5 + h, :],
                                             scalar=comb[:, t, bass.ds(j, 1)], in1=x[:, t, h * C:(h + 1) * C],
                                             op0=ALU.mult, op1=ALU.add).then_inc(S["sc_add"], 1)
            dve.drain().then_inc(S["fin_n"], 1)
            dve.wait_ge(S["fin_n"], 1)
            norm_rstd(4, m_xn)
            dve.wait_ge(S["fin_in"], 16)
            for t in range(T):
                dve.scalar_tensor_tensor(out=m_xn[:, t, :], in0=x[:, t, :], scalar=rstd[:, 4, t:t + 1], in1=gain_row[:],
                                         op0=ALU.mult, op1=ALU.mult).then_inc(S["final_ok"], 1)

        @block.tensor
        def _(pe):
            def mm3(dst, a_hi, a_lo, b_hi, b_lo, start, stop):
                pe.matmul(dst, a_hi, b_hi, start=start, stop=False)
                pe.matmul(dst, a_hi, b_lo, start=False, stop=False)
                return pe.matmul(dst, a_lo, b_hi, start=False, stop=stop)

            def half_cols(g, r, a_hi, a_lo, k0, kn, banks, wd, start, stop, rows):
                pe.wait_ge(lo_done, g + 1)
                bh, bl = cols_view(whi[:, r, :], kn), cols_view(wlo[:, r, :], kn)
                for t, rs in enumerate(rows):
                    for k in range(kn):
                        last = mm3(ps[:, banks[t], 0:wd], a_hi[:, k0 + k, rs], a_lo[:, k0 + k, rs],
                                   bh[:, k, :], bl[:, k, :], start and k == 0, stop and k == kn - 1)
                last.then_inc(pe_half, 1)

            def half_rows(g, r, a_hi, a_lo, b0, banks, first, final, rows):
                pe.wait_ge(lo_done, g + 1)
                bh, bl = cols_view(whi[:, r, :], 2), cols_view(wlo[:, r, :], 2)
                for t, rs in enumerate(rows):
                    for k in range(2):
                        for h in range(2):
                            hs = slice(h * C, (h + 1) * C)
                            last = mm3(ps[:, banks[t][h], :], a_hi[:, b0 + k, rs], a_lo[:, b0 + k, rs],
                                       bh[:, k, hs], bl[:, k, hs], first and k == 0, final and k == 1)
                last.then_inc(pe_half, 1)

            BOTH = [slice(0, P), slice(P, SEQ)]

            def turn4(dst_bank, src_of, done, n=4):
                for i in range(n):
                    last = pe.transpose(ps[:, dst_bank, i * P:(i + 1) * P], src_of(i), ident)
                last.then_inc(done, 1)

            def norm_turn(n):
                for b in range(2 * T):
                    t, h = b // 2, b % 2
                    pe.wait_ge(n_xn[n], t + 1)
                    turn4(4 + b, lambda i: XN[n][:, t, (4 * h + i) * P:(4 * h + i + 1) * P], n_tr[n])

            pe.wait_ge(S["cst_in"], 16)
            pe.wait_ge(S["row_in"], 64)
            pe.transpose(ps[:, 0, 0:4 * KD], gains_row[:], ident[0:4 * KD, 0:4 * KD]).then_inc(S["gains_tr"], 1)
            norm_turn(0)
            pe.wait_ge(n_lo[0], 2 * T)
            pe.wait_ge(S["gains_ev"], 1)
            for g in range(G_IN, G_OUT):
                n = g // 2
                if g % 2 == 0 and n >= 2:
                    pe.wait_ge(S["ip_ev"], T * (n - 1))
                half_cols(g, g % RING, e_hi, e_lo, g % 2 * 4, 4, (2 * (n % 2), 2 * (n % 2) + 1), C,
                          g % 2 == 0, g % 2 == 1, BOTH)
            pe.wait_ge(S["roped"], 1)
            pe.wait_ge(S["ip_ev"], 6 * T)
            for i in range(8):
                part, t = i // 2, i % 2
                if i >= 4:
                    pe.wait_ge(S["at_ev_a"] if i % 2 == 0 else S["at_ev_d"], (i - 4) // 2 + 1)
                c0 = (0, C, 3 * C, 4 * C)[part]
                turn4(4 + i % 4, lambda b: proj[:, t, c0 + b * P:c0 + (b + 1) * P], S["at_tr"])
            pe.wait_ge(S["at_ev_a"], 4)
            pe.wait_ge(S["at_ev_d"], 4)

            def scores(t, kT, extra, done):
                n_k = P * (t + 1)
                per = C // n_k
                for b in range(HEADS // per):
                    bank = (0 if t == 0 else 2) + b
                    col = cst[0:1, K_COL + SEQ - n_k:K_COL + SEQ].unsqueeze(1).broadcast_to([1, per, n_k])
                    pe.matmul(ps[:, bank, :].rearrange("p (h k) -> p h k", h=per), cst[0:1, K_ROW:K_ROW + P], col,
                              start=True, stop=True)
                    if extra is not None:
                        pe.matmul(ps[:, bank, :].rearrange("p (h k) -> p h k", h=per), cst[:, K_FLIP:K_FLIP + P],
                                  extra[:, PLACED[b * per]:PLACED[b * per + per - 1] + 1:2, SEQ - n_k:SEQ],
                                  start=False, stop=True, skip_group_check=True)
                    for i in range(per):
                        s = PLACED[b * per + i]
                        half = slice((s % 2) * HD, (s % 2 + 1) * HD)
                        last = pe.matmul(ps[:, bank, i * n_k:(i + 1) * n_k], kT[half, s // 2, t * P:(t + 1) * P],
                                         kT[half, 4 + s // 2, 0:n_k], start=False, stop=True, skip_group_check=True)
                last.then_inc(done, 1)

            for t in range(T):
                scores(t, qkT, None, S["a_sc"])
            for i, (bank, t, kb) in enumerate(((6, 0, 0), (7, 1, 0), (0, 1, 1))):
                pe.wait_ge(S["a_pd"], A_HEADS * (t + 1))
                n_k = P * (t + 1)
                turn4(bank, lambda h: pd[:, t * C + h * n_k + kb * P:t * C + h * n_k + (kb + 1) * P], S["a_tr"])
            for t in range(T):
                pe.wait_ge(S["a_tev"], 1 if t == 0 else 3)
                for h in range(A_HEADS):
                    for kb in range(t + 1):
                        last = pe.matmul(ps[:, 1 + t, h * P:(h + 1) * P],
                                         pdT[:, (t + kb) * C + h * P:(t + kb) * C + (h + 1) * P],
                                         proj[:, kb, 2 * C + h * P:2 * C + (h + 1) * P], start=kb == 0, stop=kb == t)
                last.then_inc(S["a_pv"], 1)
            GROUPS = ((0, 0), (1, 1), (0, 1))
            pe.wait_ge(S["a_oev"], T)
            for i, (kb, qb) in enumerate(GROUPS):
                for b in range(2):
                    bank = 2 * i + b
                    if kb == qb:
                        pe.matmul(ps[:, bank, :].rearrange("p (h k) -> p h k", h=4), ident,
                                  cst[:, K_DMASK:K_DMASK + P].unsqueeze(1).broadcast_to([P, 4, P]),
                                  start=True, stop=True)
                    for j4 in range(4):
                        h = PLACED[4 * b + j4]
                        half = slice((h % 2) * HD, (h % 2 + 1) * HD)
                        last = pe.matmul(ps[:, bank, j4 * P:(j4 + 1) * P], qkT[half, 12 + h // 2, kb * P:(kb + 1) * P],
                                         qkT[half, 8 + h // 2, qb * P:(qb + 1) * P],
                                         start=kb != qb and j4 == 0, stop=True, skip_group_check=True)
                last.then_inc(S["b_z"], 1)
            ntri, nones = cst[:, K_NTRI:K_NTRI + P], cst[:, K_NONES:K_NONES + P]
            for i in range(3):
                pe.wait_ge(S["b_sp"], i + 1)
                for b in range(2):
                    bc = slice(b * C, (b + 1) * C)
                    if i == 2:
                        pe.matmul(ps[:, 2 * i + b, :], nones, sp[:, 1, bc], start=False, stop=True, skip_group_check=True)
                    last = pe.matmul(ps[:, 2 * i + b, :], ntri, sp[:, i, bc], start=False, stop=True, skip_group_check=True)
                last.then_inc(S["b_cum"], 1)
            for t in range(T):
                pe.wait_ge(S["b_w"], 1 if t == 0 else 3)
                for i, h in enumerate(PLACED):
                    vs = slice(5 * C + h * HD, 5 * C + (h + 1) * HD)
                    hs = slice(i * P, (i + 1) * P)
                    if t == 0:
                        last = pe.matmul(ps[:, 6, h * HD:(h + 1) * HD], wt[:, 0, hs], proj[:, 0, vs], start=True, stop=True)
                    else:
                        pe.matmul(ps[:, 7, h * HD:(h + 1) * HD], wt[:, 2, hs], proj[:, 0, vs], start=True, stop=False)
                        last = pe.matmul(ps[:, 7, h * HD:(h + 1) * HD], wt[:, 1, hs], proj[:, 1, vs], start=False, stop=True)
                last.then_inc(S["b_pv"], 1)
            pe.wait_ge(S["a_done"], 1)
            pe.wait_ge(S["b_ev"], T)
            for b in range(2 * T):
                t, h = b // 2, b % 2
                turn4(4 + b, lambda i: mixed[:, t, (4 * h + i) * P:(4 * h + i + 1) * P], S["mx_tr"])
            pe.wait_ge(S["mx_lo"], 2 * T)
            for g in range(G_OUT, G_FFN):
                q = g - G_OUT
                half_cols(g, g % RING, e_hi, e_lo, q % 2 * 4, 4, (q // 2 * 2, q // 2 * 2 + 1), C,
                          q % 2 == 0, q % 2 == 1, BOTH)
            norm_turn(1)
            pe.wait_ge(n_lo[1], 2 * T)

            def f_turn(c):
                pe.wait_ge(S["f_ufree"], T * (c + 1))
                if c:
                    pe.wait_ge(S["f_lo"], T * c)
                for t in range(T):
                    turn4(4 + t, lambda i: f_a[:, t, i * P:(i + 1) * P], S["f_tr"], min(4, D_FF // P - 4 * c))

            for g in range(G_FFN, G_DOWN):
                q = g - G_FFN
                c = q // 4
                if q < 4 * FFC:
                    up = q // 2 % 2
                    if q % 4 == 0 and c:
                        pe.wait_ge(S["f_silu"], T * c)
                    if q % 4 == 2 and c:
                        pe.wait_ge(S["f_ufree"], T * c)
                    half_cols(g, g % RING, f_hi, f_lo, q % 2 * 4, 4, (2 * up, 2 * up + 1), C,
                              q % 2 == 0, q % 2 == 1, BOTH)
                    if q % 4 == 1 and c:
                        f_turn(c - 1)
                else:
                    up = q - 4 * FFC
                    pe.wait_ge(S["f_ufree" if up else "f_silu"], T * FFC)
                    half_cols(g, g % RING, f_hi, f_lo, 0, KD, (2 * up, 2 * up + 1), D_FF - FFC * C, True, True, BOTH)
                    if not up:
                        f_turn(FFC - 1)
            pe.wait_ge(S["f_silu"], T * (FFC + 1))
            NV = D_FF // 256
            for v in range(NV):
                g = G_DOWN + v
                c = v // 2
                pe.wait_ge(S["f_lo"], T * (c + 1))
                half_rows(g, g % RING, fa_hi, fa_lo, 2 * v, ((0, 1), (6, 7)), v == 0, v == NV - 1, BOTH)
                if v == 0:
                    f_turn(FFC)
            norm_turn(2)
            pe.wait_ge(n_lo[2], 2 * T)
            for g in range(G_OIN, G_OOUT):
                q = g - G_OIN
                n = q // 2
                if q % 2 == 0 and n >= 2:
                    pe.wait_ge(S["oi_ev"], T * (n - 1))
                half_cols(g, g % RING, o_hi, o_lo, q % 2 * 4, 4, (2 * (n % 2), 2 * (n % 2) + 1), C,
                          q % 2 == 0, q % 2 == 1, BOTH)
                if q == 5:
                    pe.wait_ge(S["crow_in"], 64)
                    for b in range(4):
                        last = pe.transpose(ps[:, 6, b * (TAPS + 3):(b + 1) * (TAPS + 3)],
                                            conv_row[:, b * P:(b + 1) * P], ident[0:TAPS + 3, 0:TAPS + 3])
                    last.then_inc(S["cw_tr"], 1)
                    for t in range(T):
                        pe.wait_ge(S["u_mul"], t + 1)
                        turn4(4 + t, lambda i: oproj[:, t, i * P:(i + 1) * P], S["u_tr"])
            pe.wait_ge(S["oi_ev"], 5 * T)
            pe.wait_ge(S["u_ev"], T)
            for i in range(4):
                part, t = i // 2, i % 2
                turn4(4 + i, lambda b: oproj[:, t, (2 + part) * C + b * P:(2 + part) * C + (b + 1) * P], S["ot_tr"])
            pe.wait_ge(S["ot_ev"], 4)
            pe.wait_ge(S["bias_in"], 16)
            for t in range(T):
                scores(t, oqkT, bias, S["o_sc"])
            OT = [(0, 0, 0), (0, 0, 4), (1, 0, 0), (1, 0, 4), (1, 1, 0), (1, 1, 4)]
            pe.wait_ge(S["o_ex"], HEADS * T)
            for i, (t, kb, h0) in enumerate(OT):
                n_k = P * (t + 1)
                turn4(i, lambda h: po[:, t * D + (h0 + h) * n_k + kb * P:t * D + (h0 + h) * n_k + (kb + 1) * P], S["o_tr"])
            for t in range(T):
                pe.wait_ge(S["o_tev"], 6)
                for i, h in enumerate(PLACED):
                    for kb in range(t + 1):
                        last = pe.matmul(ps[:, t, i * HD:(i + 1) * HD],
                                         poT[:, ((t + kb) * HEADS + i) * P:((t + kb) * HEADS + i + 1) * P],
                                         oproj[:, kb, 4 * C + h * HD:4 * C + (h + 1) * HD],
                                         start=kb == 0, stop=kb == t)
                last.then_inc(S["o_pv"], 1)
            pe.wait_ge(S["conv_step"], 4 * TAPS)
            for t in range(T):
                turn4(6 + t, lambda i: cv[:, i, t * P:(t + 1) * P], S["ct_tr"])
            pe.wait_ge(S["cn_done"], T)
            for b2 in range(2):
                for b in range(2):
                    for t in range(T):
                        blk = 2 * b2 + b
                        last = pe.transpose(ps[:, 2 + b2, b * SEQ + t * P:b * SEQ + (t + 1) * P],
                                            cn[:, t, blk * P:(blk + 1) * P], ident)
                last.then_inc(S["cb_tr"], 1)
            for t in range(T):
                pe.wait_ge(S["o_norm"], t + 1)
                turn4(4 + t, lambda i: od[:, t, i * P:(i + 1) * P], S["od_tr"])
            pe.wait_ge(S["c_lo"], 1)
            pe.wait_ge(S["od_lo"], T)
            for g in range(G_OOUT, G_MOE):
                q = g - G_OOUT
                half_cols(g, g % RING, o_hi, o_lo, q % 2 * 4, 4, (q // 2 * 2, q // 2 * 2 + 1), C,
                          q % 2 == 0, q % 2 == 1, BOTH)
            norm_turn(3)
            pe.wait_ge(n_lo[3], 2 * T)
            pe.wait_ge(S["r_lo_s"], 1)
            pe.wait_ge(S["oo_add"], 4)
            for t in range(T):
                for k in range(KD):
                    last = mm3(ps[:, t, 0:N_EXP], m_hi[:, k, BOTH[t]], m_lo[:, k, BOTH[t]], r_hi[:, k, :], r_lo[:, k, :],
                               k == 0, k == KD - 1)
            last.then_inc(S["r_mm"], 1)
            pe.wait_ge(S["sel_s"], 1)
            lexc = cst[:, K_LEXC:K_LEXC + P]
            pe.matmul(ps[:, 2, 0:N_EXP], lexc, sel[:, 0, :], start=True, stop=True)
            pe.matmul(ps[:, 3, 0:N_EXP], ones, sel[:, 0, :], start=True, stop=False)
            pe.matmul(ps[:, 3, 0:N_EXP], lexc, sel[:, 1, :], start=False, stop=True)
            pe.matmul(ps[:, 4, 0:N_EXP], ones, sel[:, 0, :], start=True, stop=False)
            pe.matmul(ps[:, 4, 0:N_EXP], ones, sel[:, 1, :], start=False, stop=True).then_inc(S["cnt_mm"], 1)

            def gather(i):
                pe.wait_ge(S["pk_r"], i + 1)
                for h in range(2):
                    for c in range(4):
                        dst = ps[:, 7 - 2 * h, c * P:(c + 1) * P]
                        cs = slice((4 * h + c) * P, (4 * h + c + 1) * P)
                        for t in range(T):
                            pe.matmul(dst, h_hi[:, t, cs], pick_r[:, t, :], start=t == 0, stop=False)
                            last = pe.matmul(dst, h_lo[:, t, cs], pick_r[:, t, :], start=False, stop=t == T - 1)
                    last.then_inc(S["ga_mm"], 1)

            pe.wait_ge(S["h_lo_s"], T)
            gather(0)
            pe.wait_ge(S["route"], 1)
            njobs = pe.value_load(jobs_i[0:1, JOBS + 1:JOBS + 2], min_val=N_EXP, max_val=JOBS)
            ONE = [slice(0, P)]
            with pe.Fori(0, njobs) as j:
                pe.wait_ge(S["ga_lo"], 2 * j + 2)
                for u in range(JOB):
                    g, r = gm(j, u), (G_MOE + u) % RING
                    if u < 4 * EC:
                        c, up = u // 4, u // 2 % 2
                        if u % 4 == 0 and c:
                            pe.wait_ge(S["e_silu"], EC * j + c)
                        if u % 4 == 2 and c:
                            pe.wait_ge(S["e_ufree"], EC * j + c)
                        half_cols(g, r, g_hi, g_lo, u % 2 * 4, 4, (up,), C, u % 2 == 0, u % 2 == 1, ONE)
                    else:
                        v = u - 4 * EC
                        pe.wait_ge(S["e_lo"], EC * j + (v // 2 + 1))
                        half_rows(g, r, ea_hi, ea_lo, 2 * v, ((3, 4),), v == 0, v == 2 * EC - 1, ONE)
                    if u == 1:
                        for t in range(T):
                            last = pe.transpose(ps[:, 7, t * P:(t + 1) * P], pick[:, t, :], ident)
                        last.then_inc(S["pt_mm"], 1)
                    if (u < 4 * EC and u % 4 == 1 and u > 1) or u == 4 * EC + 1:
                        c = (u - 4) // 4 if u < 4 * EC else EC - 1
                        pe.wait_ge(S["e_ufree"], EC * j + (c + 1))
                        if c:
                            pe.wait_ge(S["e_lo"], EC * j + c)
                        turn4(2, lambda i: e_a[:, i * P:(i + 1) * P], S["e_tr"])
                    if u == 4 * EC + 4:
                        pe.wait_ge(S["pt_ev"], j + 1)
                        gather(j + 1)
                pe.wait_ge(S["y_lo_s"], j + 1)
                for i in range(4):
                    t, h = i // 2, i % 2
                    if i >= 2:
                        pe.wait_ge(S["sc_add"], 4 * j + (i - 1))
                    if i == 0:
                        pe.wait_ge(S["ga_lo"], 2 * j + 4)
                    hs = slice(h * C, (h + 1) * C)
                    pe.matmul(ps[:, 5 + h, :], put_r[:, t, :], y_hi[:, hs], start=True, stop=False)
                    pe.matmul(ps[:, 5 + h, :], put_r[:, t, :], y_lo[:, hs], start=False, stop=True).then_inc(S["sc_mm"], 1)


_INS = ['x', 'ev_norm_mix', 'ev_w_in', 'ev_lambda_q1', 'ev_lambda_k1', 'ev_lambda_q2', 'ev_lambda_k2',
        'ev_subln', 'ev_w_out', 'ev_norm_ffn', 'ev_ffn_gate', 'ev_ffn_up', 'ev_ffn_down',
        'od_norm_mix', 'od_w_in', 'od_conv_w', 'od_conv_b', 'od_conv_ln_g', 'od_conv_ln_b', 'od_rel_bias',
        'od_w_out', 'od_norm_ffn', 'od_router', 'od_exp_gate', 'od_exp_up', 'od_exp_down', 'final_norm']


def kernel(**inputs):
    import numpy as _np
    import concourse.bacc as _bacc
    from concourse import mybir as _mybir
    from concourse.bass_utils import run_bass_kernel_spmd as _run

    nc = _bacc.Bacc("TRN2", target_bir_lowering=False, num_devices=1)
    arrays, aps = {}, {}
    for name in _INS + ["cst"]:
        a = constants() if name == "cst" else _np.ascontiguousarray(inputs[name])
        arrays[f"in_{name}_dram"] = a
        aps[name] = nc.dram_tensor(f"in_{name}_dram", a.shape, _mybir.dt.from_np(a.dtype), kind="ExternalInput").ap()
    out = nc.dram_tensor("out_0_dram", (1, SEQ, D), _mybir.dt.float32, kind="ExternalOutput").ap()
    trunk(nc, aps, out)
    r = _run(nc, [arrays], core_ids=[0])
    return r.results[0]["out_0_dram"]
```

```python
from contextlib import ExitStack

import numpy as np

import concourse.bass as bass
from concourse import mybir

ALU = mybir.AluOpType
ACT = mybir.ActivationFunctionType
AX = mybir.AxisListType.X
F32 = mybir.dt.float32
F32R = mybir.dt.float32r
I32 = mybir.dt.int32
U32 = mybir.dt.uint32

P = 128
SEQ = 256
T = SEQ // P
D = 1024
KD = D // P
C = 512
HD = 64
A_HEADS = 4
HEADS = 8
PLACED = [0, 2, 4, 6, 1, 3, 5, 7]
D_FF = 2816
E_FF = 3584
N_EXP = 8
TAPS = 31
CONV_C = 512
CHUNK = 64
MAX_REL = 128
REL = 2 * MAX_REL + 1
EPS = 1e-6
LAMBDA_INIT = 0.2
NEG = -1e30

TAP_CUT = (10, 15, 5)
RAW = 6
RING = 3
HALF = 2048
FFC = D_FF // C
EC = E_FF // C
G_IN = 0
G_OUT = G_IN + 12
G_FFN = G_OUT + 4
G_DOWN = G_FFN + 4 * FFC + 2
G_OIN = G_DOWN + D_FF // 256
G_OOUT = G_OIN + 10
G_MOE = G_OOUT + 4
JOB = 6 * EC
assert JOB % RAW == 0 and JOB % RING == 0 and G_MOE % RING == 0
MID = 4 * EC + 2
LEAD = 2

K_IDENT, K_IOTA, K_FOLD, K_IOTA8 = 0, P, 3 * P, 4 * P
K_KEPT = K_IOTA8 + 8
K_NTRI, K_NONES, K_DMASK, K_FLIP, K_ROW = (P * i for i in range(5))
K_COL = K_ROW + P
K_ROUND = K_COL + SEQ
K_LEXC, K_ONES = K_ROUND, K_ROUND + P
K_COS = K_ONES + P
K_SIN = K_COS + T * 32
K_ALL = K_SIN + T * 32


def constants():
    kept, c = np.zeros((P, K_KEPT), np.float32), np.zeros((P, K_ALL), np.float32)
    p, i = np.arange(P)[:, None], np.arange(P)[None, :]
    kept[:, K_IDENT:K_IDENT + P] = p == i
    kept[:, K_IOTA:K_IOTA + SEQ] = np.arange(SEQ)
    kept[:, K_FOLD:K_FOLD + P] = p % (P // 2) == i % (P // 2)
    kept[:, K_IOTA8:K_IOTA8 + 8] = np.arange(8)
    c[:, K_NTRI:K_NTRI + P] = np.where(p >= i, -1.0, 0.0)
    c[:, K_DMASK:K_DMASK + P] = np.where(p >= i, NEG, 0.0)
    c[:, K_LEXC:K_LEXC + P] = p < i
    c[:, K_ONES:K_ONES + P] = 1.0
    c[:, K_NONES:K_NONES + P] = -1.0
    c[:, K_FLIP:K_FLIP + P] = p + i == P - 1
    half = HD // 2
    freq = (np.float32(10000.0) ** (-np.arange(half, dtype=np.float32) * np.float32(2.0) / np.float32(HD)))
    ang = np.arange(SEQ, dtype=np.float32)[:, None] * freq.astype(np.float32)[None, :]
    ang = ang.reshape(T, P, half).transpose(1, 0, 2).reshape(P, T * half)
    c[:, K_COS:K_COS + T * half] = np.cos(ang)
    c[:, K_SIN:K_SIN + T * half] = np.sin(ang)
    c[:, K_ROW:K_ROW + P] = i < CHUNK
    c[:, K_COL:K_COL + SEQ] = np.where(np.arange(SEQ) >= SEQ - CHUNK, NEG, 0.0)
    return np.concatenate([kept, c], axis=1)


def trunk(nc, w, out):
    ctx = ExitStack()
    with ctx:
        def sb(name, shape, dt=F32, at=ctx):
            return at.enter_context(nc.sbuf_tensor(name, shape, dt))

        def sem(name):
            return ctx.enter_context(nc.semaphore(name))

        raw = sb("raw", [P, RAW, HALF])
        whi = sb("whi", [P, RING, HALF], F32R)
        wlo = sb("wlo", [P, RING, HALF], F32R)
        x = sb("x", [P, T, D])
        kept = sb("kept", [P, K_KEPT])
        gains_row = sb("gains_row", [4 * KD, P])
        gains = sb("gains", [P, 4, KD])
        ss = sb("ss", [P, 5, T])
        std = sb("std", [P, 5, T])
        rstd = sb("rstd", [P, 5, T])
        rstd_q = sb("rstd_q", [P, 3, T])
        eps = sb("eps", [P, 1])
        ident = kept[:, K_IDENT:K_IDENT + P]

        layers = ExitStack()
        cst = sb("cst", [P, K_ALL], F32, layers)
        ones = cst[:, K_ONES:K_ONES + P]
        cst_r = sb("cst_r", [P, K_ROUND], F32R, layers)
        ident_r = sb("ident_r", [P, P], F32R, layers)
        with ExitStack() as even:
            with ExitStack() as tmp:
                sp = sb("sp", [P, 3, D], F32, tmp)
            with ExitStack() as tmp:
                sp_lo = sb("sp_lo", [P, 3, D], F32R, tmp)
            e_hi = sb("e_hi", [P, KD, SEQ], F32R, even)
            e_lo = sb("e_lo", [P, KD, SEQ], F32R, even)
            with ExitStack() as tmp:
                e_junk = sb("e_junk", [P, D], F32, tmp)
                e_full = sb("e_full", [P, 2 * T, C], F32, tmp)
                rope_a = sb("rope_a", [P, C], F32, tmp)
                rope_b = sb("rope_b", [P, C], F32, tmp)
            with ExitStack() as tmp:
                pa = sb("pa", [P, HEADS * 3 * P], F32, tmp)
                pd = sb("pd", [P, A_HEADS * 3 * P], F32, tmp)
                pdT = sb("pdT", [P, A_HEADS * 3 * P], F32, tmp)
            with ExitStack() as tmp:
                wt = sb("wt", [P, 3, D], F32, tmp)
            sb("even_tmp", [P, 6 * D], F32, even)
            proj = sb("proj", [P, T, 6 * C], F32, even)
            with ExitStack() as tmp:
                sp_hi = sb("sp_hi", [P, 3, D], F32R, tmp)
            qkT = sb("qkT", [P, 16, SEQ], F32, even)
            mixed = sb("mixed", [P, T, D], F32, even)
            lam_in = sb("lam_in", [P, 4, HD], F32, even)
            lam_j = sb("lam_j", [P, HD], F32, even)
            lam_s = sb("lam_s", [P, 4], F32, even)
            subln = sb("subln", [P, P], F32, even)
            a_nm = sb("a_nm", [P, T, HEADS], F32, even)
            a_sum = sb("a_sum", [P, T, HEADS], F32, even)
            a_r = sb("a_r", [P, T, HEADS], F32, even)
            a_ms = sb("a_ms", [P, T, A_HEADS], F32, even)
            a_sd = sb("a_sd", [P, T, A_HEADS], F32, even)
            a_rs = sb("a_rs", [P, T, A_HEADS], F32, even)
        with ExitStack() as ffn:
            fa_lo = sb("fa_lo", [P, D_FF // P, SEQ], F32R, ffn)
            f_hi = sb("f_hi", [P, KD, SEQ], F32R, ffn)
            f_lo = sb("f_lo", [P, KD, SEQ], F32R, ffn)
            f_full = sb("f_full", [P, 2 * T, C], F32, ffn)
            fa_hi = sb("fa_hi", [P, D_FF // P, SEQ], F32R, ffn)
            f_s = sb("f_s", [P, T, C], F32, ffn)
            f_a = sb("f_a", [P, T, C], F32, ffn)
        with ExitStack() as odd:
            o_hi = sb("o_hi", [P, KD, SEQ], F32R, odd)
            o_lo = sb("o_lo", [P, KD, SEQ], F32R, odd)
            with ExitStack() as tmp:
                o_junk = sb("o_junk", [P, D], F32, tmp)
                o_full = sb("o_full", [P, 2 * T, C], F32, tmp)
            with ExitStack() as tmp:
                po = sb("po", [P, HEADS * 3 * P], F32, tmp)
                with ExitStack() as tmp2:
                    bias_hi = sb("bias_hi", [P, HEADS, SEQ], F32R, tmp2)
                poT = sb("poT", [P, HEADS * 3 * P], F32, tmp)
            sb("odd_tmp", [P, 6 * D], F32, odd)
            oproj = sb("oproj", [P, T, 5 * C], F32, odd)
            oqkT = sb("oqkT", [P, 8, SEQ], F32, odd)
            uT = sb("uT", [P, 4, TAPS - 1 + SEQ], F32, odd)
            cv = sb("cv", [P, 4, SEQ], F32, odd)
            cn = oproj[:, :, 0:C]
            od = oproj[:, :, C:2 * C]
            conv_row = sb("conv_row", [TAPS + 3, CONV_C], F32, odd)
            conv = sb("conv", [P, 4, TAPS + 3], F32, odd)
            rel_in = sb("rel_in", [HEADS, REL], F32, odd)
            rel_rev = sb("rel_rev", [HEADS, 3 * P], F32, odd)
            with ExitStack() as tmp:
                bias = sb("bias", [P, HEADS, SEQ], F32, tmp)
            bias_lo = sb("bias_lo", [P, HEADS, SEQ], F32R, odd)
            o_nm = sb("o_nm", [P, T, HEADS], F32, odd)
            o_sum = sb("o_sum", [P, T, HEADS], F32, odd)
            o_r = sb("o_r", [P, T, HEADS], F32, odd)
            bn6 = sb("bn6", [P, T, 6], F32, odd)
            bn2 = sb("bn2", [P, T, 2], F32, odd)
            bsd = sb("bsd", [P, T], F32, odd)
            brs = sb("brs", [P, T], F32, odd)
        layers.close()
        with ExitStack() as moe:
            with ExitStack() as tmp:
                sb("cst_still", [P, K_ALL + K_ROUND + P], F32, tmp)
                sb("o_hi_still", [P, 2 * KD, SEQ], F32R, tmp)
                m_full = sb("m_full", [P, 2 * T, C], F32, tmp)
                m_junk = sb("m_junk", [P, D], F32, tmp)
                gain_row = sb("gain_row", [P, D], F32, tmp)
                router = sb("router", [P, KD, N_EXP], F32, tmp)
                logit = sb("logit", [P, T, N_EXP], F32, tmp)
                top = sb("top", [P, T, 8], F32, tmp)
                topi = sb("topi", [P, T, 8], U32, tmp)
                topf = sb("topf", [P, T, 8], F32, tmp)
                gate = sb("gate", [P, T, 4], F32, tmp)
                hot = sb("hot", [P, T, 2, N_EXP], F32, tmp)
                sel = sb("sel", [P, T, N_EXP], F32, tmp)
            with ExitStack() as tmp:
                ea_hi = sb("ea_hi", [P, E_FF // P, SEQ], F32R, tmp)
                ea_lo = sb("ea_lo", [P, E_FF // P, SEQ], F32R, tmp)
            with ExitStack() as tmp:
                fin_x = sb("fin_x", [P, T, D], F32, tmp)
            sb("moe_tmp", [P, 4 * E_FF], F32, moe)
            y_hi = sb("y_hi", [P, D], F32R, moe)
            y_lo = sb("y_lo", [P, D], F32R, moe)
            h_all = sb("h_all", [P, T, D], F32, moe)
            g_hi = sb("g_hi", [P, KD, SEQ], F32R, moe)
            g_lo = sb("g_lo", [P, KD, SEQ], F32R, moe)
            e_a = sb("e_a", [P, 2, C], F32, moe)
            pick = sb("pick", [P, T, SEQ], F32, moe)
            put_r = sb("put_r", [P, 2, T, P], F32R, moe)
            comb = sb("comb", [P, T, N_EXP], F32, moe)
            slot = sb("slot", [P, T, N_EXP + 1], F32, moe)
            slot_b = sb("slot_b", [P, T, N_EXP + 1], F32, moe)
            over_f = sb("over_f", [P, 16], F32, moe)
            over_i = sb("over_i", [P, 16], I32, moe)

        ps = ctx.enter_context(nc.psum_tensor("ps", [P, 8, C], F32))
        rel_dram = nc.dram_tensor("rel_scratch", (HEADS, 3 * P), F32, kind="Internal")

        raw_in = [sem(f"raw_in{s}") for s in range(RAW)]
        hi_done = sem("hi_done")
        lo_done = sem("lo_done")
        pe_half = sem("pe_half")
        S = {n: sem(n) for n in (
            "x_in cst_in cst2_in row_in lam_ld sub_in crow_in rel_ld rel_st bias_in router_in grow_in fin_in out_st "
            "eps_set gains_tr gains_ev "
            "ip_ev roped at_tr at_ev_a at_ev_d a_sc a_mx a_ex a_pd a_tr a_tev a_pv a_oev a_msq a_sqrt a_done "
            "lam_sum lam_exp b_z b_ex b_ln b_sp b_sph b_spl cr_a cr_b b_cum b_w b_pv b_ev mx_tr mx_hi mx_lo op_add "
            "f_silu f_ufree f_tr f_hi f_lo f_add "
            "oi_ev u_mul u_tr u_ev cw_tr conv_step ct_tr ct_bn ct_sd cn_done cb_tr c_act c_hi c_lo "
            "rel_rv bias_m bias_h bias_l ot_tr ot_ev o_sc o_mx o_ex o_tr o_tev o_pv o_norm od_tr od_hi od_lo oo_add uz "
            "xg h_full r_mm cnt_mm sel_s route g_exp pk ga_mm ga_hi ga_lo pt_mm pt_ev "
            "e_raw e_fold e_silu e_ufree e_tr e_hi e_lo y_hi_s y_lo_s sc_mm sc_add fin_n load_turn dve_chain act_chain final_ok "
        ).split()}
        NORMS = 4
        n_ss = [sem(f"n_ss{i}") for i in range(NORMS + 1)]
        n_std = [sem(f"n_std{i}") for i in range(NORMS + 1)]
        n_rs = [sem(f"n_rs{i}") for i in range(NORMS)]
        n_tr = [sem(f"n_tr{i}") for i in range(NORMS)]
        n_full = [sem(f"n_full{i}") for i in range(NORMS)]
        n_hi = [sem(f"n_hi{i}") for i in range(NORMS - 1)]
        n_lo = [sem(f"n_lo{i}") for i in range(NORMS - 1)]

        BLOCKS = [(0, 0), (0, 1), (1, 0), (1, 1)]
        TURN_BANK = [(4, 5, 6, 7), (4, 5, 6, 7), (2, 3, 4, 5), (4, 5, 6, 7)]
        JUNK = [e_junk[:], f_s[:].rearrange("p t c -> p (t c)"), o_junk[:], m_junk[:]]
        FULL = [e_full, f_full, o_full, m_full]
        HI = [e_hi, f_hi, o_hi]
        LO = [e_lo, f_lo, o_lo]
        X_SUM = [None, S["op_add"], S["f_add"], S["oo_add"]]

        def cols_view(ap, k=4):
            return ap.rearrange("p (k n) -> p k n", k=k)

        def cols_src(m, k0, kn, c0, cn_):
            return m.rearrange("(k p) n -> p k n", p=P)[:, k0:k0 + kn, c0:c0 + cn_]

        def rows_src(m, b0, bn):
            return m[b0 * P:(b0 + bn) * P, :].rearrange("(b p) n -> p b n", p=P)

        W_IN, W_OUT = w["ev_w_in"][0], w["ev_w_out"][0]
        W_G, W_U, W_D = w["ev_ffn_gate"][0], w["ev_ffn_up"][0], w["ev_ffn_down"][0]
        O_IN, O_OUT = w["od_w_in"][0], w["od_w_out"][0]

        def static_src(g):
            if g < G_OUT:
                return cols_src(W_IN, g % 2 * 4, 4, g // 2 * C, C), 4
            if g < G_FFN:
                g -= G_OUT
                return cols_src(W_OUT, g % 2 * 4, 4, g // 2 * C, C), 4
            if g < G_DOWN:
                g -= G_FFN
                if g >= 4 * FFC:
                    return cols_src((W_G, W_U)[g - 4 * FFC], 0, KD, FFC * C, D_FF - FFC * C), KD
                return cols_src((W_G, W_U)[g // 2 % 2], g % 2 * 4, 4, g // 4 * C, C), 4
            if g < G_OIN:
                return rows_src(W_D, 2 * (g - G_DOWN), 2), 2
            if g < G_OOUT:
                g -= G_OIN
                return cols_src(O_IN, g % 2 * 4, 4, g // 2 * C, C), 4
            g -= G_OOUT
            return cols_src(O_OUT, g % 2 * 4, 4, g // 2 * C, C), 4

        EG = w["od_exp_gate"][0].rearrange("e (k p) n -> p e k n", p=P)
        EU = w["od_exp_up"][0].rearrange("e (k p) n -> p e k n", p=P)
        ED = w["od_exp_down"][0].rearrange("e (b p) n -> p e b n", p=P)

        def expert_src(e, u):
            one = bass.ds(e, 1)
            if u < 4 * EC:
                m, c0, k0 = (EG, EU)[u // 2 % 2], u // 4 * C, u % 2 * 4
                return m[:, one, k0:k0 + 4, c0:c0 + C].rearrange("p e k n -> p (e k) n"), 4
            b0 = 2 * (u - 4 * EC)
            return ED[:, one, b0:b0 + 2, :].rearrange("p e b n -> p (e b) n"), 2

        def gm(j, u):
            return j * JOB + (G_MOE + u)

        block = ctx.enter_context(nc.Block())

        @block.sync
        def _(sp_):
            def load_half(g, s, src, k):
                if not isinstance(g, int) or g >= RAW:
                    sp_.wait_ge(lo_done, g - (RAW - 1))
                    if not isinstance(g, int):
                        sp_.sem_inc(S["load_turn"], 1)
                sp_.dma_start(cols_view(raw[:, s, :], k), src).then_inc(raw_in[s], 16)

            sp_.dma_start(x[:], w["x"][0].rearrange("(t p) d -> p t d", p=P)).then_inc(S["x_in"], 16)
            sp_.dma_start(kept[:], w["cst"][:, 0:K_KEPT]).then_inc(S["cst_in"], 16)
            for i, name in enumerate(("ev_norm_mix", "ev_norm_ffn", "od_norm_mix", "od_norm_ffn")):
                sp_.dma_start(gains_row[i * KD:(i + 1) * KD, :],
                              w[name][0].rearrange("(k p) -> k p", p=P)).then_inc(S["row_in"], 16)
            for g in range(RAW):
                load_half(g, g % RAW, *static_src(g))
                if g == RING:
                    sp_.dma_start(cst[:], w["cst"][:, K_KEPT:K_KEPT + K_ALL]).then_inc(S["cst2_in"], 16)
            for i, name in enumerate(("ev_lambda_q1", "ev_lambda_k1", "ev_lambda_q2", "ev_lambda_k2")):
                sp_.dma_start(lam_in[:, i, :], w[name].broadcast_to([P, HD])).then_inc(S["lam_ld"], 16)
            sp_.dma_start(subln[:], w["ev_subln"].broadcast_to([P, P])).then_inc(S["sub_in"], 16)
            for g in range(RAW, G_OIN + RAW):
                load_half(g, g % RAW, *static_src(g))
            sp_.wait_ge(S["f_add"], 4)
            for r0, rn, name in ((0, TAPS, "od_conv_w"), (TAPS, 1, "od_conv_b"),
                                 (TAPS + 1, 1, "od_conv_ln_g"), (TAPS + 2, 1, "od_conv_ln_b")):
                src = w[name][0] if rn > 1 else w[name]
                sp_.dma_start(conv_row[r0:r0 + rn, :], src).then_inc(S["crow_in"], 16)
            sp_.dma_start(rel_in[:], w["od_rel_bias"][0]).then_inc(S["rel_ld"], 16)
            sp_.wait_ge(S["rel_rv"], 2)
            sp_.dma_start(rel_dram.ap(), rel_rev[:]).then_inc(S["rel_st"], 16)
            sp_.wait_ge(S["rel_st"], 16)
            hankel = bass.AP(rel_dram, 0, [[1, P], [3 * P, HEADS], [1, SEQ]])
            sp_.dma_start(bias[:], hankel).then_inc(S["bias_in"], 16)
            for g in range(G_OIN + RAW, G_MOE):
                load_half(g, g % RAW, *static_src(g))
            for u in range(RAW):
                load_half(G_MOE + u, (G_MOE + u) % RAW, *expert_src(0, u))
                if u == 0:
                    sp_.wait_ge(S["od_lo"], T)
                    sp_.dma_start(gain_row[:], w["od_norm_ffn"].broadcast_to([P, D])).then_inc(S["grow_in"], 16)
                    sp_.dma_start(router[:],
                                  w["od_router"][0].rearrange("(k p) e -> p k e", p=P)).then_inc(S["router_in"], 16)

            def load_rest(j, e, u0, u1):
                for u in range(u0, u1):
                    load_half(gm(j, u), (G_MOE + u) % RAW, *expert_src(e, u % JOB))

            with sp_.Fori(0, N_EXP - 1) as j:
                load_rest(j, j, RAW, JOB)
                load_rest(j, j + 1, JOB, JOB + RAW)
            load_rest(N_EXP - 1, N_EXP - 1, RAW, JOB)
            load_rest(N_EXP - 1, 0, JOB, JOB + RAW - 1)
            sp_.wait_ge(S["ga_mm"], 4 * (N_EXP + 1))
            sp_.dma_start(h_all[:, 0, :], w["final_norm"].rearrange("(a d) -> a d", a=1).broadcast_to([P, D])).then_inc(S["fin_in"], 16)
            for s in range(RAW):
                n_loads = (G_MOE + N_EXP * JOB + RAW - 2 - s) // RAW + 1
                sp_.wait_ge(raw_in[s], 16 * n_loads)
            for t in range(T):
                sp_.wait_ge(S["final_ok"], t + 1)
                sp_.dma_start(out[0, t * P:(t + 1) * P, :], fin_x[:, t, :]).then_inc(S["out_st"], 16)
            sp_.wait_ge(S["out_st"], 16 * T)

        Z_BANK = (6, 0, 2)
        A_TURN = (4, 5, 4)
        A_OUT = (5, 4)

        def z_of(i):
            return ps[:, Z_BANK[i]:Z_BANK[i] + 2, :].rearrange("p b c -> p (b c)")

        def place(n, r):
            return ((2, 6)[r % 2], 0) if n == 2 else ((4, 6)[r // 2], r % 2 * (C // 2))

        TILE_OF = lambda n, r: r // 2 if n == 2 else 0
        COL_OF = lambda n, r: r % 2 * C + (0 if n == 2 else r // 2 * (C // 2))
        WIDE = lambda n: n * (C // 2)

        def by_tiles(eng, many, body):
            with eng.If(many > 0):
                body(2)
            with eng.Else():
                body(1)

        def by_form(eng, many, body):
            with eng.If(many > 1):
                body(2, False)
            with eng.Else():
                by_tiles(eng, many, lambda n: body(n, n == 2))

        def many_of(eng, e):
            return eng.value_load(over_i[0:1, bass.ds(e, 1)], min_val=0, max_val=2)

        H = P // 2

        @block.scalar
        def _(act):
            chain = [0]

            def link(ins):
                chain[0] += 1
                ins.then_inc(S["act_chain"], 1)
                act.wait_ge(S["act_chain"], chain[0])

            def hi(g, s, landed):
                act.wait_ge(raw_in[s], landed)
                if not isinstance(g, int) or g >= RING:
                    act.wait_ge(pe_half, g - (RING - 1))
                r = (s % RING)
                act.copy(whi[:, r, :], raw[:, s, :]).then_inc(hi_done, 1)

            def hi_static(g):
                hi(g, g % RAW, 16 * (g // RAW + 1))

            def norm_std(n):
                if n == NORMS:
                    act.wait_ge(n_ss[n], T)
                else:
                    act.wait_ge(X_SUM[n] if n else S["x_in"], 4 if n else 16)
                    for t in range(T):
                        link(act.activation(JUNK[n], x[:, t, :], ACT.Square, accum_out=ss[:, n, t:t + 1]))
                act.activation(std[:, n, :], ss[:, n, :], ACT.Sqrt, bias=eps[:], scale=1.0 / D).then_inc(n_std[n], 1)

            def norm_hi(n, bs=range(2 * T)):
                for b in bs:
                    act.wait_ge(n_full[n], b + 1)
                    h, t = BLOCKS[b]
                    act.copy(HI[n][:, 4 * h:4 * h + 4, t * P:(t + 1) * P],
                             FULL[n][:, b, :].rearrange("p (k s) -> p k s", k=4)).then_inc(n_hi[n], 1)

            act.wait_ge(S["eps_set"], 1)
            norm_hi(0)
            for g in range(RING):
                hi_static(g)
            norm_std(0)
            act.wait_ge(S["cst2_in"], 16)
            act.copy(cst_r[:], cst[:, 0:K_ROUND]).then_inc(S["cr_a"], 1)
            act.copy(ident_r[:], ident).then_inc(S["cr_b"], 1)
            for g in range(G_IN, G_OUT):
                hi_static(g + RING)
                if g % 2:
                    n = g // 2
                    act.wait_ge(pe_half, g + 1)
                    act.wait_ge(n_rs[0], 1)
                    for t in range(T):
                        act.activation(proj[:, t, n * C:(n + 1) * C], ps[:, 2 * (n % 2) + t, :], ACT.Copy,
                                       scale=(rstd_q if n in (0, 3) else rstd)[:, 0, t:t + 1]).then_inc(S["ip_ev"], 1)
            for i in range(0, 8, 2):
                act.wait_ge(S["at_tr"], i + 1)
                part, t = i // 2, i % 2
                act.copy(qkT[:, 4 * part:4 * part + 4, t * P:(t + 1) * P],
                         ps[:, 4 + i % 4, :].rearrange("p (k s) -> p k s", k=4)).then_inc(S["at_ev_a"], 1)
            act.wait_ge(S["lam_sum"], 2)
            act.activation(lam_s[:, 2:4], lam_s[:, 0:2], ACT.Exp).then_inc(S["lam_exp"], 1)
            for t in range(T):
                act.wait_ge(S["a_mx"], t + 1)
                n_k = P * (t + 1)
                off = t * HEADS * P
                for s in range(HEADS):
                    src = ps[:, 0 if t == 0 else 2:, :].rearrange("p b c -> p (b c)")[:, s * n_k:(s + 1) * n_k]
                    act.activation(pa[:, off + s * n_k:off + (s + 1) * n_k], src, ACT.Exp,
                                   bias=a_nm[:, t, s:s + 1], accum_out=a_sum[:, t, s:s + 1]).then_inc(S["a_ex"], 1)
            def b_exp(i):
                act.wait_ge(S["b_z"], i + 1)
                link(act.activation(sp[:, i, :], z_of(i), ACT.Abs))
                act.activation(sp[:, i, :], sp[:, i, :], ACT.Exp, scale=-1.0).then_inc(S["b_ex"], 1)

            def a_turned(i):
                act.wait_ge(S["a_tr"], i + 1)
                act.copy(pdT[:, i * C:(i + 1) * C], ps[:, A_TURN[i], :]).then_inc(S["a_tev"], 1)

            b_exp(0)
            a_turned(0)
            b_exp(1)
            a_turned(1)
            a_turned(2)
            b_exp(2)
            for i in range(3):
                act.wait_ge(S["b_ex"], i + 1)
                act.activation(sp[:, i, :], sp[:, i, :], ACT.Ln, bias=1.0).then_inc(S["b_ln"], 1)
            for t in range(T):
                act.wait_ge(S["a_pv"], t + 1)
                act.copy(mixed[:, t, 0:C], ps[:, A_OUT[t], :]).then_inc(S["a_oev"], 1)
            for i in range(3):
                act.wait_ge(S["b_sp"], i + 1)
                act.copy(sp_hi[:, i, :], sp[:, i, :]).then_inc(S["b_sph"], 1)
            act.wait_ge(S["a_msq"], 1)
            act.activation(a_sd[:], a_ms[:], ACT.Sqrt, bias=eps[:], scale=1.0 / P).then_inc(S["a_sqrt"], 1)
            act.wait_ge(S["a_pd"], A_HEADS * T)
            for i in range(3):
                act.wait_ge(S["b_cum"], i + 1)
                act.activation(wt[:, i, :], z_of(i), ACT.Exp).then_inc(S["b_w"], 1)
            for t in range(T):
                act.wait_ge(S["b_pv"], t + 1)
                act.copy(mixed[:, t, C:D], ps[:, 6 + t, :]).then_inc(S["b_ev"], 1)
            for b in range(2 * T):
                act.wait_ge(S["mx_tr"], b + 1)
                t, h = b // 2, b % 2
                act.copy(e_hi[:, 4 * h:4 * h + 4, t * P:(t + 1) * P],
                         ps[:, 4 + b, :].rearrange("p (k s) -> p k s", k=4)).then_inc(S["mx_hi"], 1)
            for g in range(G_OUT, G_FFN):
                hi_static(g + RING)
                if g >= G_FFN - 2:
                    h = g - (G_FFN - 2)
                    norm_hi(1, (2 * h, 2 * h + 1))
            norm_std(1)

            def f_hi_evac(c):
                nb = min(4, D_FF // P - 4 * c)
                for t in range(T):
                    act.wait_ge(S["f_tr"], T * c + t + 1)
                    act.copy(fa_hi[:, 4 * c:4 * c + nb, t * P:(t + 1) * P],
                             ps[:, 4 + t, 0:nb * P].rearrange("p (k s) -> p k s", k=nb)).then_inc(S["f_hi"], 1)

            for g in range(G_FFN, G_DOWN + D_FF // 256):
                hi_static(g + RING)
                q = g - G_FFN
                c = q // 4
                last = q >= 4 * FFC
                if (not last and q % 4 == 1) or q == 4 * FFC:
                    act.wait_ge(pe_half, g + 1)
                    if c >= 1:
                        act.wait_ge(S["f_ufree"], T * c)
                    wd = C if c < FFC else D_FF - FFC * C
                    act.wait_ge(n_rs[1], 1)
                    for t in range(T):
                        act.activation(f_s[:, t, 0:wd], ps[:, t, 0:wd], ACT.Silu,
                                       scale=rstd[:, 1, t:t + 1]).then_inc(S["f_silu"], 1)
                    if c >= 1:
                        f_hi_evac(c - 1)
                if q == 4 * FFC + 2:
                    f_hi_evac(FFC)
            norm_hi(2)
            norm_std(2)
            for g in range(G_OIN, G_OOUT):
                hi_static(g + RING)
                if g == G_OOUT - 3:
                    act.wait_ge(S["bias_m"], 1)
                    act.copy(bias_hi[:], bias[:]).then_inc(S["bias_h"], 1)
                if (g - G_OIN) % 2:
                    n = (g - G_OIN) // 2
                    act.wait_ge(pe_half, g + 1)
                    act.wait_ge(n_rs[2], 1)
                    for t in range(T):
                        act.activation(oproj[:, t, n * C:(n + 1) * C], ps[:, 2 * (n % 2) + t, :],
                                       ACT.Sigmoid if n == 1 else ACT.Copy,
                                       scale=(rstd_q if n == 2 else rstd)[:, 2, t:t + 1]).then_inc(S["oi_ev"], 1)
            for i in range(4):
                act.wait_ge(S["ot_tr"], i + 1)
                part, t = i // 2, i % 2
                act.copy(oqkT[:, 4 * part:4 * part + 4, t * P:(t + 1) * P],
                         ps[:, 4 + i, :].rearrange("p (k s) -> p k s", k=4)).then_inc(S["ot_ev"], 1)
            for t in range(T):
                act.wait_ge(S["o_mx"], t + 1)
                n_k = P * (t + 1)
                off = t * HEADS * P
                for s in range(HEADS):
                    src = ps[:, 0 if t == 0 else 2:, :].rearrange("p b c -> p (b c)")[:, s * n_k:(s + 1) * n_k]
                    act.activation(po[:, off + s * n_k:off + (s + 1) * n_k], src, ACT.Exp,
                                   bias=o_nm[:, t, s:s + 1], accum_out=o_sum[:, t, s:s + 1]).then_inc(S["o_ex"], 1)
            for i in range(6):
                act.wait_ge(S["o_tr"], i + 1)
                act.copy(poT[:, i * C:(i + 1) * C], ps[:, i, :]).then_inc(S["o_tev"], 1)
            act.wait_ge(S["ct_bn"], T)
            act.activation(bsd[:], bn2[:, :, 1], ACT.Sqrt, bias=eps[:]).then_inc(S["ct_sd"], 1)
            for t in range(T):
                act.wait_ge(S["od_tr"], t + 1)
                act.copy(o_hi[:, 4:8, t * P:(t + 1) * P],
                         ps[:, 4 + t, :].rearrange("p (k s) -> p k s", k=4)).then_inc(S["od_hi"], 1)
            for b in range(4):
                act.wait_ge(S["cb_tr"], b // 2 + 1)
                act.activation(cv[:, b, :], ps[:, 2 + b // 2, (b % 2) * SEQ:(b % 2 + 1) * SEQ], ACT.Silu,
                               bias=conv[:, b, TAPS + 2:TAPS + 3],
                               scale=conv[:, b, TAPS + 1:TAPS + 2]).then_inc(S["c_act"], 1)
            act.wait_ge(S["c_act"], 4)
            act.copy(o_hi[:, 0:4, :], cv[:]).then_inc(S["c_hi"], 1)
            for g in range(G_OOUT, G_MOE):
                hi_static(g + RING)
            norm_std(3)
            act.wait_ge(S["xg"], 2 * T)
            act.wait_ge(n_rs[3], 1)
            for t in range(T):
                act.activation(h_all[:, t, :], h_all[:, t, :], ACT.Copy, scale=rstd[:, 3, t:t + 1]).then_inc(S["h_full"], 1)
            act.wait_ge(S["g_exp"], 1)
            for t in range(T):
                act.activation(gate[:, t, 1:2], gate[:, t, 0:1], ACT.Exp, scale=rstd[:, 3, t:t + 1]).then_inc(S["g_exp"], 1)

            def gather_hi(i, n):
                for r in range(4):
                    act.wait_ge(S["ga_mm"], 4 * i + (r + 1 if n == 2 else 4))
                    if r >= 2:
                        act.wait_ge(S["ga_lo"], 4 * i + (r - 1))
                    c0 = 0 if n == 2 else r // 2 * SEQ
                    act.copy(g_hi[:, 2 * r:2 * r + 2, 0:n * P],
                             ps[:, 2 + r % 2, c0:c0 + 2 * n * P].rearrange("p (k s) -> p k s", k=2)).then_inc(S["ga_hi"], 1)

            def step(j, u, n, packed):
                hi(gm(j, u + RING), (G_MOE + u + RING) % RAW, 16 * (JOB // RAW) * j + 16 * ((G_MOE + u + RING) // RAW + 1))
                if u == 3:
                    act.wait_ge(S["pt_mm"], j + 1)
                    act.copy(put_r[:], ps[:, 6, :].rearrange("p (n t s) -> p n t s", n=2, t=T)).then_inc(S["pt_ev"], 1)
                c = u // 4 if u < 4 * EC else EC
                if u % 4 == 1 and c <= EC and u <= 4 * EC + 1:
                    if c or not isinstance(j, int):
                        act.wait_ge(S["e_tr"], EC * j + c)
                    if c < EC:
                        act.wait_ge(pe_half, gm(j, u + 1))
                        if packed:
                            act.copy(e_a[:, 1, :], ps[:, 1, :]).then_inc(S["e_raw"], 1)
                        else:
                            act.nop().then_inc(S["e_raw"], 1)
                        for t in range(n):
                            if packed and t:
                                act.wait_ge(S["e_fold"], EC * j + (c + 1))
                            last = act.activation(e_a[:, t, :], e_a[:, t, :] if packed and t else ps[:, t, :], ACT.Silu)
                        last.then_inc(S["e_silu"], 1)
                    if c:
                        b0 = 0 if c == EC else 4
                        for t in range(n):
                            last = act.copy(ea_hi[:, 4 * c - 4:4 * c, t * P:(t + 1) * P],
                                            ps[:, b0 + t, :].rearrange("p (k s) -> p k s", k=4))
                        last.then_inc(S["e_hi"], 1)

            def steps(j, us, n, packed):
                for u in us:
                    step(j, u, n, packed)

            def outputs_hi(j, n):
                for r in range(4):
                    t, c0, wd = TILE_OF(n, r), COL_OF(n, r), WIDE(n)
                    act.wait_ge(pe_half, gm(j, JOB))
                    if n == 2 and r >= 2:
                        act.wait_ge(S["sc_mm"], 8 * j + 2 * (r - 1))
                    if n == 1 and r >= 2:
                        act.wait_ge(S["y_lo_s"], 4 * j + (r - 1))
                    act.copy(y_hi[:, c0:c0 + wd], ps[:, (6, 4)[t] + c0 // C, c0 % C:c0 % C + wd]).then_inc(S["y_hi_s"], 1)

            act.wait_ge(S["route"], 1)
            many = many_of(act, 0)
            by_tiles(act, many, lambda n: gather_hi(0, n))
            by_form(act, many, lambda n, packed: steps(0, range(LEAD), n, packed))
            with act.Fori(0, N_EXP) as j:
                many, many2 = many_of(act, j), many_of(act, j + 1)
                by_form(act, many, lambda n, packed: steps(j, range(LEAD, MID), n, packed))
                by_tiles(act, many2, lambda n: gather_hi(j + 1, n))
                by_form(act, many, lambda n, packed: steps(j, range(MID, JOB), n, packed))
                by_tiles(act, many, lambda n: outputs_hi(j, n))
                by_form(act, many2, lambda n, packed: steps(j + 1, range(LEAD), n, packed))
            norm_std(4)

        @block.vector
        def _(dve):
            chain = [0]

            def link(ins):
                chain[0] += 1
                ins.then_inc(S["dve_chain"], 1)
                dve.wait_ge(S["dve_chain"], chain[0])

            def lo(g, s):
                dve.wait_ge(hi_done, g + 1)
                r = s % RING
                dve.tensor_tensor(wlo[:, r, :], raw[:, s, :], whi[:, r, :].bitcast(F32),
                                  ALU.subtract).then_inc(lo_done, 1)

            def lo_static(g):
                lo(g, g % RAW)

            def norm_rs(n):
                dve.wait_ge(n_std[n], 1)
                ins = dve.reciprocal(rstd[:, n, :], std[:, n, :])
                if n in (0, 2):
                    link(ins)
                    ins = dve.tensor_scalar(rstd_q[:, n, :], rstd[:, n, :], HD ** -0.5, None, ALU.mult)
                if n < NORMS:
                    ins.then_inc(n_rs[n], 1)
                    dve.wait_ge(n_rs[n], 1)
                else:
                    link(ins)

            def norm_gain(n, bs=range(2 * T)):
                for b in bs:
                    dve.wait_ge(n_tr[n], b + 1)
                    h, _ = BLOCKS[b]
                    dve.tensor_tensor(FULL[n][:, b, :].rearrange("p (k s) -> p k s", k=4),
                                      ps[:, TURN_BANK[n][b], :].rearrange("p (k s) -> p k s", k=4),
                                      gains[:, n, 4 * h:4 * h + 4].unsqueeze(2).broadcast_to([P, 4, P]),
                                      ALU.mult).then_inc(n_full[n], 1)

            def norm_lo(n, bs=range(2 * T)):
                for b in bs:
                    dve.wait_ge(n_hi[n], b + 1)
                    h, t = BLOCKS[b]
                    tt = slice(t * P, (t + 1) * P)
                    dve.tensor_tensor(LO[n][:, 4 * h:4 * h + 4, tt], FULL[n][:, b, :].rearrange("p (k s) -> p k s", k=4),
                                      HI[n][:, 4 * h:4 * h + 4, tt].bitcast(F32), ALU.subtract).then_inc(n_lo[n], 1)

            dve.memset(eps[:], EPS).then_inc(S["eps_set"], 1)
            dve.wait_ge(S["gains_tr"], 1)
            dve.tensor_copy(gains[:].rearrange("p n k -> p (n k)"), ps[:, 0, 0:4 * KD]).then_inc(S["gains_ev"], 1)
            dve.wait_ge(S["gains_ev"], 1)
            norm_gain(0)
            norm_lo(0)
            for g in range(RING):
                lo_static(g)
            norm_rs(0)
            dve.wait_ge(S["cst2_in"], 16)
            dve.wait_ge(S["lam_ld"], 64)
            for i in range(2):
                if i:
                    dve.wait_ge(S["lam_sum"], i)
                dve.tensor_tensor_reduce(out=lam_j[:], in0=lam_in[:, 2 * i, :], in1=lam_in[:, 2 * i + 1, :],
                                         scale=1.0, scalar=0.0, op0=ALU.mult, op1=ALU.add,
                                         accum_out=lam_s[:, i:i + 1]).then_inc(S["lam_sum"], 1)

            def rope(part, t):
                v = proj[:, t, part * C:(part + 1) * C].rearrange("p (h a d) -> p h a d", a=2, d=HD // 2)
                a = rope_a[:].rearrange("p (h a d) -> p h a d", a=2, d=HD // 2)
                b = rope_b[:].rearrange("p (h a d) -> p h a d", a=2, d=HD // 2)
                cos = cst[:, K_COS + 32 * t:K_COS + 32 * (t + 1)].unsqueeze(1).broadcast_to([P, HEADS, 32])
                sin = cst[:, K_SIN + 32 * t:K_SIN + 32 * (t + 1)].unsqueeze(1).broadcast_to([P, HEADS, 32])
                dve.wait_ge(S["ip_ev"], T * part + t + 1)
                for i in range(2):
                    dve.tensor_tensor(a[:, :, i, :], v[:, :, i, :], cos, ALU.mult)
                    last = dve.tensor_tensor(b[:, :, i, :], v[:, :, 1 - i, :], sin, ALU.mult)
                link(last)
                dve.tensor_tensor(v[:, :, 0, :], a[:, :, 0, :], b[:, :, 0, :], ALU.subtract)
                last = dve.tensor_tensor(v[:, :, 1, :], a[:, :, 1, :], b[:, :, 1, :], ALU.add)
                link(last)

            for g in range(G_IN, G_OUT):
                lo_static(g + RING)
                if 4 <= g < 8:
                    rope(g % 2, (g - 4) // 2)
            dve.nop().then_inc(S["roped"], 1)
            for i in range(1, 8, 2):
                dve.wait_ge(S["at_tr"], i + 1)
                part, t = i // 2, i % 2
                dve.tensor_copy(qkT[:, 4 * part:4 * part + 4, t * P:(t + 1) * P],
                                ps[:, 4 + i % 4, :].rearrange("p (k s) -> p k s", k=4)).then_inc(S["at_ev_d"], 1)
            def a_max(t):
                dve.wait_ge(S["a_sc"], t + 1)
                src = ps[:, 0:2, :] if t == 0 else ps[:, 2:6, :]
                dve.tensor_reduce(a_nm[:, t, :], src.rearrange("p b (h k) -> p (b h) k", k=P * (t + 1)), AX, ALU.max,
                                  negate=True).then_inc(S["a_mx"], 1)

            def a_diff(t):
                n_k = P * (t + 1)
                off, offd = t * HEADS * P, t * A_HEADS * P
                dve.wait_ge(S["a_ex"], HEADS * (t + 1))
                link(dve.reciprocal(a_r[:, t, :], a_sum[:, t, :]))
                odd_r = a_r[:, t, A_HEADS:HEADS]
                link(dve.tensor_scalar(odd_r, odd_r, lam_s[:, 1:2], None, ALU.mult))
                p_of = lambda s: pa[:, off + s * n_k:off + (s + 1) * n_k]
                for h in range(A_HEADS):
                    last = dve.tensor_scalar(p_of(A_HEADS + h), p_of(A_HEADS + h), a_r[:, t, A_HEADS + h:A_HEADS + h + 1],
                                             None, ALU.mult)
                link(last)
                for h in range(A_HEADS):
                    dve.scalar_tensor_tensor(out=pd[:, offd + h * n_k:offd + (h + 1) * n_k], in0=p_of(h),
                                             scalar=a_r[:, t, h:h + 1], in1=p_of(A_HEADS + h),
                                             op0=ALU.mult, op1=ALU.subtract).then_inc(S["a_pd"], 1)

            a_max(0)
            dve.wait_ge(S["lam_exp"], 1)
            link(dve.tensor_tensor(lam_s[:, 0:1], lam_s[:, 2:3], lam_s[:, 3:4], ALU.subtract))
            link(dve.tensor_scalar(lam_s[:, 1:2], lam_s[:, 0:1], LAMBDA_INIT, None, ALU.add))
            a_max(1)
            a_diff(0)
            a_diff(1)
            for i in range(3):
                dve.wait_ge(S["b_ln"], i + 1)
                dve.scalar_tensor_tensor(out=sp[:, i, :], in0=z_of(i), scalar=0.0, in1=sp[:, i, :],
                                         op0=ALU.max, op1=ALU.add).then_inc(S["b_sp"], 1)
            for i in range(3):
                dve.wait_ge(S["b_sph"], i + 1)
                dve.tensor_tensor(sp_lo[:, i, :], sp[:, i, :], sp_hi[:, i, :].bitcast(F32),
                                  ALU.subtract).then_inc(S["b_spl"], 1)
            dve.wait_ge(S["sub_in"], 16)
            link(dve.tensor_scalar(subln[:], subln[:], 1.0 - LAMBDA_INIT, None, ALU.mult))
            dve.wait_ge(S["a_oev"], T)
            sq = pd[:, 0:T * C].rearrange("p (t h d) -> p t h d", t=T, h=A_HEADS)
            mv = mixed[:, :, 0:C].rearrange("p t (h d) -> p t h d", h=A_HEADS)
            for t in range(T):
                last = dve.tensor_tensor(sq[:, t], mv[:, t], mv[:, t], ALU.mult)
            link(last)
            for t in range(T):
                last = dve.tensor_reduce(a_ms[:, t, :], sq[:, t], AX, ALU.add)
            last.then_inc(S["a_msq"], 1)
            dve.wait_ge(S["a_sqrt"], 1)
            link(dve.reciprocal(a_rs[:], a_sd[:]))
            for t in range(T):
                for h in range(A_HEADS):
                    last = dve.scalar_tensor_tensor(out=mv[:, t, h, :], in0=mv[:, t, h, :], scalar=a_rs[:, t, h:h + 1],
                                                    in1=subln[:], op0=ALU.mult, op1=ALU.mult)
            last.then_inc(S["a_done"], 1)
            for b in range(2 * T):
                dve.wait_ge(S["mx_hi"], b + 1)
                t, h = b // 2, b % 2
                tt = slice(t * P, (t + 1) * P)
                dve.tensor_tensor(e_lo[:, 4 * h:4 * h + 4, tt], ps[:, 4 + b, :].rearrange("p (k s) -> p k s", k=4),
                                  e_hi[:, 4 * h:4 * h + 4, tt].bitcast(F32), ALU.subtract).then_inc(S["mx_lo"], 1)

            def residual(n, banks, done):
                for t in range(T):
                    dve.tensor_tensor(x[:, t, n * C:(n + 1) * C], x[:, t, n * C:(n + 1) * C],
                                      ps[:, banks[t], :], ALU.add).then_inc(done, 1)

            def out_halves(g0, n_norm, done, more):
                lo_static(g0 + RING)
                lo_static(g0 + 1 + RING)
                dve.wait_ge(pe_half, g0 + 2)
                residual(0, (0, 1), done)
                lo_static(g0 + 2 + RING)
                norm_gain(n_norm, (0, 1))
                more(0)
                dve.wait_ge(pe_half, g0 + 4)
                residual(1, (2, 3), done)
                norm_gain(n_norm, (2, 3))
                more(1)
                lo_static(g0 + 3 + RING)
                norm_rs(n_norm)

            out_halves(G_OUT, 1, S["op_add"], lambda h: norm_lo(1, (2 * h, 2 * h + 1)))

            def f_lo_evac(c):
                nb = min(4, D_FF // P - 4 * c)
                for t in range(T):
                    dve.wait_ge(S["f_hi"], T * c + t + 1)
                    dst = (slice(4 * c, 4 * c + nb), slice(t * P, (t + 1) * P))
                    dve.tensor_tensor(fa_lo[:, dst[0], dst[1]],
                                      ps[:, 4 + t, 0:nb * P].rearrange("p (k s) -> p k s", k=nb),
                                      fa_hi[:, dst[0], dst[1]].bitcast(F32), ALU.subtract).then_inc(S["f_lo"], 1)

            for g in range(G_FFN, G_OIN - 1):
                lo_static(g + RING)
                q = g - G_FFN
                if (q < 4 * FFC and q % 4 == 1) or q == 4 * FFC:
                    c = q // 4
                    if c >= 1:
                        f_lo_evac(c - 1)
                if (q < 4 * FFC and q % 4 == 3) or q == 4 * FFC + 1:
                    c = q // 4
                    wd = C if c < FFC else D_FF - FFC * C
                    dve.wait_ge(pe_half, g + 1)
                    dve.wait_ge(S["f_silu"], T * (c + 1))
                    for t in range(T):
                        if c >= 1:
                            dve.wait_ge(S["f_tr"], T * (c - 1) + t + 1)
                        dve.scalar_tensor_tensor(out=f_a[:, t, 0:wd], in0=ps[:, 2 + t, 0:wd], scalar=rstd[:, 1, t:t + 1],
                                                 in1=f_s[:, t, 0:wd], op0=ALU.mult, op1=ALU.mult).then_inc(S["f_ufree"], 1)
                if q == 4 * FFC + 2:
                    f_lo_evac(FFC)
            dve.wait_ge(pe_half, G_OIN)
            for n in range(2):
                residual(n, ((0, 6), (1, 7))[n], S["f_add"])
            norm_gain(2)
            norm_lo(2)
            lo_static(G_OIN - 1 + RING)
            norm_rs(2)
            dve.wait_ge(S["rel_ld"], 16)
            dve.tensor_copy(rel_rev[:, 0:P - 1], rel_in[:, REL - 1:REL].broadcast_to([HEADS, P - 1])).then_inc(S["rel_rv"], 1)
            dve.tensor_copy(rel_rev[:, P - 1:P - 1 + REL], rel_in[:, ::-1]).then_inc(S["rel_rv"], 1)

            def o_max(t):
                dve.wait_ge(S["o_sc"], t + 1)
                src = ps[:, 0:2, :] if t == 0 else ps[:, 2:6, :]
                dve.tensor_reduce(o_nm[:, t, :], src.rearrange("p b (h k) -> p (b h) k", k=P * (t + 1)), AX, ALU.max,
                                  negate=True).then_inc(S["o_mx"], 1)

            def taps(k0, k1):
                with dve.Fori(k0, k1) as k:
                    for b in range(4):
                        dve.wait_ge(S["conv_step"], k * 4 + (b - 3))
                        dve.scalar_tensor_tensor(out=cv[:, b, :], in0=uT[:, b, bass.ds(k, SEQ)],
                                                 scalar=conv[:, b, bass.ds(k, 1)], in1=cv[:, b, :],
                                                 op0=ALU.mult, op1=ALU.add).then_inc(S["conv_step"], 1)

            for g in range(G_OIN, G_OOUT - RING):
                lo_static(g + RING)
                q = g - G_OIN
                if q == 5:
                    dve.wait_ge(S["bias_in"], 16)
                    late = bias[P - CHUNK:P, :, SEQ - CHUNK:SEQ]
                    dve.tensor_scalar(late, late, NEG, None, ALU.add).then_inc(S["bias_m"], 1)
                if q == 3:
                    dve.memset(uT[:, :, 0:TAPS - 1], 0.0).then_inc(S["uz"], 1)
                    for t in range(T):
                        dve.wait_ge(S["oi_ev"], T + t + 1)
                        dve.tensor_tensor(oproj[:, t, 0:C], oproj[:, t, 0:C], oproj[:, t, C:2 * C],
                                          ALU.mult).then_inc(S["u_mul"], 1)
                if q == 6:
                    dve.wait_ge(S["cw_tr"], 1)
                    link(dve.tensor_copy(conv[:], ps[:, 6, 0:4 * (TAPS + 3)].rearrange("p (b n) -> p b n", b=4)))
                    for t in range(T):
                        dve.wait_ge(S["u_tr"], t + 1)
                        last = dve.tensor_copy(uT[:, :, TAPS - 1 + t * P:TAPS - 1 + (t + 1) * P],
                                               ps[:, 4 + t, :].rearrange("p (b s) -> p b s", b=4))
                        last.then_inc(S["u_ev"], 1)
            dve.wait_ge(S["u_ev"], T)
            dve.wait_ge(S["uz"], 1)
            for b in range(4):
                dve.tensor_scalar(cv[:, b, :], uT[:, b, 0:SEQ], conv[:, b, 0:1], conv[:, b, TAPS:TAPS + 1],
                                  ALU.mult, ALU.add).then_inc(S["conv_step"], 1)
            taps(1, TAP_CUT[2])
            dve.wait_ge(S["bias_h"], 1)
            dve.tensor_tensor(bias_lo[:], bias[:], bias_hi[:].bitcast(F32), ALU.subtract).then_inc(S["bias_l"], 1)
            taps(TAP_CUT[2], TAP_CUT[0])
            o_max(0)
            taps(TAP_CUT[0], TAP_CUT[1])
            o_max(1)
            taps(TAP_CUT[1], TAPS)
            for t in range(T):
                dve.wait_ge(S["ct_tr"], t + 1)
                link(dve.bn_stats(bn6[:, t, :], ps[:, 6 + t, :]))
                dve.bn_aggr(bn2[:, t, :], bn6[:, t, :]).then_inc(S["ct_bn"], 1)
            dve.wait_ge(S["o_ex"], HEADS * T)
            link(dve.reciprocal(o_r[:], o_sum[:]))
            for t in range(T):
                dve.wait_ge(S["o_pv"], t + 1)
                for a in range(2):
                    last = dve.tensor_tensor(od[:, t, :].rearrange("p (h a d) -> p a h d", a=2, d=HD)[:, a],
                                             ps[:, t, :].rearrange("p (a h d) -> p a h d", a=2, d=HD)[:, a],
                                             o_r[:, t, 4 * a:4 * a + 4].unsqueeze(2).broadcast_to([P, 4, HD]),
                                             ALU.mult)
                last.then_inc(S["o_norm"], 1)
            dve.wait_ge(S["ct_sd"], 1)
            link(dve.reciprocal(brs[:], bsd[:]))
            for t in range(T):
                dve.tensor_scalar(cn[:, t, :], ps[:, 6 + t, :], bn2[:, t, 0:1], brs[:, t:t + 1],
                                  ALU.subtract, ALU.mult).then_inc(S["cn_done"], 1)
            for t in range(T):
                dve.wait_ge(S["od_hi"], t + 1)
                tt = slice(t * P, (t + 1) * P)
                dve.tensor_tensor(o_lo[:, 4:8, tt], ps[:, 4 + t, :].rearrange("p (k s) -> p k s", k=4),
                                  o_hi[:, 4:8, tt].bitcast(F32), ALU.subtract).then_inc(S["od_lo"], 1)
            lo_static(G_OOUT)
            dve.wait_ge(S["c_hi"], 1)
            dve.tensor_tensor(o_lo[:, 0:4, :], cv[:], o_hi[:, 0:4, :].bitcast(F32), ALU.subtract).then_inc(S["c_lo"], 1)
            lo_static(G_OOUT + 1)
            lo_static(G_OOUT + 2)
            def gain_tokens(h):
                for t in range(T):
                    dve.wait_ge(S["oo_add"], 2 * h + t + 1)
                    dve.tensor_tensor(h_all[:, t, h * C:(h + 1) * C], x[:, t, h * C:(h + 1) * C],
                                      gain_row[:, h * C:(h + 1) * C], ALU.mult).then_inc(S["xg"], 1)

            dve.wait_ge(S["grow_in"], 16)
            out_halves(G_OOUT, 3, S["oo_add"], gain_tokens)
            dve.memset(slot[:], -1.0)
            dve.memset(over_f[:], 0.0)
            dve.wait_ge(S["r_mm"], 1)
            link(dve.tensor_copy(logit[:], ps[:, 0:T, 0:N_EXP]))
            for t in range(T):
                last = dve.max(top[:, t, :], logit[:, t, :])
            link(last)
            for t in range(T):
                last = dve.max_index(topi[:, t, :], top[:, t, :], logit[:, t, :])
            link(last)
            link(dve.tensor_copy(topf[:], topi[:]))
            dve.tensor_tensor(gate[:, :, 0], top[:, :, 1], top[:, :, 0], ALU.subtract).then_inc(S["g_exp"], 1)
            iota8 = kept[:, K_IOTA8:K_IOTA8 + 8]
            for t in range(T):
                for c in range(2):
                    last = dve.tensor_scalar(hot[:, t, c, :], iota8, topf[:, t, c:c + 1], None, ALU.is_equal)
            link(last)
            dve.tensor_tensor(sel[:], hot[:, :, 0, :], hot[:, :, 1, :], ALU.add).then_inc(S["sel_s"], 1)
            dve.wait_ge(S["cnt_mm"], 1)
            for t in range(T):
                last = dve.scalar_tensor_tensor(out=slot[:, t, 0:N_EXP], in0=ps[:, 2 + t, 0:N_EXP], scalar=1.0,
                                                in1=sel[:, t, :], op0=ALU.add, op1=ALU.mult)
            link(last)
            link(dve.tensor_scalar(slot[:, :, 0:N_EXP], slot[:, :, 0:N_EXP], -1.0, None, ALU.add))
            dve.tensor_scalar(over_f[:, N_EXP:2 * N_EXP], ps[:, 4, 0:N_EXP], float(P + H), None, ALU.is_gt)
            link(dve.tensor_scalar(over_f[:, 0:N_EXP], ps[:, 4, 0:N_EXP], float(P), None, ALU.is_gt))
            link(dve.tensor_tensor(over_f[:, 0:N_EXP], over_f[:, 0:N_EXP], over_f[:, N_EXP:2 * N_EXP], ALU.subtract))
            dve.tensor_copy(slot_b[:, :, N_EXP:N_EXP + 1], slot[:, :, N_EXP:N_EXP + 1])
            for t in range(T):
                last = dve.scalar_tensor_tensor(out=slot_b[:, t, 0:N_EXP], in0=over_f[:, 0:N_EXP], scalar=float(H),
                                                in1=slot[:, t, 0:N_EXP], op0=ALU.mult, op1=ALU.add)
            link(last)
            link(dve.scalar_tensor_tensor(out=over_f[:, 0:N_EXP], in0=over_f[:, N_EXP:2 * N_EXP], scalar=2.0,
                                          in1=over_f[:, 0:N_EXP], op0=ALU.mult, op1=ALU.add))
            link(dve.memset(over_f[:, N_EXP:2 * N_EXP], 0.0))
            link(dve.tensor_copy(over_i[:], over_f[:]))

            def make_pick(i):
                for t in range(T):
                    dve.tensor_scalar(pick[:, t, 0:P + H], kept[:, K_IOTA:K_IOTA + P + H], slot[:, t, bass.ds(i, 1)],
                                      None, ALU.is_equal)
                    last = dve.tensor_scalar(pick[:, t, P + H:SEQ], kept[:, K_IOTA + P + H:K_IOTA + SEQ],
                                             slot_b[:, t, bass.ds(i, 1)], None, ALU.is_equal)
                last.then_inc(S["pk"], 1)

            def gather_lo(i, n, packed):
                for r in range(4):
                    dve.wait_ge(S["ga_hi"], 4 * i + (r + 1))
                    c0 = 0 if n == 2 else r // 2 * SEQ
                    rs = slice(2 * r, 2 * r + 2)
                    got = ps[:, 2 + r % 2, c0:c0 + 2 * n * P].rearrange("p (k s) -> p k s", k=2)
                    if packed:
                        copy2 = g_hi[:, rs, P + H:SEQ]
                        dve.tensor_tensor(copy2, got[:, :, P + H:SEQ], copy2.bitcast(F32), ALU.subtract)
                    n_lo_ = P if packed else n * P
                    dve.tensor_tensor(g_lo[:, rs, 0:n_lo_], got[:, :, 0:n_lo_], g_hi[:, rs, 0:n_lo_].bitcast(F32),
                                      ALU.subtract).then_inc(S["ga_lo"], 1)

            def step(j, u, n, packed):
                lo(gm(j, u + RING), (G_MOE + u + RING) % RAW)
                c = u // 4 if u < 4 * EC else EC
                if u % 4 == 1 and c < EC:
                    if packed:
                        dve.wait_ge(S["e_raw"], EC * j + (c + 1))
                        for h in range(2):
                            own, other = slice(h * H, (h + 1) * H), slice((1 - h) * H, (2 - h) * H)
                            last = dve.tensor_tensor(e_a[own, 1, :], e_a[own, 1, :], ps[other, 1, :], ALU.add)
                        last.then_inc(S["e_fold"], 1)
                    else:
                        dve.nop().then_inc(S["e_fold"], 1)
                if u % 4 == 1 and c and u <= 4 * EC + 1:
                    dve.wait_ge(S["e_hi"], EC * j + c)
                    b0 = 0 if c == EC else 4
                    blk = slice(4 * c - 4, 4 * c)
                    if packed:
                        src = ps[:, b0 + 1, :].rearrange("p (k s) -> p k s", k=4)[:, :, H:P]
                        copy2 = ea_hi[:, blk, P + H:SEQ]
                        dve.tensor_tensor(copy2, src, copy2.bitcast(F32), ALU.subtract)
                    for t in range(1 if packed else n):
                        tt = slice(t * P, (t + 1) * P)
                        last = dve.tensor_tensor(ea_lo[:, blk, tt], ps[:, b0 + t, :].rearrange("p (k s) -> p k s", k=4),
                                                 ea_hi[:, blk, tt].bitcast(F32), ALU.subtract)
                    last.then_inc(S["e_lo"], 1)
                if u < 4 * EC and u % 4 == 3:
                    dve.wait_ge(pe_half, gm(j, u + 1))
                    dve.wait_ge(S["e_silu"], EC * j + (c + 1))
                    for t in range(n):
                        last = dve.tensor_tensor(e_a[:, t, :], ps[:, 2 + t, :], e_a[:, t, :], ALU.mult)
                    last.then_inc(S["e_ufree"], 1)
                if u == 8:
                    dve.wait_ge(S["pt_mm"], j + 1)
                    make_pick(j + 1)

            def steps(j, us, n, packed):
                for u in us:
                    step(j, u, n, packed)

            def outputs_lo(j, n):
                for r in range(4):
                    t, c0, wd = TILE_OF(n, r), COL_OF(n, r), WIDE(n)
                    dve.wait_ge(S["y_hi_s"], 4 * j + (r + 1))
                    dve.tensor_tensor(y_lo[:, c0:c0 + wd], ps[:, (6, 4)[t] + c0 // C, c0 % C:c0 % C + wd],
                                      y_hi[:, c0:c0 + wd].bitcast(F32), ALU.subtract).then_inc(S["y_lo_s"], 1)
                    if n == 2 and r >= 1:
                        add_piece(j, n, r - 1)

            def add_piece(j, n, r):
                c0, wd = COL_OF(n, r), WIDE(n)
                for t in range(T):
                    dve.wait_ge(S["sc_mm"], 8 * j + (2 * r + t + 1 if n == 2 else 4 * (r // 2) + 4))
                    bank, b0 = place(n, r)
                    dve.scalar_tensor_tensor(out=x[:, t, c0:c0 + wd], in0=ps[:, bank + t, b0:b0 + wd],
                                             scalar=comb[:, t, bass.ds(j, 1)], in1=x[:, t, c0:c0 + wd],
                                             op0=ALU.mult, op1=ALU.add).then_inc(S["sc_add"], 1)

            dve.drain().then_inc(S["sc_add"], 1)
            make_pick(0)
            dve.drain().then_inc(S["route"], 1)
            dve.wait_ge(S["route"], 1)
            dve.wait_ge(S["g_exp"], 1 + T)
            link(dve.tensor_scalar(gate[:, :, 2], gate[:, :, 1], 1.0, None, ALU.add))
            link(dve.reciprocal(gate[:, :, 3], gate[:, :, 2]))
            link(dve.tensor_tensor(gate[:, :, 2], gate[:, :, 1], gate[:, :, 3], ALU.mult))
            for t in range(T):
                last = dve.tensor_scalar(comb[:, t, 0:N_EXP], hot[:, t, 0, :], gate[:, t, 3:4], None, ALU.mult)
            link(last)
            for t in range(T):
                last = dve.scalar_tensor_tensor(out=comb[:, t, 0:N_EXP], in0=hot[:, t, 1, :], scalar=gate[:, t, 2:3],
                                                in1=comb[:, t, 0:N_EXP], op0=ALU.mult, op1=ALU.add)
            link(last)
            many = many_of(dve, 0)
            by_form(dve, many, lambda n, packed: gather_lo(0, n, packed))
            by_form(dve, many, lambda n, packed: steps(0, range(LEAD), n, packed))
            with dve.Fori(0, N_EXP) as j:
                many, many2 = many_of(dve, j), many_of(dve, j + 1)
                by_form(dve, many, lambda n, packed: steps(j, range(LEAD, MID), n, packed))
                by_form(dve, many2, lambda n, packed: gather_lo(j + 1, n, packed))
                by_form(dve, many, lambda n, packed: steps(j, range(MID, JOB), n, packed))
                by_tiles(dve, many, lambda n: outputs_lo(j, n))
                by_form(dve, many2, lambda n, packed: steps(j + 1, range(LEAD), n, packed))

                def add_rest(n):
                    for r in range(3 if n == 2 else 0, 4):
                        add_piece(j, n, r)

                by_tiles(dve, many, add_rest)
            dve.drain().then_inc(S["fin_n"], 1)
            dve.wait_ge(S["fin_n"], 1)
            for t in range(T):
                dve.tensor_tensor_reduce(out=fin_x[:, t, :], in0=x[:, t, :], in1=x[:, t, :], scale=1.0, scalar=0.0,
                                         op0=ALU.mult, op1=ALU.add, accum_out=ss[:, 4, t:t + 1]).then_inc(n_ss[4], 1)
            norm_rs(4)
            dve.wait_ge(S["fin_in"], 16)
            for t in range(T):
                dve.scalar_tensor_tensor(out=fin_x[:, t, :], in0=x[:, t, :], scalar=rstd[:, 4, t:t + 1], in1=h_all[:, 0, :],
                                         op0=ALU.mult, op1=ALU.mult).then_inc(S["final_ok"], 1)

        @block.tensor
        def _(pe):
            def mm3(dst, a_hi, a_lo, b_hi, b_lo, start, stop):
                pe.matmul(dst, a_hi, b_hi, start=start, stop=False)
                pe.matmul(dst, a_hi, b_lo, start=False, stop=False)
                return pe.matmul(dst, a_lo, b_hi, start=False, stop=stop)

            def product(dst, a_hi, a_lo, b_hi, b_lo, start, stop, packed):
                if not packed:
                    return mm3(dst, a_hi, a_lo, b_hi, b_lo, start, stop)
                pe.matmul(dst, a_hi, b_hi, start=start, stop=False)
                return pe.matmul(dst, a_hi, b_lo, start=False, stop=stop)

            def half_cols(g, r, a_hi, a_lo, k0, kn, banks, wd, start, stop, rows, packed=False):
                pe.wait_ge(lo_done, g + 1)
                bh, bl = cols_view(whi[:, r, :], kn), cols_view(wlo[:, r, :], kn)
                for t, rs in enumerate(rows):
                    for k in range(kn):
                        last = product(ps[:, banks[t], 0:wd], a_hi[:, k0 + k, rs], a_lo[:, k0 + k, rs], bh[:, k, :],
                                       bl[:, k, :], start and k == 0, stop and k == kn - 1, packed and t == 1)
                last.then_inc(pe_half, 1)

            def half_rows(g, r, a_hi, a_lo, b0, banks, first, final, rows, packed=False):
                pe.wait_ge(lo_done, g + 1)
                bh, bl = cols_view(whi[:, r, :], 2), cols_view(wlo[:, r, :], 2)
                for t, rs in enumerate(rows):
                    for k in range(2):
                        for h in range(2):
                            hs = slice(h * C, (h + 1) * C)
                            last = product(ps[:, banks[t][h], :], a_hi[:, b0 + k, rs], a_lo[:, b0 + k, rs],
                                           bh[:, k, hs], bl[:, k, hs], first and k == 0, final and k == 1,
                                           packed and t == 1)
                last.then_inc(pe_half, 1)

            BOTH = [slice(0, P), slice(P, SEQ)]

            def turn4(dst_bank, src_of, done, n=4):
                for i in range(n):
                    last = pe.transpose(ps[:, dst_bank, i * P:(i + 1) * P], src_of(i), ident)
                last.then_inc(done, 1)

            def norm_turn(n, bs=range(2 * T)):
                for b in bs:
                    h, t = BLOCKS[b]
                    if n:
                        pe.wait_ge(X_SUM[n], b + 1)
                    turn4(TURN_BANK[n][b], lambda i: x[:, t, (4 * h + i) * P:(4 * h + i + 1) * P], n_tr[n])

            pe.wait_ge(S["cst_in"], 16)
            pe.wait_ge(S["row_in"], 64)
            pe.transpose(ps[:, 0, 0:4 * KD], gains_row[:], ident[0:4 * KD, 0:4 * KD]).then_inc(S["gains_tr"], 1)
            pe.wait_ge(S["x_in"], 16)
            norm_turn(0)
            pe.wait_ge(n_lo[0], 2 * T)
            pe.wait_ge(S["gains_ev"], 1)
            for g in range(G_IN, G_OUT):
                n = g // 2
                if g % 2 == 0 and n >= 2:
                    pe.wait_ge(S["ip_ev"], T * (n - 1))
                half_cols(g, g % RING, e_hi, e_lo, g % 2 * 4, 4, (2 * (n % 2), 2 * (n % 2) + 1), C,
                          g % 2 == 0, g % 2 == 1, BOTH)
            pe.wait_ge(S["cr_a"], 1)
            pe.wait_ge(S["cr_b"], 1)
            pe.wait_ge(S["roped"], 1)
            pe.wait_ge(S["ip_ev"], 6 * T)
            for i in range(8):
                part, t = i // 2, i % 2
                if i >= 4:
                    pe.wait_ge(S["at_ev_a"] if i % 2 == 0 else S["at_ev_d"], (i - 4) // 2 + 1)
                c0 = (0, C, 3 * C, 4 * C)[part]
                turn4(4 + i % 4, lambda b: proj[:, t, c0 + b * P:c0 + (b + 1) * P], S["at_tr"])
            pe.wait_ge(S["at_ev_a"], 4)
            pe.wait_ge(S["at_ev_d"], 4)

            def scores(t, kT, extra, done):
                n_k = P * (t + 1)
                per = C // n_k
                for b in range(HEADS // per):
                    bank = (0 if t == 0 else 2) + b
                    by_head = ps[:, bank, :].rearrange("p (h k) -> p h k", h=per)
                    if extra is None:
                        col = cst_r[0:1, K_COL + SEQ - n_k:K_COL + SEQ].unsqueeze(1).broadcast_to([1, per, n_k])
                        pe.matmul(by_head, cst_r[0:1, K_ROW:K_ROW + P], col, start=True, stop=True)
                    else:
                        for i, part in enumerate(extra):
                            pe.matmul(by_head, cst_r[:, K_FLIP:K_FLIP + P],
                                      part[:, PLACED[b * per]:PLACED[b * per + per - 1] + 1:2, SEQ - n_k:SEQ],
                                      start=i == 0, stop=True, skip_group_check=True)
                    for i in range(per):
                        s = PLACED[b * per + i]
                        half = slice((s % 2) * HD, (s % 2 + 1) * HD)
                        last = pe.matmul(ps[:, bank, i * n_k:(i + 1) * n_k], kT[half, s // 2, t * P:(t + 1) * P],
                                         kT[half, 4 + s // 2, 0:n_k], start=False, stop=True, skip_group_check=True)
                last.then_inc(done, 1)

            for t in range(T):
                scores(t, qkT, None, S["a_sc"])
            GROUPS = ((0, 0), (1, 1), (0, 1))

            def z_group(i):
                kb, qb = GROUPS[i]
                for b in range(2):
                    bank = Z_BANK[i] + b
                    if kb == qb:
                        pe.matmul(ps[:, bank, :].rearrange("p (h k) -> p h k", h=4), ident_r[:],
                                  cst_r[:, K_DMASK:K_DMASK + P].unsqueeze(1).broadcast_to([P, 4, P]),
                                  start=True, stop=True)
                    for j4 in range(4):
                        h = PLACED[4 * b + j4]
                        half = slice((h % 2) * HD, (h % 2 + 1) * HD)
                        last = pe.matmul(ps[:, bank, j4 * P:(j4 + 1) * P], qkT[half, 12 + h // 2, kb * P:(kb + 1) * P],
                                         qkT[half, 8 + h // 2, qb * P:(qb + 1) * P],
                                         start=kb != qb and j4 == 0, stop=True, skip_group_check=True)
                last.then_inc(S["b_z"], 1)

            def a_turn(i):
                t, kb = ((0, 0), (1, 0), (1, 1))[i]
                n_k = P * (t + 1)
                pe.wait_ge(S["a_pd"], A_HEADS * (t + 1))
                turn4(A_TURN[i], lambda h: pd[:, t * C + h * n_k + kb * P:t * C + h * n_k + (kb + 1) * P], S["a_tr"])

            z_group(0)
            pe.wait_ge(S["a_ex"], HEADS)
            z_group(1)
            pe.wait_ge(S["a_ex"], HEADS * T)
            z_group(2)
            a_turn(0)
            a_turn(1)
            pe.wait_ge(S["a_tev"], 1)
            a_turn(2)
            for t in range(T):
                pe.wait_ge(S["a_tev"], t + 2)
                for h in range(A_HEADS):
                    for kb in range(t + 1):
                        last = pe.matmul(ps[:, A_OUT[t], h * P:(h + 1) * P],
                                         pdT[:, (t + kb) * C + h * P:(t + kb) * C + (h + 1) * P],
                                         proj[:, kb, 2 * C + h * P:2 * C + (h + 1) * P], start=kb == 0, stop=kb == t)
                last.then_inc(S["a_pv"], 1)
            for i in range(3):
                pe.wait_ge(S["b_spl"], i + 1)
                for b in range(2):
                    dst, bc = ps[:, Z_BANK[i] + b, :], slice(b * C, (b + 1) * C)
                    for part in (sp_hi, sp_lo):
                        if i == 2:
                            pe.matmul(dst, cst_r[:, K_NONES:K_NONES + P], part[:, 1, bc],
                                      start=False, stop=True, skip_group_check=True)
                        last = pe.matmul(dst, cst_r[:, K_NTRI:K_NTRI + P], part[:, i, bc],
                                         start=False, stop=True, skip_group_check=True)
                last.then_inc(S["b_cum"], 1)
            for t in range(T):
                pe.wait_ge(S["b_w"], 1 if t == 0 else 3)
                for i, h in enumerate(PLACED):
                    vs = slice(5 * C + h * HD, 5 * C + (h + 1) * HD)
                    hs = slice(i * P, (i + 1) * P)
                    if t == 0:
                        last = pe.matmul(ps[:, 6, h * HD:(h + 1) * HD], wt[:, 0, hs], proj[:, 0, vs], start=True, stop=True)
                    else:
                        pe.matmul(ps[:, 7, h * HD:(h + 1) * HD], wt[:, 2, hs], proj[:, 0, vs], start=True, stop=False)
                        last = pe.matmul(ps[:, 7, h * HD:(h + 1) * HD], wt[:, 1, hs], proj[:, 1, vs], start=False, stop=True)
                last.then_inc(S["b_pv"], 1)
            pe.wait_ge(S["a_done"], 1)
            pe.wait_ge(S["b_ev"], T)
            for b in range(2 * T):
                t, h = b // 2, b % 2
                turn4(4 + b, lambda i: mixed[:, t, (4 * h + i) * P:(4 * h + i + 1) * P], S["mx_tr"])
            pe.wait_ge(S["mx_lo"], 2 * T)
            for g in range(G_OUT, G_FFN):
                q = g - G_OUT
                half_cols(g, g % RING, e_hi, e_lo, q % 2 * 4, 4, (q // 2 * 2, q // 2 * 2 + 1), C,
                          q % 2 == 0, q % 2 == 1, BOTH)
                if q >= 2:
                    norm_turn(1, (2 * (q - 2), 2 * (q - 2) + 1))

            def f_turn(c):
                pe.wait_ge(S["f_ufree"], T * (c + 1))
                if c:
                    pe.wait_ge(S["f_lo"], T * c)
                for t in range(T):
                    turn4(4 + t, lambda i: f_a[:, t, i * P:(i + 1) * P], S["f_tr"], min(4, D_FF // P - 4 * c))

            for g in range(G_FFN, G_DOWN):
                q = g - G_FFN
                c = q // 4
                if q < 2:
                    pe.wait_ge(n_lo[1], 2 * (q + 1))
                if q < 4 * FFC:
                    up = q // 2 % 2
                    if q % 4 == 0 and c:
                        pe.wait_ge(S["f_silu"], T * c)
                    if q % 4 == 2 and c:
                        pe.wait_ge(S["f_ufree"], T * c)
                    half_cols(g, g % RING, f_hi, f_lo, q % 2 * 4, 4, (2 * up, 2 * up + 1), C,
                              q % 2 == 0, q % 2 == 1, BOTH)
                    if q % 4 == 1 and c:
                        f_turn(c - 1)
                else:
                    up = q - 4 * FFC
                    pe.wait_ge(S["f_ufree" if up else "f_silu"], T * FFC)
                    half_cols(g, g % RING, f_hi, f_lo, 0, KD, (2 * up, 2 * up + 1), D_FF - FFC * C, True, True, BOTH)
                    if not up:
                        f_turn(FFC - 1)
            pe.wait_ge(S["f_silu"], T * (FFC + 1))
            NV = D_FF // 256
            for v in range(NV):
                g = G_DOWN + v
                c = v // 2
                pe.wait_ge(S["f_lo"], T * (c + 1))
                half_rows(g, g % RING, fa_hi, fa_lo, 2 * v, ((0, 1), (6, 7)), v == 0, v == NV - 1, BOTH)
                if v == 0:
                    f_turn(FFC)
            norm_turn(2)
            for g in range(G_OIN, G_OOUT):
                q = g - G_OIN
                if q < 2:
                    pe.wait_ge(n_lo[2], 2 * (q + 1))
                n = q // 2
                if q % 2 == 0 and n >= 2:
                    pe.wait_ge(S["oi_ev"], T * (n - 1))
                half_cols(g, g % RING, o_hi, o_lo, q % 2 * 4, 4, (2 * (n % 2), 2 * (n % 2) + 1), C,
                          q % 2 == 0, q % 2 == 1, BOTH)
                if q == 5:
                    pe.wait_ge(S["crow_in"], 64)
                    for b in range(4):
                        last = pe.transpose(ps[:, 6, b * (TAPS + 3):(b + 1) * (TAPS + 3)],
                                            conv_row[:, b * P:(b + 1) * P], ident[0:TAPS + 3, 0:TAPS + 3])
                    last.then_inc(S["cw_tr"], 1)
                    for t in range(T):
                        pe.wait_ge(S["u_mul"], t + 1)
                        turn4(4 + t, lambda i: oproj[:, t, i * P:(i + 1) * P], S["u_tr"])
            pe.wait_ge(S["oi_ev"], 5 * T)
            pe.wait_ge(S["u_ev"], T)
            for i in range(4):
                part, t = i // 2, i % 2
                turn4(4 + i, lambda b: oproj[:, t, (2 + part) * C + b * P:(2 + part) * C + (b + 1) * P], S["ot_tr"])
            pe.wait_ge(S["ot_ev"], 4)
            pe.wait_ge(S["bias_l"], 1)
            for t in range(T):
                scores(t, oqkT, (bias_hi, bias_lo), S["o_sc"])
            OT = [(0, 0, 0), (0, 0, 4), (1, 0, 0), (1, 0, 4), (1, 1, 0), (1, 1, 4)]
            pe.wait_ge(S["o_ex"], HEADS * T)
            for i, (t, kb, h0) in enumerate(OT):
                n_k = P * (t + 1)
                turn4(i, lambda h: po[:, t * D + (h0 + h) * n_k + kb * P:t * D + (h0 + h) * n_k + (kb + 1) * P], S["o_tr"])
            for t in range(T):
                pe.wait_ge(S["o_tev"], 6)
                for i, h in enumerate(PLACED):
                    for kb in range(t + 1):
                        last = pe.matmul(ps[:, t, i * HD:(i + 1) * HD],
                                         poT[:, ((t + kb) * HEADS + i) * P:((t + kb) * HEADS + i + 1) * P],
                                         oproj[:, kb, 4 * C + h * HD:4 * C + (h + 1) * HD],
                                         start=kb == 0, stop=kb == t)
                last.then_inc(S["o_pv"], 1)
            pe.wait_ge(S["conv_step"], 4 * TAPS)
            for t in range(T):
                turn4(6 + t, lambda i: cv[:, i, t * P:(t + 1) * P], S["ct_tr"])
            for t in range(T):
                pe.wait_ge(S["o_norm"], t + 1)
                turn4(4 + t, lambda i: od[:, t, i * P:(i + 1) * P], S["od_tr"])
            pe.wait_ge(S["cn_done"], T)
            for b2 in range(2):
                for b in range(2):
                    for t in range(T):
                        blk = 2 * b2 + b
                        last = pe.transpose(ps[:, 2 + b2, b * SEQ + t * P:b * SEQ + (t + 1) * P],
                                            cn[:, t, blk * P:(blk + 1) * P], ident)
                last.then_inc(S["cb_tr"], 1)
            pe.wait_ge(S["c_lo"], 1)
            pe.wait_ge(S["od_lo"], T)
            for g in range(G_OOUT, G_MOE):
                q = g - G_OOUT
                half_cols(g, g % RING, o_hi, o_lo, q % 2 * 4, 4, (q // 2 * 2, q // 2 * 2 + 1), C,
                          q % 2 == 0, q % 2 == 1, BOTH)
                if q >= 2:
                    norm_turn(3, (2 * (q - 2), 2 * (q - 2) + 1))
            pe.wait_ge(S["router_in"], 16)
            for b, (h, t) in enumerate(BLOCKS):
                pe.wait_ge(n_full[3], b + 1)
                for k in range(4):
                    last = pe.matmul(ps[:, t, 0:N_EXP], m_full[:, b, k * P:(k + 1) * P], router[:, 4 * h + k, :],
                                     start=h == 0 and k == 0, stop=h == 1 and k == 3)
            last.then_inc(S["r_mm"], 1)
            pe.wait_ge(S["sel_s"], 1)
            lexc = cst[:, K_LEXC:K_LEXC + P]
            pe.matmul(ps[:, 2, 0:N_EXP], lexc, sel[:, 0, :], start=True, stop=True)
            pe.matmul(ps[:, 3, 0:N_EXP], ones, sel[:, 0, :], start=True, stop=False)
            pe.matmul(ps[:, 3, 0:N_EXP], lexc, sel[:, 1, :], start=False, stop=True)
            pe.matmul(ps[:, 4, 0:N_EXP], ones, sel[:, 0, :], start=True, stop=False)
            pe.matmul(ps[:, 4, 0:N_EXP], ones, sel[:, 1, :], start=False, stop=True).then_inc(S["cnt_mm"], 1)

            def gather(i, n):
                pe.wait_ge(S["pk"], i + 1)
                for r in range(4):
                    if n == 2 and r >= 2:
                        pe.wait_ge(S["ga_lo"], 4 * i + (r - 1))
                    c0 = 0 if n == 2 else r // 2 * SEQ
                    for c in range(2):
                        for t in range(T):
                            last = pe.matmul(ps[:, 2 + r % 2, c0 + c * n * P:c0 + (c + 1) * n * P],
                                             h_all[:, t, (2 * r + c) * P:(2 * r + c + 1) * P], pick[:, t, 0:n * P],
                                             start=t == 0, stop=t == T - 1)
                    last.then_inc(S["ga_mm"], 1)

            def halves(j, us, n, packed):
                rows = [slice(t * P, (t + 1) * P) for t in range(n)]
                for u in us:
                    g, r = gm(j, u), (G_MOE + u) % RING
                    c, up = u // 4, u // 2 % 2
                    if u < 4 * EC:
                        if u % 4 == 0 and c:
                            pe.wait_ge(S["e_silu"], EC * j + c)
                        if u % 4 == 2 and c:
                            pe.wait_ge(S["e_ufree"], EC * j + c)
                        half_cols(g, r, g_hi, g_lo, u % 2 * 4, 4, (2 * up, 2 * up + 1), C, u % 2 == 0, u % 2 == 1,
                                  rows, packed)
                    else:
                        v = u - 4 * EC
                        pe.wait_ge(S["e_lo"], EC * j + (max(v // 2 + 1, EC - 1) if v == 0 else v // 2 + 1))
                        half_rows(g, r, ea_hi, ea_lo, 2 * v, ((6, 7), (4, 5)), v == 0, v == 2 * EC - 1, rows, packed)
                    if u == 3:
                        pe.wait_ge(S["sc_add"], 8 * j + 1)
                        for n_ in range(2):
                            for t in range(T):
                                last = pe.transpose(ps[:, 6, (n_ * T + t) * P:(n_ * T + t + 1) * P],
                                                    pick[:, t, n_ * P:(n_ + 1) * P], ident)
                        last.then_inc(S["pt_mm"], 1)
                    if u % 4 == 1 and (4 < u < 4 * EC or u == 4 * EC + 1):
                        c = min(c, EC)
                        pe.wait_ge(S["e_ufree"], EC * j + c)
                        if c > 1:
                            pe.wait_ge(S["e_lo"], EC * j + (c - 1))
                        for t in range(n):
                            for i in range(4):
                                dst = ps[:, (0 if c == EC else 4) + t, i * P:(i + 1) * P]
                                block_in = e_a[:, t, i * P:(i + 1) * P]
                                if packed and t:
                                    last = pe.matmul(dst, block_in, kept[:, K_FOLD:K_FOLD + P], start=True, stop=True)
                                else:
                                    last = pe.transpose(dst, block_in, ident)
                        last.then_inc(S["e_tr"], 1)

            def scatter(j, n):
                pe.wait_ge(S["pt_ev"], j + 1)
                for r in range(4):
                    tile, c0, wd = TILE_OF(n, r), COL_OF(n, r), WIDE(n)
                    bank, b0 = place(n, r)
                    pe.wait_ge(S["y_lo_s"], 4 * j + (4 if n == 1 and r >= 2 else 2 if n == 2 and r == 1 else r + 1))
                    if n == 2 and r >= 2:
                        pe.wait_ge(S["sc_add"], 8 * j + (2 * r - 1))
                    for t in range(T):
                        pe.matmul(ps[:, bank + t, b0:b0 + wd], put_r[:, tile, t, :], y_hi[:, c0:c0 + wd],
                                  start=True, stop=False)
                        pe.matmul(ps[:, bank + t, b0:b0 + wd], put_r[:, tile, t, :], y_lo[:, c0:c0 + wd],
                                  start=False, stop=True).then_inc(S["sc_mm"], 1)
                if n == 2:
                    pe.wait_ge(S["sc_add"], 8 * j + 9)

            pe.wait_ge(S["h_full"], T)
            pe.wait_ge(S["route"], 1)
            many = many_of(pe, 0)
            by_tiles(pe, many, lambda n: gather(0, n))
            pe.wait_ge(S["ga_lo"], 4)
            by_form(pe, many, lambda n, packed: halves(0, range(LEAD), n, packed))
            with pe.Fori(0, N_EXP) as j:
                many, many2 = many_of(pe, j), many_of(pe, j + 1)
                by_form(pe, many, lambda n, packed: halves(j, range(LEAD, MID), n, packed))
                pe.wait_ge(S["e_ufree"], EC * j + EC)
                by_tiles(pe, many2, lambda n: gather(j + 1, n))
                by_form(pe, many, lambda n, packed: halves(j, range(MID, JOB), n, packed))
                pe.wait_ge(S["ga_lo"], 4 * j + 8)
                by_form(pe, many2, lambda n, packed: halves(j + 1, range(LEAD), n, packed))
                by_tiles(pe, many, lambda n: scatter(j, n))


_INS = ['x', 'ev_norm_mix', 'ev_w_in', 'ev_lambda_q1', 'ev_lambda_k1', 'ev_lambda_q2', 'ev_lambda_k2',
        'ev_subln', 'ev_w_out', 'ev_norm_ffn', 'ev_ffn_gate', 'ev_ffn_up', 'ev_ffn_down',
        'od_norm_mix', 'od_w_in', 'od_conv_w', 'od_conv_b', 'od_conv_ln_g', 'od_conv_ln_b', 'od_rel_bias',
        'od_w_out', 'od_norm_ffn', 'od_router', 'od_exp_gate', 'od_exp_up', 'od_exp_down', 'final_norm']


def kernel(**inputs):
    import numpy as _np
    import concourse.bacc as _bacc
    from concourse import mybir as _mybir
    from concourse.bass_utils import run_bass_kernel_spmd as _run

    nc = _bacc.Bacc("TRN2", target_bir_lowering=False, num_devices=1)
    arrays, aps = {}, {}
    for name in _INS + ["cst"]:
        a = constants() if name == "cst" else _np.ascontiguousarray(inputs[name])
        arrays[f"in_{name}_dram"] = a
        aps[name] = nc.dram_tensor(f"in_{name}_dram", a.shape, _mybir.dt.from_np(a.dtype), kind="ExternalInput").ap()
    out = nc.dram_tensor("out_0_dram", (1, SEQ, D), _mybir.dt.float32, kind="ExternalOutput").ap()
    trunk(nc, aps, out)
    r = _run(nc, [arrays], core_ids=[0])
    return r.results[0]["out_0_dram"]
```

```python
from contextlib import ExitStack

import numpy as np

import concourse.bass as bass
from concourse import mybir

ALU = mybir.AluOpType
ACT = mybir.ActivationFunctionType
AX = mybir.AxisListType.X
F32 = mybir.dt.float32
F32R = mybir.dt.float32r
I32 = mybir.dt.int32
U32 = mybir.dt.uint32

P = 128
SEQ = 256
T = SEQ // P
D = 1024
KD = D // P
C = 512
HD = 64
A_HEADS = 4
HEADS = 8
PLACED = [0, 2, 4, 6, 1, 3, 5, 7]
D_FF = 2816
E_FF = 3584
N_EXP = 8
TAPS = 31
CONV_C = 512
CHUNK = 64
MAX_REL = 128
REL = 2 * MAX_REL + 1
EPS = 1e-6
LAMBDA_INIT = 0.2
NEG = -1e30

TAP_CUT = (1, 3, 5, 8, 20, 24)
POOL_BLOCK = 3
TAP_RING = 8
ACT_TAPS = (1, 4, 9, 15, 21, 27, TAPS)
RAW = 6
RING = 3
HALF = 2048
FFC = D_FF // C
EC = E_FF // C
G_IN = 0
G_OUT = G_IN + 12
G_FFN = G_OUT + 4
G_DOWN = G_FFN + 4 * FFC + 2
G_OIN = G_DOWN + D_FF // 256
G_OOUT = G_OIN + 10
G_MOE = G_OOUT + 4
JOB = 6 * EC
assert JOB % RAW == 0 and JOB % RING == 0 and G_MOE % RING == 0
MID = 4 * EC + 2
LEAD = 2

K_IDENT, K_IOTA, K_FOLD, K_IOTA8 = 0, P, 3 * P, 4 * P
K_KEPT = K_IOTA8 + 8
K_NTRI, K_NONES, K_DMASK, K_FLIP, K_ROW = (P * i for i in range(5))
K_COL = K_ROW + P
K_ROUND = K_COL + SEQ
K_LEXC, K_ONES = K_ROUND, K_ROUND + P
K_COS = K_ONES + P
K_SIN = K_COS + T * 32
K_ALL = K_SIN + T * 32


def constants():
    kept, c = np.zeros((P, K_KEPT), np.float32), np.zeros((P, K_ALL), np.float32)
    p, i = np.arange(P)[:, None], np.arange(P)[None, :]
    kept[:, K_IDENT:K_IDENT + P] = p == i
    kept[:, K_IOTA:K_IOTA + SEQ] = np.arange(SEQ)
    kept[:, K_FOLD:K_FOLD + P] = p % (P // 2) == i % (P // 2)
    kept[:, K_IOTA8:K_IOTA8 + 8] = np.arange(8)
    c[:, K_NTRI:K_NTRI + P] = np.where(p >= i, -1.0, 0.0)
    c[:, K_DMASK:K_DMASK + P] = np.where(p >= i, NEG, 0.0)
    c[:, K_LEXC:K_LEXC + P] = p < i
    c[:, K_ONES:K_ONES + P] = 1.0
    c[:, K_NONES:K_NONES + P] = -1.0
    c[:, K_FLIP:K_FLIP + P] = p + i == P - 1
    half = HD // 2
    freq = (np.float32(10000.0) ** (-np.arange(half, dtype=np.float32) * np.float32(2.0) / np.float32(HD)))
    ang = np.arange(SEQ, dtype=np.float32)[:, None] * freq.astype(np.float32)[None, :]
    ang = ang.reshape(T, P, half).transpose(1, 0, 2).reshape(P, T * half)
    c[:, K_COS:K_COS + T * half] = np.cos(ang)
    c[:, K_SIN:K_SIN + T * half] = np.sin(ang)
    c[:, K_ROW:K_ROW + P] = i < CHUNK
    c[:, K_COL:K_COL + SEQ] = np.where(np.arange(SEQ) >= SEQ - CHUNK, NEG, 0.0)
    return np.concatenate([kept, c], axis=1)


def trunk(nc, w, out):
    ctx = ExitStack()
    with ctx:
        def sb(name, shape, dt=F32, at=ctx):
            return at.enter_context(nc.sbuf_tensor(name, shape, dt))

        def sem(name):
            return ctx.enter_context(nc.semaphore(name))

        raw = sb("raw", [P, RAW, HALF])
        whi = sb("whi", [P, RING, HALF], F32R)
        wlo = sb("wlo", [P, RING, HALF], F32R)
        x = sb("x", [P, T, D])
        kept = sb("kept", [P, K_KEPT])
        gains_row = sb("gains_row", [4 * KD, P])
        gains = sb("gains", [P, 4, KD])
        ss = sb("ss", [P, 5, T])
        std = sb("std", [P, 5, T])
        rstd = sb("rstd", [P, 5, T])
        rstd_q = sb("rstd_q", [P, 3, T])
        eps = sb("eps", [P, 1])
        ident = kept[:, K_IDENT:K_IDENT + P]

        layers = ExitStack()
        cst = sb("cst", [P, K_ALL], F32, layers)
        ones = cst[:, K_ONES:K_ONES + P]
        cst_r = sb("cst_r", [P, K_ROUND], F32R, layers)
        ident_r = sb("ident_r", [P, P], F32R, layers)
        with ExitStack() as even:
            with ExitStack() as tmp:
                sp = sb("sp", [P, 3, D], F32, tmp)
            with ExitStack() as tmp:
                sp_lo = sb("sp_lo", [P, 3, D], F32R, tmp)
            e_hi = sb("e_hi", [P, KD, SEQ], F32R, even)
            e_lo = sb("e_lo", [P, KD, SEQ], F32R, even)
            with ExitStack() as tmp:
                e_junk = sb("e_junk", [P, D], F32, tmp)
                e_full = sb("e_full", [P, 2 * T, C], F32, tmp)
                rope_a = sb("rope_a", [P, C], F32, tmp)
                rope_b = sb("rope_b", [P, C], F32, tmp)
            with ExitStack() as tmp:
                pa = sb("pa", [P, HEADS * 3 * P], F32, tmp)
                pd = sb("pd", [P, A_HEADS * 3 * P], F32, tmp)
                pdT = sb("pdT", [P, A_HEADS * 3 * P], F32, tmp)
            with ExitStack() as tmp:
                wt = sb("wt", [P, 3, D], F32, tmp)
            sb("even_tmp", [P, 6 * D], F32, even)
            proj = sb("proj", [P, T, 6 * C], F32, even)
            with ExitStack() as tmp:
                sp_hi = sb("sp_hi", [P, 3, D], F32R, tmp)
            qkT = sb("qkT", [P, 16, SEQ], F32, even)
            mixed = sb("mixed", [P, T, D], F32, even)
            lam_in = sb("lam_in", [P, 4, HD], F32, even)
            lam_j = sb("lam_j", [P, HD], F32, even)
            lam_s = sb("lam_s", [P, 4], F32, even)
            subln = sb("subln", [P, P], F32, even)
            a_nm = sb("a_nm", [P, T, HEADS], F32, even)
            a_sum = sb("a_sum", [P, T, HEADS], F32, even)
            a_r = sb("a_r", [P, T, HEADS], F32, even)
            a_ms = sb("a_ms", [P, T, A_HEADS], F32, even)
            a_sd = sb("a_sd", [P, T, A_HEADS], F32, even)
            a_rs = sb("a_rs", [P, T, A_HEADS], F32, even)
        with ExitStack() as ffn:
            fa_lo = sb("fa_lo", [P, D_FF // P, SEQ], F32R, ffn)
            f_hi = sb("f_hi", [P, KD, SEQ], F32R, ffn)
            f_lo = sb("f_lo", [P, KD, SEQ], F32R, ffn)
            f_full = sb("f_full", [P, 2 * T, C], F32, ffn)
            fa_hi = sb("fa_hi", [P, D_FF // P, SEQ], F32R, ffn)
            f_s = sb("f_s", [P, T, C], F32, ffn)
            f_a = sb("f_a", [P, T, C], F32, ffn)
        with ExitStack() as odd:
            o_hi = sb("o_hi", [P, KD, SEQ], F32R, odd)
            o_lo = sb("o_lo", [P, KD, SEQ], F32R, odd)
            with ExitStack() as tmp:
                o_junk = sb("o_junk", [P, D], F32, tmp)
                o_full = sb("o_full", [P, 2 * T, C], F32, tmp)
            with ExitStack() as tmp:
                po = sb("po", [P, HEADS * 3 * P], F32, tmp)
                tap_out = po[:, D:D + TAP_RING * SEQ].rearrange("p (k s) -> p k s", s=SEQ)
                with ExitStack() as tmp2:
                    bias_hi = sb("bias_hi", [P, HEADS, SEQ], F32R, tmp2)
                poT = sb("poT", [P, HEADS * 3 * P], F32, tmp)
            sb("odd_tmp", [P, 6 * D], F32, odd)
            oproj = sb("oproj", [P, T, 5 * C], F32, odd)
            oqkT = sb("oqkT", [P, 8, SEQ], F32, odd)
            uT = sb("uT", [P, 4, TAPS - 1 + SEQ], F32, odd)
            cv = sb("cv", [P, 4, SEQ], F32, odd)
            cn = oproj[:, :, 0:C]
            od = oproj[:, :, C:2 * C]
            conv_row = sb("conv_row", [TAPS + 3, CONV_C], F32, odd)
            conv = sb("conv", [P, 4, TAPS + 3], F32, odd)
            rel_in = sb("rel_in", [HEADS, REL], F32, odd)
            rel_rev = sb("rel_rev", [HEADS, 3 * P], F32, odd)
            with ExitStack() as tmp:
                bias = sb("bias", [P, HEADS, SEQ], F32, tmp)
            bias_lo = sb("bias_lo", [P, HEADS, SEQ], F32R, odd)
            o_nm = sb("o_nm", [P, T, HEADS], F32, odd)
            o_sum = sb("o_sum", [P, T, HEADS], F32, odd)
            o_r = sb("o_r", [P, T, HEADS], F32, odd)
            bn6 = sb("bn6", [P, T, 6], F32, odd)
            bn2 = sb("bn2", [P, T, 2], F32, odd)
            bsd = sb("bsd", [P, T], F32, odd)
            brs = sb("brs", [P, T], F32, odd)
        layers.close()
        with ExitStack() as moe:
            with ExitStack() as tmp:
                sb("cst_still", [P, K_ALL + K_ROUND + P], F32, tmp)
                sb("o_hi_still", [P, 2 * KD, SEQ], F32R, tmp)
                m_full = sb("m_full", [P, 2 * T, C], F32, tmp)
                m_junk = sb("m_junk", [P, D], F32, tmp)
                gain_row = sb("gain_row", [P, D], F32, tmp)
                router = sb("router", [P, KD, N_EXP], F32, tmp)
                logit = sb("logit", [P, T, N_EXP], F32, tmp)
                top = sb("top", [P, T, 8], F32, tmp)
                topi = sb("topi", [P, T, 8], U32, tmp)
                topf = sb("topf", [P, T, 8], F32, tmp)
                gate = sb("gate", [P, T, 4], F32, tmp)
                hot = sb("hot", [P, T, 2, N_EXP], F32, tmp)
                sel = sb("sel", [P, T, N_EXP], F32, tmp)
            with ExitStack() as tmp:
                ea_hi = sb("ea_hi", [P, E_FF // P, SEQ], F32R, tmp)
                ea_lo = sb("ea_lo", [P, E_FF // P, SEQ], F32R, tmp)
            with ExitStack() as tmp:
                fin_x = sb("fin_x", [P, T, D], F32, tmp)
            sb("moe_tmp", [P, 4 * E_FF], F32, moe)
            y_hi = sb("y_hi", [P, D], F32R, moe)
            y_lo = sb("y_lo", [P, D], F32R, moe)
            h_all = sb("h_all", [P, T, D], F32, moe)
            g_hi = sb("g_hi", [P, KD, SEQ], F32R, moe)
            g_lo = sb("g_lo", [P, KD, SEQ], F32R, moe)
            e_a = sb("e_a", [P, 2, C], F32, moe)
            pick = sb("pick", [P, T, SEQ], F32, moe)
            put_r = sb("put_r", [P, 2, T, P], F32R, moe)
            comb = sb("comb", [P, T, N_EXP], F32, moe)
            slot = sb("slot", [P, T, N_EXP + 1], F32, moe)
            slot_b = sb("slot_b", [P, T, N_EXP + 1], F32, moe)
            over_f = sb("over_f", [P, 16], F32, moe)
            over_i = sb("over_i", [P, 16], I32, moe)

        ps = ctx.enter_context(nc.psum_tensor("ps", [P, 8, C], F32))
        rel_dram = nc.dram_tensor("rel_scratch", (HEADS, 3 * P), F32, kind="Internal")

        raw_in = [sem(f"raw_in{s}") for s in range(RAW)]
        hi_done = sem("hi_done")
        lo_done = sem("lo_done")
        pe_half = sem("pe_half")
        S = {n: sem(n) for n in (
            "x_in cst_in cst2_in row_in lam_ld sub_in crow_in rel_ld rel_st bias_in router_in grow_in fin_in out_st "
            "eps_set gains_tr gains_ev "
            "ip_ev roped at_tr at_ev_a at_ev_d a_sc a_mx a_ex a_pd a_tr a_tev a_pv a_oev a_msq a_sqrt a_done "
            "lam_sum lam_exp b_z b_ex b_ln b_sp b_sph b_spl cr_a cr_b b_cum b_w b_pv b_ev mx_tr mx_hi mx_lo op_add "
            "f_silu f_ufree f_tr f_hi f_lo f_add "
            "oi_ev u_mul u_tr u_ev cw_tr conv_d conv_p tap_mul ct_tr ct_bn ct_sd cn_done cb_tr c_act c_hi c_lo "
            "rel_rv bias_m bias_h bias_l ot_tr ot_ev o_sc o_mx o_ex o_tr o_tev o_pv o_norm od_tr od_hi od_lo oo_add uz "
            "xg h_full r_mm cnt_mm sel_s route g_exp pk ga_mm ga_hi ga_lo pt_mm pt_ev "
            "e_raw e_fold e_silu e_ufree e_tr e_hi e_lo y_hi_s y_lo_s sc_mm sc_add fin_n load_turn dve_chain act_chain final_ok "
        ).split()}
        NORMS = 4
        n_ss = [sem(f"n_ss{i}") for i in range(NORMS + 1)]
        n_std = [sem(f"n_std{i}") for i in range(NORMS + 1)]
        n_rs = [sem(f"n_rs{i}") for i in range(NORMS)]
        n_tr = [sem(f"n_tr{i}") for i in range(NORMS)]
        n_full = [sem(f"n_full{i}") for i in range(NORMS)]
        n_hi = [sem(f"n_hi{i}") for i in range(NORMS - 1)]
        n_lo = [sem(f"n_lo{i}") for i in range(NORMS - 1)]

        BLOCKS = [(0, 0), (0, 1), (1, 0), (1, 1)]
        TURN_BANK = [(4, 5, 6, 7), (4, 5, 6, 7), (2, 3, 4, 5), (4, 5, 6, 7)]
        JUNK = [e_junk[:], f_s[:].rearrange("p t c -> p (t c)"), o_junk[:], m_junk[:]]
        FULL = [e_full, f_full, o_full, m_full]
        HI = [e_hi, f_hi, o_hi]
        LO = [e_lo, f_lo, o_lo]
        X_SUM = [None, S["op_add"], S["f_add"], S["oo_add"]]

        def cols_view(ap, k=4):
            return ap.rearrange("p (k n) -> p k n", k=k)

        def cols_src(m, k0, kn, c0, cn_):
            return m.rearrange("(k p) n -> p k n", p=P)[:, k0:k0 + kn, c0:c0 + cn_]

        def rows_src(m, b0, bn):
            return m[b0 * P:(b0 + bn) * P, :].rearrange("(b p) n -> p b n", p=P)

        W_IN, W_OUT = w["ev_w_in"][0], w["ev_w_out"][0]
        W_G, W_U, W_D = w["ev_ffn_gate"][0], w["ev_ffn_up"][0], w["ev_ffn_down"][0]
        O_IN, O_OUT = w["od_w_in"][0], w["od_w_out"][0]

        def static_src(g):
            if g < G_OUT:
                return cols_src(W_IN, g % 2 * 4, 4, g // 2 * C, C), 4
            if g < G_FFN:
                g -= G_OUT
                return cols_src(W_OUT, g // 2 * 4, 4, g % 2 * C, C), 4
            if g < G_DOWN:
                g -= G_FFN
                if g >= 4 * FFC:
                    return cols_src((W_G, W_U)[g - 4 * FFC], 0, KD, FFC * C, D_FF - FFC * C), KD
                return cols_src((W_G, W_U)[g // 2 % 2], g % 2 * 4, 4, g // 4 * C, C), 4
            if g < G_OIN:
                return rows_src(W_D, 2 * (g - G_DOWN), 2), 2
            if g < G_OOUT:
                g -= G_OIN
                return cols_src(O_IN, g % 2 * 4, 4, g // 2 * C, C), 4
            g -= G_OOUT
            return cols_src(O_OUT, g // 2 * 4, 4, g % 2 * C, C), 4

        EG = w["od_exp_gate"][0].rearrange("e (k p) n -> p e k n", p=P)
        EU = w["od_exp_up"][0].rearrange("e (k p) n -> p e k n", p=P)
        ED = w["od_exp_down"][0].rearrange("e (b p) n -> p e b n", p=P)

        def expert_src(e, u):
            one = bass.ds(e, 1)
            if u < 4 * EC:
                m, c0, k0 = (EG, EU)[u // 2 % 2], u // 4 * C, u % 2 * 4
                return m[:, one, k0:k0 + 4, c0:c0 + C].rearrange("p e k n -> p (e k) n"), 4
            b0 = 2 * (u - 4 * EC)
            return ED[:, one, b0:b0 + 2, :].rearrange("p e b n -> p (e b) n"), 2

        def gm(j, u):
            return j * JOB + (G_MOE + u)

        block = ctx.enter_context(nc.Block())

        @block.sync
        def _(sp_):
            def load_half(g, s, src, k):
                if not isinstance(g, int) or g >= RAW:
                    sp_.wait_ge(lo_done, g - (RAW - 1))
                    if not isinstance(g, int):
                        sp_.sem_inc(S["load_turn"], 1)
                sp_.dma_start(cols_view(raw[:, s, :], k), src).then_inc(raw_in[s], 16)

            sp_.dma_start(x[:], w["x"][0].rearrange("(t p) d -> p t d", p=P)).then_inc(S["x_in"], 16)
            sp_.dma_start(kept[:], w["cst"][:, 0:K_KEPT]).then_inc(S["cst_in"], 16)
            for i, name in enumerate(("ev_norm_mix", "ev_norm_ffn", "od_norm_mix", "od_norm_ffn")):
                sp_.dma_start(gains_row[i * KD:(i + 1) * KD, :],
                              w[name][0].rearrange("(k p) -> k p", p=P)).then_inc(S["row_in"], 16)
            for g in range(RAW):
                load_half(g, g % RAW, *static_src(g))
                if g == RING:
                    sp_.dma_start(cst[:], w["cst"][:, K_KEPT:K_KEPT + K_ALL]).then_inc(S["cst2_in"], 16)
            for i, name in enumerate(("ev_lambda_q1", "ev_lambda_k1", "ev_lambda_q2", "ev_lambda_k2")):
                sp_.dma_start(lam_in[:, i, :], w[name].broadcast_to([P, HD])).then_inc(S["lam_ld"], 16)
            sp_.dma_start(subln[:], w["ev_subln"].broadcast_to([P, P])).then_inc(S["sub_in"], 16)
            for g in range(RAW, G_OIN + RAW):
                load_half(g, g % RAW, *static_src(g))
            sp_.wait_ge(S["f_add"], 4)
            for r0, rn, name in ((0, TAPS, "od_conv_w"), (TAPS, 1, "od_conv_b"),
                                 (TAPS + 1, 1, "od_conv_ln_g"), (TAPS + 2, 1, "od_conv_ln_b")):
                src = w[name][0] if rn > 1 else w[name]
                sp_.dma_start(conv_row[r0:r0 + rn, :], src).then_inc(S["crow_in"], 16)
            sp_.dma_start(rel_in[:], w["od_rel_bias"][0]).then_inc(S["rel_ld"], 16)
            sp_.wait_ge(S["rel_rv"], 2)
            sp_.dma_start(rel_dram.ap(), rel_rev[:]).then_inc(S["rel_st"], 16)
            sp_.wait_ge(S["rel_st"], 16)
            hankel = bass.AP(rel_dram, 0, [[1, P], [3 * P, HEADS], [1, SEQ]])
            sp_.dma_start(bias[:], hankel).then_inc(S["bias_in"], 16)
            for g in range(G_OIN + RAW, G_MOE):
                load_half(g, g % RAW, *static_src(g))
            for u in range(RAW):
                load_half(G_MOE + u, (G_MOE + u) % RAW, *expert_src(0, u))
                if u == 0:
                    sp_.wait_ge(S["od_lo"], T)
                    sp_.dma_start(gain_row[:], w["od_norm_ffn"].broadcast_to([P, D])).then_inc(S["grow_in"], 16)
                    sp_.dma_start(router[:],
                                  w["od_router"][0].rearrange("(k p) e -> p k e", p=P)).then_inc(S["router_in"], 16)

            def load_rest(j, e, u0, u1):
                for u in range(u0, u1):
                    load_half(gm(j, u), (G_MOE + u) % RAW, *expert_src(e, u % JOB))

            with sp_.Fori(0, N_EXP - 1) as j:
                load_rest(j, j, RAW, JOB)
                load_rest(j, j + 1, JOB, JOB + RAW)
            load_rest(N_EXP - 1, N_EXP - 1, RAW, JOB)
            sp_.wait_ge(S["ga_mm"], 4 * N_EXP)
            sp_.dma_start(h_all[:, 0, :], w["final_norm"].rearrange("(a d) -> a d", a=1).broadcast_to([P, D])).then_inc(S["fin_in"], 16)
            for s in range(RAW):
                n_loads = (G_MOE + N_EXP * JOB - 1 - s) // RAW + 1
                sp_.wait_ge(raw_in[s], 16 * n_loads)
            for t in range(T):
                sp_.wait_ge(S["final_ok"], t + 1)
                sp_.dma_start(out[0, t * P:(t + 1) * P, :], fin_x[:, t, :]).then_inc(S["out_st"], 16)
            sp_.wait_ge(S["out_st"], 16 * T)

        def conv_start(eng, blocks, done):
            eng.wait_ge(S["u_ev"], T)
            eng.wait_ge(S["uz"], 1)
            for b in blocks:
                eng.tensor_scalar(cv[:, b, :], uT[:, b, 0:SEQ], conv[:, b, 0:1], conv[:, b, TAPS:TAPS + 1],
                                  ALU.mult, ALU.add).then_inc(done, 1)

        Z_BANK = (6, 0, 2)
        A_TURN = (4, 5, 4)
        A_OUT = (5, 4)
        O_OUT = (0, 4)

        def z_of(i):
            return ps[:, Z_BANK[i]:Z_BANK[i] + 2, :].rearrange("p b c -> p (b c)")

        def place(n, r):
            return ((2, 6, 4, 6)[r], 0) if n == 2 else ((4, 6)[r // 2], r % 2 * (C // 2))

        def out_piece(part, n, r):
            flat = part[1][:, 0:D // SEQ, :].rearrange("p k s -> p (k s)") if TILE_OF(n, r) else part[0]
            return flat[:, COL_OF(n, r):COL_OF(n, r) + WIDE(n)]

        Y_HI, Y_LO = (y_hi, ea_hi), (y_lo, ea_lo)
        TILE_OF = lambda n, r: r // 2 if n == 2 else 0
        COL_OF = lambda n, r: r % 2 * C + (0 if n == 2 else r // 2 * (C // 2))
        WIDE = lambda n: n * (C // 2)

        def by_tiles(eng, many, body):
            with eng.If(many > 0):
                body(2)
            with eng.Else():
                body(1)

        def by_form(eng, many, body):
            with eng.If(many > 1):
                body(2, False)
            with eng.Else():
                by_tiles(eng, many, lambda n: body(n, n == 2))

        def many_of(eng, e):
            return eng.value_load(over_i[0:1, bass.ds(e, 1)], min_val=0, max_val=2)

        H = P // 2
        LAST = N_EXP - 1

        def is_(j, e):
            return isinstance(j, int) and j == e

        def each_expert(eng, body):
            with eng.Fori(0, LAST) as j:
                body(j, False)
            body(LAST, True)

        @block.scalar
        def _(act):
            chain = [0]

            def link(ins):
                chain[0] += 1
                ins.then_inc(S["act_chain"], 1)
                act.wait_ge(S["act_chain"], chain[0])

            def hi(g, s, landed):
                act.wait_ge(raw_in[s], landed)
                if not isinstance(g, int) or g >= RING:
                    act.wait_ge(pe_half, g - (RING - 1))
                r = (s % RING)
                act.copy(whi[:, r, :], raw[:, s, :]).then_inc(hi_done, 1)

            def hi_static(g):
                hi(g, g % RAW, 16 * (g // RAW + 1))

            def norm_std(n):
                if n == NORMS:
                    act.wait_ge(n_ss[n], T)
                else:
                    act.wait_ge(X_SUM[n] if n else S["x_in"], 4 if n else 16)
                    for t in range(T):
                        link(act.activation(JUNK[n], x[:, t, :], ACT.Square, accum_out=ss[:, n, t:t + 1]))
                act.activation(std[:, n, :], ss[:, n, :], ACT.Sqrt, bias=eps[:], scale=1.0 / D).then_inc(n_std[n], 1)

            def norm_hi(n, bs=range(2 * T)):
                for b in bs:
                    act.wait_ge(n_full[n], b + 1)
                    h, t = BLOCKS[b]
                    act.copy(HI[n][:, 4 * h:4 * h + 4, t * P:(t + 1) * P],
                             FULL[n][:, b, :].rearrange("p (k s) -> p k s", k=4)).then_inc(n_hi[n], 1)

            act.wait_ge(S["eps_set"], 1)
            act.copy(std[:, NORMS, 0:1], eps[:])
            norm_hi(0)
            for g in range(RING):
                hi_static(g)
            norm_std(0)
            act.wait_ge(S["cst2_in"], 16)
            act.copy(cst_r[:], cst[:, 0:K_ROUND]).then_inc(S["cr_a"], 1)
            act.copy(ident_r[:], ident).then_inc(S["cr_b"], 1)
            for g in range(G_IN, G_OUT):
                hi_static(g + RING)
                if g % 2:
                    n = g // 2
                    act.wait_ge(pe_half, g + 1)
                    act.wait_ge(n_rs[0], 1)
                    for t in range(T):
                        act.activation(proj[:, t, n * C:(n + 1) * C], ps[:, 2 * (n % 2) + t, :], ACT.Copy,
                                       scale=(rstd_q if n in (0, 3) else rstd)[:, 0, t:t + 1]).then_inc(S["ip_ev"], 1)
            for i in range(0, 8, 2):
                act.wait_ge(S["at_tr"], i + 1)
                part, t = i // 2, i % 2
                act.copy(qkT[:, 4 * part:4 * part + 4, t * P:(t + 1) * P],
                         ps[:, 4 + i % 4, :].rearrange("p (k s) -> p k s", k=4)).then_inc(S["at_ev_a"], 1)
            act.wait_ge(S["lam_sum"], 2)
            act.activation(lam_s[:, 2:4], lam_s[:, 0:2], ACT.Exp).then_inc(S["lam_exp"], 1)
            for t in range(T):
                act.wait_ge(S["a_mx"], t + 1)
                n_k = P * (t + 1)
                off = t * HEADS * P
                for s in range(HEADS):
                    src = ps[:, 0 if t == 0 else 2:, :].rearrange("p b c -> p (b c)")[:, s * n_k:(s + 1) * n_k]
                    act.activation(pa[:, off + s * n_k:off + (s + 1) * n_k], src, ACT.Exp,
                                   bias=a_nm[:, t, s:s + 1], accum_out=a_sum[:, t, s:s + 1]).then_inc(S["a_ex"], 1)
            def b_exp(i):
                act.wait_ge(S["b_z"], i + 1)
                link(act.activation(sp[:, i, :], z_of(i), ACT.Abs))
                act.activation(sp[:, i, :], sp[:, i, :], ACT.Exp, scale=-1.0).then_inc(S["b_ex"], 1)

            def a_turned(i):
                act.wait_ge(S["a_tr"], i + 1)
                act.copy(pdT[:, i * C:(i + 1) * C], ps[:, A_TURN[i], :]).then_inc(S["a_tev"], 1)

            b_exp(0)
            a_turned(0)
            b_exp(1)
            a_turned(1)
            a_turned(2)
            b_exp(2)
            for i in range(3):
                act.wait_ge(S["b_ex"], i + 1)
                act.activation(sp[:, i, :], sp[:, i, :], ACT.Ln, bias=1.0).then_inc(S["b_ln"], 1)
            for i in range(3):
                if i == 2:
                    for t in range(T):
                        act.wait_ge(S["a_pv"], t + 1)
                        act.copy(mixed[:, t, 0:C], ps[:, A_OUT[t], :]).then_inc(S["a_oev"], 1)
                act.wait_ge(S["b_sp"], i + 1)
                act.copy(sp_hi[:, i, :], sp[:, i, :]).then_inc(S["b_sph"], 1)
            for t in range(T):
                for h in range(A_HEADS):
                    sq = pd[:, t * C + h * P:t * C + (h + 1) * P]
                    act.activation(sq, ps[:, A_OUT[t], h * P:(h + 1) * P], ACT.Square,
                                   accum_out=a_ms[:, t, h:h + 1]).then_inc(S["a_msq"], 1)
            act.wait_ge(S["a_msq"], A_HEADS * T)
            act.activation(a_sd[:], a_ms[:], ACT.Sqrt, bias=eps[:], scale=1.0 / P).then_inc(S["a_sqrt"], 1)
            act.wait_ge(S["a_pd"], A_HEADS * T)
            for i in range(3):
                act.wait_ge(S["b_cum"], i + 1)
                act.activation(wt[:, i, :], z_of(i), ACT.Exp).then_inc(S["b_w"], 1)

            def mixed_hi(h):
                for t in range(T):
                    b = 2 * h + t
                    act.wait_ge(S["mx_tr"], b + 1)
                    act.copy(e_hi[:, 4 * h:4 * h + 4, t * P:(t + 1) * P],
                             ps[:, 4 + b, :].rearrange("p (k s) -> p k s", k=4)).then_inc(S["mx_hi"], 1)

            mixed_hi(0)
            for t in range(T):
                act.wait_ge(S["b_pv"], t + 1)
                act.copy(mixed[:, t, C:D], ps[:, 6 + t, :]).then_inc(S["b_ev"], 1)
            mixed_hi(1)
            for g in range(G_OUT, G_FFN - 1):
                hi_static(g + RING)
            norm_hi(1)
            hi_static(G_FFN - 1 + RING)
            norm_std(1)

            def f_hi_evac(c):
                nb = min(4, D_FF // P - 4 * c)
                for t in range(T):
                    act.wait_ge(S["f_tr"], T * c + t + 1)
                    act.copy(fa_hi[:, 4 * c:4 * c + nb, t * P:(t + 1) * P],
                             ps[:, 4 + t, 0:nb * P].rearrange("p (k s) -> p k s", k=nb)).then_inc(S["f_hi"], 1)

            for g in range(G_FFN, G_DOWN + D_FF // 256):
                hi_static(g + RING)
                q = g - G_FFN
                c = q // 4
                last = q >= 4 * FFC
                if (not last and q % 4 == 1) or q == 4 * FFC:
                    act.wait_ge(pe_half, g + 1)
                    if c >= 1:
                        act.wait_ge(S["f_ufree"], T * c)
                    wd = C if c < FFC else D_FF - FFC * C
                    act.wait_ge(n_rs[1], 1)
                    for t in range(T):
                        act.activation(f_s[:, t, 0:wd], ps[:, t, 0:wd], ACT.Silu,
                                       scale=rstd[:, 1, t:t + 1]).then_inc(S["f_silu"], 1)
                    if c >= 1:
                        f_hi_evac(c - 1)
                if q == 4 * FFC + 2:
                    f_hi_evac(FFC)
            norm_hi(2)
            norm_std(2)
            for g in range(G_OIN, G_OOUT):
                hi_static(g + RING)
                if g == G_OOUT - 3:
                    act.wait_ge(S["bias_m"], 1)
                    act.copy(bias_hi[:], bias[:]).then_inc(S["bias_h"], 1)
                if (g - G_OIN) % 2:
                    n = (g - G_OIN) // 2
                    act.wait_ge(pe_half, g + 1)
                    act.wait_ge(n_rs[2], 1)
                    for t in range(T):
                        act.activation(oproj[:, t, n * C:(n + 1) * C], ps[:, 2 * (n % 2) + t, :],
                                       ACT.Sigmoid if n == 1 else ACT.Copy,
                                       scale=(rstd_q if n == 2 else rstd)[:, 2, t:t + 1]).then_inc(S["oi_ev"], 1)
                if g >= G_OIN + 4:
                    if g == G_OIN + 4:
                        act.wait_ge(S["u_ev"], T)
                        act.wait_ge(S["uz"], 1)
                    for k in range(*ACT_TAPS[g - G_OIN - 4:g - G_OIN - 2]):
                        if k >= TAP_RING:
                            act.wait_ge(S["conv_p"], k - TAP_RING + 1)
                        act.activation(tap_out[:, k % TAP_RING, :], uT[:, POOL_BLOCK, k:k + SEQ], ACT.Copy,
                                       scale=conv[:, POOL_BLOCK, k:k + 1]).then_inc(S["tap_mul"], 1)
            for i in range(4):
                act.wait_ge(S["ot_tr"], i + 1)
                part, t = i // 2, i % 2
                act.copy(oqkT[:, 4 * part:4 * part + 4, t * P:(t + 1) * P],
                         ps[:, 4 + i, :].rearrange("p (k s) -> p k s", k=4)).then_inc(S["ot_ev"], 1)
            def o_exp(t):
                act.wait_ge(S["o_mx"], t + 1)
                n_k = P * (t + 1)
                off = t * HEADS * P
                for s in range(HEADS):
                    src = ps[:, 0 if t == 0 else 2:, :].rearrange("p b c -> p (b c)")[:, s * n_k:(s + 1) * n_k]
                    act.activation(po[:, off + s * n_k:off + (s + 1) * n_k], src, ACT.Exp,
                                   bias=o_nm[:, t, s:s + 1], accum_out=o_sum[:, t, s:s + 1]).then_inc(S["o_ex"], 1)

            for t in range(T):
                if t:
                    act.wait_ge(S["conv_p"], TAPS)
                o_exp(t)
                for i in range(2, 6) if t else range(2):
                    act.wait_ge(S["o_tr"], i + 1)
                    act.copy(poT[:, i * C:(i + 1) * C], ps[:, i, :]).then_inc(S["o_tev"], 1)
            act.wait_ge(S["ct_bn"], T)
            act.activation(bsd[:], bn2[:, :, 1], ACT.Sqrt, bias=eps[:]).then_inc(S["ct_sd"], 1)
            for b in range(4):
                act.wait_ge(S["cb_tr"], b // 2 + 1)
                act.activation(cv[:, b, :], ps[:, 6 + b // 2, (b % 2) * SEQ:(b % 2 + 1) * SEQ], ACT.Silu,
                               bias=conv[:, b, TAPS + 2:TAPS + 3],
                               scale=conv[:, b, TAPS + 1:TAPS + 2]).then_inc(S["c_act"], 1)
            act.wait_ge(S["c_act"], 4)
            act.copy(o_hi[:, 0:4, :], cv[:]).then_inc(S["c_hi"], 1)
            for t in range(T):
                act.wait_ge(S["od_tr"], t + 1)
                act.copy(o_hi[:, 4:8, t * P:(t + 1) * P],
                         ps[:, 6 + t, :].rearrange("p (k s) -> p k s", k=4)).then_inc(S["od_hi"], 1)
            for g in range(G_OOUT, G_MOE):
                hi_static(g + RING)
            norm_std(3)
            act.wait_ge(S["xg"], 2 * T)
            act.wait_ge(n_rs[3], 1)
            for t in range(T):
                act.activation(h_all[:, t, :], h_all[:, t, :], ACT.Copy, scale=rstd[:, 3, t:t + 1]).then_inc(S["h_full"], 1)
            act.wait_ge(S["g_exp"], 1)
            for t in range(T):
                act.activation(gate[:, t, 1:2], gate[:, t, 0:1], ACT.Exp, scale=rstd[:, 3, t:t + 1]).then_inc(S["g_exp"], 1)

            def gather_hi(i, n):
                for r in range(4):
                    act.wait_ge(S["ga_mm"], 4 * i + (r + 1 if n == 2 else 4))
                    if r >= 2:
                        act.wait_ge(S["ga_lo"], 4 * i + (r - 1))
                    c0 = 0 if n == 2 else r // 2 * SEQ
                    act.copy(g_hi[:, 2 * r:2 * r + 2, 0:n * P],
                             ps[:, 2 + r % 2, c0:c0 + 2 * n * P].rearrange("p (k s) -> p k s", k=2)).then_inc(S["ga_hi"], 1)

            def step(j, u, n, packed):
                if not is_(j, LAST) or u + RING < JOB:
                    hi(gm(j, u + RING), (G_MOE + u + RING) % RAW, 16 * (JOB // RAW) * j + 16 * ((G_MOE + u + RING) // RAW + 1))
                if u == 3:
                    act.wait_ge(S["pt_mm"], j + 1)
                    act.copy(put_r[:], ps[:, 6, :].rearrange("p (n t s) -> p n t s", n=2, t=T)).then_inc(S["pt_ev"], 1)
                c = u // 4 if u < 4 * EC else EC
                if u % 4 == 1 and c <= EC and u <= 4 * EC + 1:
                    if c or not is_(j, 0):
                        act.wait_ge(S["e_tr"], EC * j + c)
                    if c < EC:
                        act.wait_ge(pe_half, gm(j, u + 1))
                        if packed:
                            act.copy(e_a[:, 1, :], ps[:, 1, :]).then_inc(S["e_raw"], 1)
                        else:
                            act.nop().then_inc(S["e_raw"], 1)
                        for t in range(n):
                            if packed and t:
                                act.wait_ge(S["e_fold"], EC * j + (c + 1))
                            last = act.activation(e_a[:, t, :], e_a[:, t, :] if packed and t else ps[:, t, :], ACT.Silu)
                        last.then_inc(S["e_silu"], 1)
                    if c:
                        b0 = 0 if c == EC else 4
                        for t in range(n):
                            last = act.copy(ea_hi[:, 4 * c - 4:4 * c, t * P:(t + 1) * P],
                                            ps[:, b0 + t, :].rearrange("p (k s) -> p k s", k=4))
                        last.then_inc(S["e_hi"], 1)

            def steps(j, us, n, packed):
                for u in us:
                    step(j, u, n, packed)

            def outputs_hi(j, n):
                for r in range(4):
                    t, c0, wd = TILE_OF(n, r), COL_OF(n, r), WIDE(n)
                    act.wait_ge(pe_half, gm(j, JOB))
                    if n == 1 and r >= 2:
                        act.wait_ge(S["y_lo_s"], 4 * j + (r - 1))
                    act.copy(out_piece(Y_HI, n, r), ps[:, (6, 4)[t] + c0 // C, c0 % C:c0 % C + wd]).then_inc(S["y_hi_s"], 1)

            act.wait_ge(S["route"], 1)
            many = many_of(act, 0)
            by_tiles(act, many, lambda n: gather_hi(0, n))
            by_form(act, many, lambda n, packed: steps(0, range(LEAD), n, packed))

            def expert(j, last):
                many = many_of(act, j)
                by_form(act, many, lambda n, packed: steps(j, range(LEAD, MID), n, packed))
                if not last:
                    many2 = many_of(act, j + 1)
                    by_tiles(act, many2, lambda n: gather_hi(j + 1, n))
                by_form(act, many, lambda n, packed: steps(j, range(MID, JOB), n, packed))
                by_tiles(act, many, lambda n: outputs_hi(j, n))
                if not last:
                    by_form(act, many2, lambda n, packed: steps(j + 1, range(LEAD), n, packed))

            each_expert(act, expert)
            norm_std(4)

        @block.vector
        def _(dve):
            chain = [0]

            def link(ins):
                chain[0] += 1
                ins.then_inc(S["dve_chain"], 1)
                dve.wait_ge(S["dve_chain"], chain[0])

            def lo(g, s):
                dve.wait_ge(hi_done, g + 1)
                r = s % RING
                dve.tensor_tensor(wlo[:, r, :], raw[:, s, :], whi[:, r, :].bitcast(F32),
                                  ALU.subtract).then_inc(lo_done, 1)

            def lo_static(g):
                lo(g, g % RAW)

            def norm_rs(n):
                dve.wait_ge(n_std[n], 1)
                ins = dve.reciprocal(rstd[:, n, :], std[:, n, :])
                if n in (0, 2):
                    link(ins)
                    ins = dve.tensor_scalar(rstd_q[:, n, :], rstd[:, n, :], HD ** -0.5, None, ALU.mult)
                if n < NORMS:
                    ins.then_inc(n_rs[n], 1)
                    dve.wait_ge(n_rs[n], 1)
                else:
                    link(ins)

            def norm_gain(n, bs=range(2 * T)):
                for b in bs:
                    dve.wait_ge(n_tr[n], b + 1)
                    h, _ = BLOCKS[b]
                    dve.tensor_tensor(FULL[n][:, b, :].rearrange("p (k s) -> p k s", k=4),
                                      ps[:, TURN_BANK[n][b], :].rearrange("p (k s) -> p k s", k=4),
                                      gains[:, n, 4 * h:4 * h + 4].unsqueeze(2).broadcast_to([P, 4, P]),
                                      ALU.mult).then_inc(n_full[n], 1)

            def norm_lo(n, bs=range(2 * T)):
                for b in bs:
                    dve.wait_ge(n_hi[n], b + 1)
                    h, t = BLOCKS[b]
                    tt = slice(t * P, (t + 1) * P)
                    dve.tensor_tensor(LO[n][:, 4 * h:4 * h + 4, tt], FULL[n][:, b, :].rearrange("p (k s) -> p k s", k=4),
                                      HI[n][:, 4 * h:4 * h + 4, tt].bitcast(F32), ALU.subtract).then_inc(n_lo[n], 1)

            dve.memset(eps[:], EPS).then_inc(S["eps_set"], 1)
            dve.wait_ge(S["gains_tr"], 1)
            dve.tensor_copy(gains[:].rearrange("p n k -> p (n k)"), ps[:, 0, 0:4 * KD]).then_inc(S["gains_ev"], 1)
            dve.wait_ge(S["gains_ev"], 1)
            norm_gain(0)
            norm_lo(0)
            for g in range(RING):
                lo_static(g)
            norm_rs(0)
            dve.wait_ge(S["cst2_in"], 16)
            dve.wait_ge(S["lam_ld"], 64)
            for i in range(2):
                if i:
                    dve.wait_ge(S["lam_sum"], i)
                dve.tensor_tensor_reduce(out=lam_j[:], in0=lam_in[:, 2 * i, :], in1=lam_in[:, 2 * i + 1, :],
                                         scale=1.0, scalar=0.0, op0=ALU.mult, op1=ALU.add,
                                         accum_out=lam_s[:, i:i + 1]).then_inc(S["lam_sum"], 1)

            def rope(part, t):
                v = proj[:, t, part * C:(part + 1) * C].rearrange("p (h a d) -> p h a d", a=2, d=HD // 2)
                a = rope_a[:].rearrange("p (h a d) -> p h a d", a=2, d=HD // 2)
                b = rope_b[:].rearrange("p (h a d) -> p h a d", a=2, d=HD // 2)
                cos = cst[:, K_COS + 32 * t:K_COS + 32 * (t + 1)].unsqueeze(1).broadcast_to([P, HEADS, 32])
                sin = cst[:, K_SIN + 32 * t:K_SIN + 32 * (t + 1)].unsqueeze(1).broadcast_to([P, HEADS, 32])
                dve.wait_ge(S["ip_ev"], T * part + t + 1)
                for i in range(2):
                    dve.tensor_tensor(a[:, :, i, :], v[:, :, i, :], cos, ALU.mult)
                    last = dve.tensor_tensor(b[:, :, i, :], v[:, :, 1 - i, :], sin, ALU.mult)
                link(last)
                dve.tensor_tensor(v[:, :, 0, :], a[:, :, 0, :], b[:, :, 0, :], ALU.subtract)
                last = dve.tensor_tensor(v[:, :, 1, :], a[:, :, 1, :], b[:, :, 1, :], ALU.add)
                link(last)

            for g in range(G_IN, G_OUT):
                lo_static(g + RING)
                if 4 <= g < 8:
                    rope(g % 2, (g - 4) // 2)
            dve.nop().then_inc(S["roped"], 1)
            for i in range(1, 8, 2):
                dve.wait_ge(S["at_tr"], i + 1)
                part, t = i // 2, i % 2
                dve.tensor_copy(qkT[:, 4 * part:4 * part + 4, t * P:(t + 1) * P],
                                ps[:, 4 + i % 4, :].rearrange("p (k s) -> p k s", k=4)).then_inc(S["at_ev_d"], 1)
            def a_max(t):
                dve.wait_ge(S["a_sc"], t + 1)
                src = ps[:, 0:2, :] if t == 0 else ps[:, 2:6, :]
                dve.tensor_reduce(a_nm[:, t, :], src.rearrange("p b (h k) -> p (b h) k", k=P * (t + 1)), AX, ALU.max,
                                  negate=True).then_inc(S["a_mx"], 1)

            def a_diff(t):
                n_k = P * (t + 1)
                off, offd = t * HEADS * P, t * A_HEADS * P
                dve.wait_ge(S["a_ex"], HEADS * (t + 1))
                link(dve.reciprocal(a_r[:, t, :], a_sum[:, t, :]))
                odd_r = a_r[:, t, A_HEADS:HEADS]
                link(dve.tensor_scalar(odd_r, odd_r, lam_s[:, 1:2], None, ALU.mult))
                p_of = lambda s: pa[:, off + s * n_k:off + (s + 1) * n_k]
                for h in range(A_HEADS):
                    last = dve.tensor_scalar(p_of(A_HEADS + h), p_of(A_HEADS + h), a_r[:, t, A_HEADS + h:A_HEADS + h + 1],
                                             None, ALU.mult)
                link(last)
                for h in range(A_HEADS):
                    dve.scalar_tensor_tensor(out=pd[:, offd + h * n_k:offd + (h + 1) * n_k], in0=p_of(h),
                                             scalar=a_r[:, t, h:h + 1], in1=p_of(A_HEADS + h),
                                             op0=ALU.mult, op1=ALU.subtract).then_inc(S["a_pd"], 1)

            a_max(0)
            dve.wait_ge(S["lam_exp"], 1)
            link(dve.tensor_tensor(lam_s[:, 0:1], lam_s[:, 2:3], lam_s[:, 3:4], ALU.subtract))
            link(dve.tensor_scalar(lam_s[:, 1:2], lam_s[:, 0:1], LAMBDA_INIT, None, ALU.add))
            a_max(1)
            a_diff(0)
            a_diff(1)
            def b_softplus(i):
                dve.wait_ge(S["b_ln"], i + 1)
                dve.scalar_tensor_tensor(out=sp[:, i, :], in0=z_of(i), scalar=0.0, in1=sp[:, i, :],
                                         op0=ALU.max, op1=ALU.add).then_inc(S["b_sp"], 1)

            def b_split(i):
                dve.wait_ge(S["b_sph"], i + 1)
                dve.tensor_tensor(sp_lo[:, i, :], sp[:, i, :], sp_hi[:, i, :].bitcast(F32),
                                  ALU.subtract).then_inc(S["b_spl"], 1)

            b_softplus(0)
            b_softplus(1)
            b_split(0)
            b_softplus(2)
            b_split(1)
            b_split(2)
            dve.wait_ge(S["sub_in"], 16)
            link(dve.tensor_scalar(subln[:], subln[:], 1.0 - LAMBDA_INIT, None, ALU.mult))
            dve.wait_ge(S["a_oev"], T)
            mv = mixed[:, :, 0:C].rearrange("p t (h d) -> p t h d", h=A_HEADS)
            dve.wait_ge(S["a_sqrt"], 1)
            link(dve.reciprocal(a_rs[:], a_sd[:]))
            for t in range(T):
                for h in range(A_HEADS):
                    last = dve.scalar_tensor_tensor(out=mv[:, t, h, :], in0=mv[:, t, h, :], scalar=a_rs[:, t, h:h + 1],
                                                    in1=subln[:], op0=ALU.mult, op1=ALU.mult)
            last.then_inc(S["a_done"], 1)
            for b, (h, t) in enumerate(BLOCKS):
                dve.wait_ge(S["mx_hi"], b + 1)
                tt = slice(t * P, (t + 1) * P)
                dve.tensor_tensor(e_lo[:, 4 * h:4 * h + 4, tt], ps[:, 4 + b, :].rearrange("p (k s) -> p k s", k=4),
                                  e_hi[:, 4 * h:4 * h + 4, tt].bitcast(F32), ALU.subtract).then_inc(S["mx_lo"], 1)

            def residual(n, banks, done):
                for t in range(T):
                    dve.tensor_tensor(x[:, t, n * C:(n + 1) * C], x[:, t, n * C:(n + 1) * C],
                                      ps[:, banks[t], :], ALU.add).then_inc(done, 1)

            def out_halves(g0, n_norm, done, more):
                lo_static(g0 + RING)
                lo_static(g0 + 1 + RING)
                dve.wait_ge(pe_half, g0 + 3)
                residual(0, (0, 1), done)
                norm_gain(n_norm, (0, 1))
                more(0)
                lo_static(g0 + 2 + RING)
                dve.wait_ge(pe_half, g0 + 4)
                residual(1, (2, 3), done)
                norm_gain(n_norm, (2, 3))
                more(1)
                lo_static(g0 + 3 + RING)
                norm_rs(n_norm)

            out_halves(G_OUT, 1, S["op_add"], lambda h: norm_lo(1, (2 * h, 2 * h + 1)))

            def f_lo_evac(c):
                nb = min(4, D_FF // P - 4 * c)
                for t in range(T):
                    dve.wait_ge(S["f_hi"], T * c + t + 1)
                    dst = (slice(4 * c, 4 * c + nb), slice(t * P, (t + 1) * P))
                    dve.tensor_tensor(fa_lo[:, dst[0], dst[1]],
                                      ps[:, 4 + t, 0:nb * P].rearrange("p (k s) -> p k s", k=nb),
                                      fa_hi[:, dst[0], dst[1]].bitcast(F32), ALU.subtract).then_inc(S["f_lo"], 1)

            for g in range(G_FFN, G_OIN - 1):
                lo_static(g + RING)
                q = g - G_FFN
                if (q < 4 * FFC and q % 4 == 1) or q == 4 * FFC:
                    c = q // 4
                    if c >= 1:
                        f_lo_evac(c - 1)
                if (q < 4 * FFC and q % 4 == 3) or q == 4 * FFC + 1:
                    c = q // 4
                    wd = C if c < FFC else D_FF - FFC * C
                    dve.wait_ge(pe_half, g + 1)
                    dve.wait_ge(S["f_silu"], T * (c + 1))
                    for t in range(T):
                        if c >= 1:
                            dve.wait_ge(S["f_tr"], T * (c - 1) + t + 1)
                        dve.scalar_tensor_tensor(out=f_a[:, t, 0:wd], in0=ps[:, 2 + t, 0:wd], scalar=rstd[:, 1, t:t + 1],
                                                 in1=f_s[:, t, 0:wd], op0=ALU.mult, op1=ALU.mult).then_inc(S["f_ufree"], 1)
                if q == 4 * FFC + 2:
                    f_lo_evac(FFC)
            dve.wait_ge(pe_half, G_OIN)
            for h in range(2):
                residual(h, ((0, 6), (1, 7))[h], S["f_add"])
                norm_gain(2, (2 * h, 2 * h + 1))
                norm_lo(2, (2 * h, 2 * h + 1))
            lo_static(G_OIN - 1 + RING)
            norm_rs(2)
            dve.wait_ge(S["rel_ld"], 16)
            dve.tensor_copy(rel_rev[:, 0:P - 1], rel_in[:, REL - 1:REL].broadcast_to([HEADS, P - 1])).then_inc(S["rel_rv"], 1)
            dve.tensor_copy(rel_rev[:, P - 1:P - 1 + REL], rel_in[:, ::-1]).then_inc(S["rel_rv"], 1)

            def o_divide(t):
                dve.wait_ge(S["o_ex"], HEADS * (t + 1))
                link(dve.reciprocal(o_r[:, t, :], o_sum[:, t, :]))
                dve.wait_ge(S["o_pv"], t + 1)
                for a in range(2):
                    last = dve.tensor_tensor(od[:, t, :].rearrange("p (h a d) -> p a h d", a=2, d=HD)[:, a],
                                             ps[:, O_OUT[t], :].rearrange("p (a h d) -> p a h d", a=2, d=HD)[:, a],
                                             o_r[:, t, 4 * a:4 * a + 4].unsqueeze(2).broadcast_to([P, 4, HD]),
                                             ALU.mult)
                last.then_inc(S["o_norm"], 1)

            def o_max(t):
                dve.wait_ge(S["o_sc"], t + 1)
                src = ps[:, 0:2, :] if t == 0 else ps[:, 2:6, :]
                dve.tensor_reduce(o_nm[:, t, :], src.rearrange("p b (h k) -> p (b h) k", k=P * (t + 1)), AX, ALU.max,
                                  negate=True).then_inc(S["o_mx"], 1)

            def taps(k0, k1):
                with dve.Fori(k0, k1) as k:
                    for b in range(3):
                        dve.wait_ge(S["conv_d"], k * 3 + (b - 2))
                        dve.scalar_tensor_tensor(out=cv[:, b, :], in0=uT[:, b, bass.ds(k, SEQ)],
                                                 scalar=conv[:, b, bass.ds(k, 1)], in1=cv[:, b, :],
                                                 op0=ALU.mult, op1=ALU.add).then_inc(S["conv_d"], 1)

            for g in range(G_OIN, G_OOUT - RING):
                lo_static(g + RING)
                q = g - G_OIN
                if q == 5:
                    dve.wait_ge(S["bias_in"], 16)
                    late = bias[P - CHUNK:P, :, SEQ - CHUNK:SEQ]
                    dve.tensor_scalar(late, late, NEG, None, ALU.add).then_inc(S["bias_m"], 1)
                if q == 3:
                    dve.memset(uT[:, :, 0:TAPS - 1], 0.0).then_inc(S["uz"], 1)
                    for t in range(T):
                        dve.wait_ge(S["oi_ev"], T + t + 1)
                        dve.tensor_tensor(oproj[:, t, 0:C], oproj[:, t, 0:C], oproj[:, t, C:2 * C],
                                          ALU.mult).then_inc(S["u_mul"], 1)
                if q == 4:
                    dve.wait_ge(S["cw_tr"], 1)
                    link(dve.tensor_copy(conv[:], ps[:, 6, 0:4 * (TAPS + 3)].rearrange("p (b n) -> p b n", b=4)))
                    for t in range(T):
                        dve.wait_ge(S["u_tr"], t + 1)
                        last = dve.tensor_copy(uT[:, :, TAPS - 1 + t * P:TAPS - 1 + (t + 1) * P],
                                               ps[:, 4 + t, :].rearrange("p (b s) -> p b s", b=4))
                        last.then_inc(S["u_ev"], 1)
                    conv_start(dve, range(3), S["conv_d"])
                if q >= 4:
                    taps(*TAP_CUT[q - 4:q - 2])
            dve.wait_ge(S["bias_h"], 1)
            dve.tensor_tensor(bias_lo[:], bias[:], bias_hi[:].bitcast(F32), ALU.subtract).then_inc(S["bias_l"], 1)
            taps(TAP_CUT[3], TAP_CUT[4])
            o_max(0)
            taps(TAP_CUT[4], TAP_CUT[5])
            o_max(1)
            taps(TAP_CUT[5], TAPS)
            o_divide(0)
            for t in range(T):
                dve.wait_ge(S["ct_tr"], t + 1)
                link(dve.bn_stats(bn6[:, t, :], ps[:, 6 + t, :]))
                dve.bn_aggr(bn2[:, t, :], bn6[:, t, :]).then_inc(S["ct_bn"], 1)
            dve.wait_ge(S["ct_sd"], 1)
            link(dve.reciprocal(brs[:], bsd[:]))
            for t in range(T):
                dve.tensor_scalar(cn[:, t, :], ps[:, 6 + t, :], bn2[:, t, 0:1], brs[:, t:t + 1],
                                  ALU.subtract, ALU.mult).then_inc(S["cn_done"], 1)
            lo_static(G_OOUT)
            dve.wait_ge(S["c_hi"], 1)
            dve.tensor_tensor(o_lo[:, 0:4, :], cv[:], o_hi[:, 0:4, :].bitcast(F32), ALU.subtract).then_inc(S["c_lo"], 1)
            o_divide(1)
            lo_static(G_OOUT + 1)
            for t in range(T):
                dve.wait_ge(S["od_hi"], t + 1)
                tt = slice(t * P, (t + 1) * P)
                dve.tensor_tensor(o_lo[:, 4:8, tt], ps[:, 6 + t, :].rearrange("p (k s) -> p k s", k=4),
                                  o_hi[:, 4:8, tt].bitcast(F32), ALU.subtract).then_inc(S["od_lo"], 1)
            lo_static(G_OOUT + 2)

            def gain_tokens(h):
                for t in range(T):
                    dve.wait_ge(S["oo_add"], 2 * h + t + 1)
                    dve.tensor_tensor(h_all[:, t, h * C:(h + 1) * C], x[:, t, h * C:(h + 1) * C],
                                      gain_row[:, h * C:(h + 1) * C], ALU.mult).then_inc(S["xg"], 1)

            dve.wait_ge(S["grow_in"], 16)
            out_halves(G_OOUT, 3, S["oo_add"], gain_tokens)
            dve.memset(slot[:], -1.0)
            dve.memset(over_f[:], 0.0)
            dve.wait_ge(S["r_mm"], 1)
            link(dve.tensor_copy(logit[:], ps[:, 0:T, 0:N_EXP]))
            for t in range(T):
                last = dve.max(top[:, t, :], logit[:, t, :])
            link(last)
            for t in range(T):
                last = dve.max_index(topi[:, t, :], top[:, t, :], logit[:, t, :])
            link(last)
            link(dve.tensor_copy(topf[:], topi[:]))
            dve.tensor_tensor(gate[:, :, 0], top[:, :, 1], top[:, :, 0], ALU.subtract).then_inc(S["g_exp"], 1)
            iota8 = kept[:, K_IOTA8:K_IOTA8 + 8]
            for t in range(T):
                for c in range(2):
                    last = dve.tensor_scalar(hot[:, t, c, :], iota8, topf[:, t, c:c + 1], None, ALU.is_equal)
            link(last)
            dve.tensor_tensor(sel[:], hot[:, :, 0, :], hot[:, :, 1, :], ALU.add).then_inc(S["sel_s"], 1)
            dve.wait_ge(S["cnt_mm"], 1)
            for t in range(T):
                last = dve.scalar_tensor_tensor(out=slot[:, t, 0:N_EXP], in0=ps[:, 2 + t, 0:N_EXP], scalar=1.0,
                                                in1=sel[:, t, :], op0=ALU.add, op1=ALU.mult)
            link(last)
            link(dve.tensor_scalar(slot[:, :, 0:N_EXP], slot[:, :, 0:N_EXP], -1.0, None, ALU.add))
            dve.tensor_scalar(over_f[:, N_EXP:2 * N_EXP], ps[:, 4, 0:N_EXP], float(P + H), None, ALU.is_gt)
            link(dve.tensor_scalar(over_f[:, 0:N_EXP], ps[:, 4, 0:N_EXP], float(P), None, ALU.is_gt))
            link(dve.tensor_tensor(over_f[:, 0:N_EXP], over_f[:, 0:N_EXP], over_f[:, N_EXP:2 * N_EXP], ALU.subtract))
            dve.tensor_copy(slot_b[:, :, N_EXP:N_EXP + 1], slot[:, :, N_EXP:N_EXP + 1])
            for t in range(T):
                last = dve.scalar_tensor_tensor(out=slot_b[:, t, 0:N_EXP], in0=over_f[:, 0:N_EXP], scalar=float(H),
                                                in1=slot[:, t, 0:N_EXP], op0=ALU.mult, op1=ALU.add)
            link(last)
            link(dve.scalar_tensor_tensor(out=over_f[:, 0:N_EXP], in0=over_f[:, N_EXP:2 * N_EXP], scalar=2.0,
                                          in1=over_f[:, 0:N_EXP], op0=ALU.mult, op1=ALU.add))
            link(dve.memset(over_f[:, N_EXP:2 * N_EXP], 0.0))
            link(dve.tensor_copy(over_i[:], over_f[:]))

            def make_pick(i):
                for t in range(T):
                    dve.tensor_scalar(pick[:, t, 0:P + H], kept[:, K_IOTA:K_IOTA + P + H], slot[:, t, bass.ds(i, 1)],
                                      None, ALU.is_equal)
                    last = dve.tensor_scalar(pick[:, t, P + H:SEQ], kept[:, K_IOTA + P + H:K_IOTA + SEQ],
                                             slot_b[:, t, bass.ds(i, 1)], None, ALU.is_equal)
                last.then_inc(S["pk"], 1)

            def gather_lo(i, n, packed):
                for r in range(4):
                    dve.wait_ge(S["ga_hi"], 4 * i + (r + 1))
                    c0 = 0 if n == 2 else r // 2 * SEQ
                    rs = slice(2 * r, 2 * r + 2)
                    got = ps[:, 2 + r % 2, c0:c0 + 2 * n * P].rearrange("p (k s) -> p k s", k=2)
                    if packed:
                        copy2 = g_hi[:, rs, P + H:SEQ]
                        dve.tensor_tensor(copy2, got[:, :, P + H:SEQ], copy2.bitcast(F32), ALU.subtract)
                    n_lo_ = P if packed else n * P
                    dve.tensor_tensor(g_lo[:, rs, 0:n_lo_], got[:, :, 0:n_lo_], g_hi[:, rs, 0:n_lo_].bitcast(F32),
                                      ALU.subtract).then_inc(S["ga_lo"], 1)

            def step(j, u, n, packed):
                if not is_(j, LAST) or u + RING < JOB:
                    lo(gm(j, u + RING), (G_MOE + u + RING) % RAW)
                c = u // 4 if u < 4 * EC else EC
                if u % 4 == 1 and c < EC:
                    if packed:
                        dve.wait_ge(S["e_raw"], EC * j + (c + 1))
                        for h in range(2):
                            own, other = slice(h * H, (h + 1) * H), slice((1 - h) * H, (2 - h) * H)
                            last = dve.tensor_tensor(e_a[own, 1, :], e_a[own, 1, :], ps[other, 1, :], ALU.add)
                        last.then_inc(S["e_fold"], 1)
                    else:
                        dve.nop().then_inc(S["e_fold"], 1)
                if u % 4 == 1 and c and u <= 4 * EC + 1:
                    dve.wait_ge(S["e_hi"], EC * j + c)
                    b0 = 0 if c == EC else 4
                    blk = slice(4 * c - 4, 4 * c)
                    if packed:
                        src = ps[:, b0 + 1, :].rearrange("p (k s) -> p k s", k=4)[:, :, H:P]
                        copy2 = ea_hi[:, blk, P + H:SEQ]
                        dve.tensor_tensor(copy2, src, copy2.bitcast(F32), ALU.subtract)
                    for t in range(1 if packed else n):
                        tt = slice(t * P, (t + 1) * P)
                        last = dve.tensor_tensor(ea_lo[:, blk, tt], ps[:, b0 + t, :].rearrange("p (k s) -> p k s", k=4),
                                                 ea_hi[:, blk, tt].bitcast(F32), ALU.subtract)
                    last.then_inc(S["e_lo"], 1)
                if u < 4 * EC and u % 4 == 3:
                    dve.wait_ge(pe_half, gm(j, u + 1))
                    dve.wait_ge(S["e_silu"], EC * j + (c + 1))
                    for t in range(n):
                        last = dve.tensor_tensor(e_a[:, t, :], ps[:, 2 + t, :], e_a[:, t, :], ALU.mult)
                    last.then_inc(S["e_ufree"], 1)
                if u == 8 and not is_(j, LAST):
                    dve.wait_ge(S["pt_mm"], j + 1)
                    make_pick(j + 1)

            def steps(j, us, n, packed):
                for u in us:
                    step(j, u, n, packed)

            def outputs_lo(j, n):
                for r in range(4):
                    t, c0, wd = TILE_OF(n, r), COL_OF(n, r), WIDE(n)
                    dve.wait_ge(S["y_hi_s"], 4 * j + (r + 1))
                    dve.tensor_tensor(out_piece(Y_LO, n, r), ps[:, (6, 4)[t] + c0 // C, c0 % C:c0 % C + wd],
                                      out_piece(Y_HI, n, r).bitcast(F32), ALU.subtract).then_inc(S["y_lo_s"], 1)
                for r in range(4 if n == 2 else 0):
                    add_piece(j, n, r)

            def add_piece(j, n, r):
                c0, wd = COL_OF(n, r), WIDE(n)
                for t in range(T):
                    dve.wait_ge(S["sc_mm"], 8 * j + (2 * r + t + 1 if n == 2 else 4 * (r // 2) + 4))
                    if n == 2 and r >= 2:
                        dve.wait_ge(S["sc_add"], 8 * j + (2 * r + t - 2))
                    bank, b0 = place(n, r)
                    dve.scalar_tensor_tensor(out=x[:, t, c0:c0 + wd], in0=ps[:, bank + t, b0:b0 + wd],
                                             scalar=comb[:, t, bass.ds(j, 1)], in1=x[:, t, c0:c0 + wd],
                                             op0=ALU.mult, op1=ALU.add).then_inc(S["sc_add"], 1)

            dve.drain().then_inc(S["sc_add"], 1)
            make_pick(0)
            dve.drain().then_inc(S["route"], 1)
            dve.wait_ge(S["route"], 1)
            dve.wait_ge(S["g_exp"], 1 + T)
            link(dve.tensor_scalar(gate[:, :, 2], gate[:, :, 1], 1.0, None, ALU.add))
            link(dve.reciprocal(gate[:, :, 3], gate[:, :, 2]))
            link(dve.tensor_tensor(gate[:, :, 2], gate[:, :, 1], gate[:, :, 3], ALU.mult))
            for t in range(T):
                last = dve.tensor_scalar(comb[:, t, 0:N_EXP], hot[:, t, 0, :], gate[:, t, 3:4], None, ALU.mult)
            link(last)
            for t in range(T):
                last = dve.scalar_tensor_tensor(out=comb[:, t, 0:N_EXP], in0=hot[:, t, 1, :], scalar=gate[:, t, 2:3],
                                                in1=comb[:, t, 0:N_EXP], op0=ALU.mult, op1=ALU.add)
            link(last)
            many = many_of(dve, 0)
            by_form(dve, many, lambda n, packed: gather_lo(0, n, packed))
            by_form(dve, many, lambda n, packed: steps(0, range(LEAD), n, packed))

            def expert(j, last):
                many = many_of(dve, j)
                by_form(dve, many, lambda n, packed: steps(j, range(LEAD, MID), n, packed))
                if not last:
                    many2 = many_of(dve, j + 1)
                    by_form(dve, many2, lambda n, packed: gather_lo(j + 1, n, packed))
                by_form(dve, many, lambda n, packed: steps(j, range(MID, JOB), n, packed))
                by_tiles(dve, many, lambda n: outputs_lo(j, n))
                if not last:
                    by_form(dve, many2, lambda n, packed: steps(j + 1, range(LEAD), n, packed))

                def add_rest(n):
                    if n == 2:
                        dve.nop()
                    for r in range(4 if n == 1 else 0):
                        add_piece(j, n, r)

                by_tiles(dve, many, add_rest)

            each_expert(dve, expert)
            dve.drain().then_inc(S["fin_n"], 1)
            dve.wait_ge(S["fin_n"], 1)
            for t in range(T):
                dve.tensor_tensor_reduce(out=fin_x[:, t, :], in0=x[:, t, :], in1=x[:, t, :], scale=1.0, scalar=0.0,
                                         op0=ALU.mult, op1=ALU.add, accum_out=ss[:, 4, t:t + 1]).then_inc(n_ss[4], 1)
            norm_rs(4)
            dve.wait_ge(S["fin_in"], 16)
            for t in range(T):
                dve.scalar_tensor_tensor(out=fin_x[:, t, :], in0=x[:, t, :], scalar=rstd[:, 4, t:t + 1], in1=h_all[:, 0, :],
                                         op0=ALU.mult, op1=ALU.mult).then_inc(S["final_ok"], 1)

        @block.gpsimd
        def _(pool):
            conv_start(pool, (POOL_BLOCK,), S["conv_p"])
            acc = cv[:, POOL_BLOCK, :]
            for k in range(1, TAPS):
                pool.wait_ge(S["tap_mul"], k)
                pool.wait_ge(S["conv_p"], k)
                pool.tensor_tensor(acc, acc, tap_out[:, k % TAP_RING, :], ALU.add).then_inc(S["conv_p"], 1)

        @block.tensor
        def _(pe):
            def mm3(dst, a_hi, a_lo, b_hi, b_lo, start, stop):
                pe.matmul(dst, a_hi, b_hi, start=start, stop=False)
                pe.matmul(dst, a_hi, b_lo, start=False, stop=False)
                return pe.matmul(dst, a_lo, b_hi, start=False, stop=stop)

            def product(dst, a_hi, a_lo, b_hi, b_lo, start, stop, packed):
                if not packed:
                    return mm3(dst, a_hi, a_lo, b_hi, b_lo, start, stop)
                pe.matmul(dst, a_hi, b_hi, start=start, stop=False)
                return pe.matmul(dst, a_hi, b_lo, start=False, stop=stop)

            def half_cols(g, r, a_hi, a_lo, k0, kn, banks, wd, start, stop, rows, packed=False,
                          between=None):
                pe.wait_ge(lo_done, g + 1)
                bh, bl = cols_view(whi[:, r, :], kn), cols_view(wlo[:, r, :], kn)
                for t, rs in enumerate(rows):
                    if t and between:
                        between()
                    for k in range(kn):
                        last = product(ps[:, banks[t], 0:wd], a_hi[:, k0 + k, rs], a_lo[:, k0 + k, rs], bh[:, k, :],
                                       bl[:, k, :], start and k == 0, stop and k == kn - 1, packed and t == 1)
                last.then_inc(pe_half, 1)

            def half_rows(g, r, a_hi, a_lo, b0, banks, first, final, rows, packed=False):
                pe.wait_ge(lo_done, g + 1)
                bh, bl = cols_view(whi[:, r, :], 2), cols_view(wlo[:, r, :], 2)
                for t, rs in enumerate(rows):
                    for k in range(2):
                        for h in range(2):
                            hs = slice(h * C, (h + 1) * C)
                            last = product(ps[:, banks[t][h], :], a_hi[:, b0 + k, rs], a_lo[:, b0 + k, rs],
                                           bh[:, k, hs], bl[:, k, hs], first and k == 0, final and k == 1,
                                           packed and t == 1)
                last.then_inc(pe_half, 1)

            BOTH = [slice(0, P), slice(P, SEQ)]

            def turn4(dst_bank, src_of, done, n=4):
                for i in range(n):
                    last = pe.transpose(ps[:, dst_bank, i * P:(i + 1) * P], src_of(i), ident)
                last.then_inc(done, 1)

            def keep_warm(n, bank):
                for _ in range(n):
                    pe.matmul(ps[:, bank, :], ident, kept[:, 0:C], start=True, stop=True)

            def norm_turn(n, bs=range(2 * T)):
                for b in bs:
                    h, t = BLOCKS[b]
                    if n:
                        pe.wait_ge(X_SUM[n], b + 1)
                    turn4(TURN_BANK[n][b], lambda i: x[:, t, (4 * h + i) * P:(4 * h + i + 1) * P], n_tr[n])

            pe.wait_ge(S["cst_in"], 16)
            pe.wait_ge(S["row_in"], 64)
            pe.transpose(ps[:, 0, 0:4 * KD], gains_row[:], ident[0:4 * KD, 0:4 * KD]).then_inc(S["gains_tr"], 1)
            pe.wait_ge(S["x_in"], 16)
            norm_turn(0)
            keep_warm(6, 1)
            pe.wait_ge(n_lo[0], 2 * T)
            pe.wait_ge(S["gains_ev"], 1)
            for g in range(G_IN, G_OUT):
                n = g // 2
                if g % 2 == 0 and n >= 2:
                    pe.wait_ge(S["ip_ev"], T * (n - 1))
                half_cols(g, g % RING, e_hi, e_lo, g % 2 * 4, 4, (2 * (n % 2), 2 * (n % 2) + 1), C,
                          g % 2 == 0, g % 2 == 1, BOTH)
            pe.wait_ge(S["cr_a"], 1)
            pe.wait_ge(S["cr_b"], 1)
            pe.wait_ge(S["roped"], 1)
            pe.wait_ge(S["ip_ev"], 6 * T)
            for i in range(8):
                part, t = i // 2, i % 2
                if i >= 4:
                    pe.wait_ge(S["at_ev_a"] if i % 2 == 0 else S["at_ev_d"], (i - 4) // 2 + 1)
                c0 = (0, C, 3 * C, 4 * C)[part]
                turn4(4 + i % 4, lambda b: proj[:, t, c0 + b * P:c0 + (b + 1) * P], S["at_tr"])
            pe.wait_ge(S["at_ev_a"], 4)
            pe.wait_ge(S["at_ev_d"], 4)

            def scores(t, kT, extra, done):
                n_k = P * (t + 1)
                per = C // n_k
                for b in range(HEADS // per):
                    bank = (0 if t == 0 else 2) + b
                    by_head = ps[:, bank, :].rearrange("p (h k) -> p h k", h=per)
                    if extra is None:
                        col = cst_r[0:1, K_COL + SEQ - n_k:K_COL + SEQ].unsqueeze(1).broadcast_to([1, per, n_k])
                        pe.matmul(by_head, cst_r[0:1, K_ROW:K_ROW + P], col, start=True, stop=True)
                    else:
                        for i, part in enumerate(extra):
                            pe.matmul(by_head, cst_r[:, K_FLIP:K_FLIP + P],
                                      part[:, PLACED[b * per]:PLACED[b * per + per - 1] + 1:2, SEQ - n_k:SEQ],
                                      start=i == 0, stop=True, skip_group_check=True)
                    for i in range(per):
                        s = PLACED[b * per + i]
                        half = slice((s % 2) * HD, (s % 2 + 1) * HD)
                        last = pe.matmul(ps[:, bank, i * n_k:(i + 1) * n_k], kT[half, s // 2, t * P:(t + 1) * P],
                                         kT[half, 4 + s // 2, 0:n_k], start=False, stop=True, skip_group_check=True)
                last.then_inc(done, 1)

            for t in range(T):
                scores(t, qkT, None, S["a_sc"])
            GROUPS = ((0, 0), (1, 1), (0, 1))

            def z_group(i):
                kb, qb = GROUPS[i]
                for b in range(2):
                    bank = Z_BANK[i] + b
                    if kb == qb:
                        pe.matmul(ps[:, bank, :].rearrange("p (h k) -> p h k", h=4), ident_r[:],
                                  cst_r[:, K_DMASK:K_DMASK + P].unsqueeze(1).broadcast_to([P, 4, P]),
                                  start=True, stop=True)
                    for j4 in range(4):
                        h = PLACED[4 * b + j4]
                        half = slice((h % 2) * HD, (h % 2 + 1) * HD)
                        last = pe.matmul(ps[:, bank, j4 * P:(j4 + 1) * P], qkT[half, 12 + h // 2, kb * P:(kb + 1) * P],
                                         qkT[half, 8 + h // 2, qb * P:(qb + 1) * P],
                                         start=kb != qb and j4 == 0, stop=True, skip_group_check=True)
                last.then_inc(S["b_z"], 1)

            def a_turn(i):
                t, kb = ((0, 0), (1, 0), (1, 1))[i]
                n_k = P * (t + 1)
                pe.wait_ge(S["a_pd"], A_HEADS * (t + 1))
                turn4(A_TURN[i], lambda h: pd[:, t * C + h * n_k + kb * P:t * C + h * n_k + (kb + 1) * P], S["a_tr"])

            z_group(0)
            pe.wait_ge(S["a_ex"], HEADS)
            z_group(1)
            pe.wait_ge(S["a_ex"], HEADS * T)
            z_group(2)
            a_turn(0)
            a_turn(1)
            pe.wait_ge(S["a_tev"], 1)
            a_turn(2)
            for t in range(T):
                pe.wait_ge(S["a_tev"], t + 2)
                for h in range(A_HEADS):
                    for kb in range(t + 1):
                        last = pe.matmul(ps[:, A_OUT[t], h * P:(h + 1) * P],
                                         pdT[:, (t + kb) * C + h * P:(t + kb) * C + (h + 1) * P],
                                         proj[:, kb, 2 * C + h * P:2 * C + (h + 1) * P], start=kb == 0, stop=kb == t)
                last.then_inc(S["a_pv"], 1)
            for i in range(3):
                pe.wait_ge(S["b_spl"], i + 1)
                for b in range(2):
                    dst, bc = ps[:, Z_BANK[i] + b, :], slice(b * C, (b + 1) * C)
                    for part in (sp_hi, sp_lo):
                        if i == 2:
                            pe.matmul(dst, cst_r[:, K_NONES:K_NONES + P], part[:, 1, bc],
                                      start=False, stop=True, skip_group_check=True)
                        last = pe.matmul(dst, cst_r[:, K_NTRI:K_NTRI + P], part[:, i, bc],
                                         start=False, stop=True, skip_group_check=True)
                last.then_inc(S["b_cum"], 1)
            def mixed_turn(h):
                for t in range(T):
                    turn4(4 + 2 * h + t, lambda i: mixed[:, t, (4 * h + i) * P:(4 * h + i + 1) * P], S["mx_tr"])

            for t in range(T):
                pe.wait_ge(S["b_w"], 1 if t == 0 else 3)
                for i, h in enumerate(PLACED):
                    vs = slice(5 * C + h * HD, 5 * C + (h + 1) * HD)
                    hs = slice(i * P, (i + 1) * P)
                    if t == 0:
                        last = pe.matmul(ps[:, 6, h * HD:(h + 1) * HD], wt[:, 0, hs], proj[:, 0, vs], start=True, stop=True)
                    else:
                        pe.matmul(ps[:, 7, h * HD:(h + 1) * HD], wt[:, 2, hs], proj[:, 0, vs], start=True, stop=False)
                        last = pe.matmul(ps[:, 7, h * HD:(h + 1) * HD], wt[:, 1, hs], proj[:, 1, vs], start=False, stop=True)
                last.then_inc(S["b_pv"], 1)
                if t == 0:
                    pe.wait_ge(S["a_done"], 1)
                    mixed_turn(0)

            def out_half(g0, q, a_hi, a_lo, between=None):
                half_cols(g0 + q, (g0 + q) % RING, a_hi, a_lo, q // 2 * 4, 4, (q % 2 * 2, q % 2 * 2 + 1), C,
                          q < 2, q >= 2, BOTH, between=between)

            pe.wait_ge(S["mx_lo"], T)
            out_half(G_OUT, 0, e_hi, e_lo)
            pe.wait_ge(S["b_ev"], T)
            mixed_turn(1)
            out_half(G_OUT, 1, e_hi, e_lo)
            pe.wait_ge(S["mx_lo"], 2 * T)
            out_half(G_OUT, 2, e_hi, e_lo)
            out_half(G_OUT, 3, e_hi, e_lo, lambda: norm_turn(1, (0, 1)))

            def f_turn(c):
                pe.wait_ge(S["f_ufree"], T * (c + 1))
                if c:
                    pe.wait_ge(S["f_lo"], T * c)
                for t in range(T):
                    turn4(4 + t, lambda i: f_a[:, t, i * P:(i + 1) * P], S["f_tr"], min(4, D_FF // P - 4 * c))

            for g in range(G_FFN, G_DOWN):
                q = g - G_FFN
                c = q // 4
                if q < 2:
                    pe.wait_ge(n_lo[1], 2 * (q + 1))
                if q < 4 * FFC:
                    up = q // 2 % 2
                    if q % 4 == 0 and c:
                        pe.wait_ge(S["f_silu"], T * c)
                    if q % 4 == 2 and c:
                        pe.wait_ge(S["f_ufree"], T * c)
                    half_cols(g, g % RING, f_hi, f_lo, q % 2 * 4, 4, (2 * up, 2 * up + 1), C, q % 2 == 0, q % 2 == 1,
                              BOTH, between=(lambda: norm_turn(1, (2, 3))) if q == 0 else None)
                    if q % 4 == 1 and c:
                        f_turn(c - 1)
                else:
                    up = q - 4 * FFC
                    pe.wait_ge(S["f_ufree" if up else "f_silu"], T * FFC)
                    half_cols(g, g % RING, f_hi, f_lo, 0, KD, (2 * up, 2 * up + 1), D_FF - FFC * C, True, True, BOTH)
                    if not up:
                        f_turn(FFC - 1)
            pe.wait_ge(S["f_silu"], T * (FFC + 1))
            NV = D_FF // 256
            for v in range(NV):
                g = G_DOWN + v
                c = v // 2
                pe.wait_ge(S["f_lo"], T * (c + 1))
                half_rows(g, g % RING, fa_hi, fa_lo, 2 * v, ((0, 1), (6, 7)), v == 0, v == NV - 1, BOTH)
                if v == 0:
                    f_turn(FFC)
            norm_turn(2, (0, 1))
            for g in range(G_OIN, G_OOUT):
                q = g - G_OIN
                if q < 2:
                    pe.wait_ge(n_lo[2], 2 * (q + 1))
                n = q // 2
                if q % 2 == 0 and n >= 2:
                    pe.wait_ge(S["oi_ev"], T * (n - 1))
                half_cols(g, g % RING, o_hi, o_lo, q % 2 * 4, 4, (2 * (n % 2), 2 * (n % 2) + 1), C, q % 2 == 0, q % 2 == 1,
                          BOTH, between=(lambda: norm_turn(2, (2, 3))) if q == 0 else None)
                if q == 4:
                    pe.wait_ge(S["crow_in"], 64)
                    for b in range(4):
                        last = pe.transpose(ps[:, 6, b * (TAPS + 3):(b + 1) * (TAPS + 3)],
                                            conv_row[:, b * P:(b + 1) * P], ident[0:TAPS + 3, 0:TAPS + 3])
                    last.then_inc(S["cw_tr"], 1)
                    for t in range(T):
                        pe.wait_ge(S["u_mul"], t + 1)
                        turn4(4 + t, lambda i: oproj[:, t, i * P:(i + 1) * P], S["u_tr"])
            keep_warm(3, 7)
            pe.wait_ge(S["oi_ev"], 5 * T)
            pe.wait_ge(S["u_ev"], T)
            for i in range(4):
                part, t = i // 2, i % 2
                turn4(4 + i, lambda b: oproj[:, t, (2 + part) * C + b * P:(2 + part) * C + (b + 1) * P], S["ot_tr"])
            keep_warm(1, 3)
            pe.wait_ge(S["ot_ev"], 4)
            pe.wait_ge(S["bias_l"], 1)
            for t in range(T):
                scores(t, oqkT, (bias_hi, bias_lo), S["o_sc"])
            OT = [(0, 0, 0), (0, 0, 4), (1, 0, 0), (1, 0, 4), (1, 1, 0), (1, 1, 4)]

            def o_turn(i):
                t, kb, h0 = OT[i]
                n_k = P * (t + 1)
                pe.wait_ge(S["o_ex"], HEADS * (t + 1))
                turn4(i, lambda h: po[:, t * D + (h0 + h) * n_k + kb * P:t * D + (h0 + h) * n_k + (kb + 1) * P], S["o_tr"])

            def o_values(t):
                pe.wait_ge(S["o_tev"], 6 if t else 2)
                for i, h in enumerate(PLACED):
                    for kb in range(t + 1):
                        last = pe.matmul(ps[:, O_OUT[t], i * HD:(i + 1) * HD],
                                         poT[:, ((t + kb) * HEADS + i) * P:((t + kb) * HEADS + i + 1) * P],
                                         oproj[:, kb, 4 * C + h * HD:4 * C + (h + 1) * HD],
                                         start=kb == 0, stop=kb == t)
                last.then_inc(S["o_pv"], 1)

            o_turn(0)
            o_turn(1)
            o_values(0)
            keep_warm(2, 7)
            for i in range(2, 6):
                o_turn(i)
            pe.wait_ge(S["conv_d"], 3 * TAPS)
            pe.wait_ge(S["conv_p"], TAPS)
            for t in range(T):
                turn4(6 + t, lambda i: cv[:, i, t * P:(t + 1) * P], S["ct_tr"])
            o_values(1)
            pe.wait_ge(S["cn_done"], T)
            for b2 in range(2):
                for b in range(2):
                    for t in range(T):
                        blk = 2 * b2 + b
                        last = pe.transpose(ps[:, 6 + b2, b * SEQ + t * P:b * SEQ + (t + 1) * P],
                                            cn[:, t, blk * P:(blk + 1) * P], ident)
                last.then_inc(S["cb_tr"], 1)
            keep_warm(2, 5)
            pe.wait_ge(S["c_lo"], 1)
            pe.wait_ge(S["o_norm"], 1)
            out_half(G_OOUT, 0, o_hi, o_lo)
            pe.wait_ge(S["c_act"], 4)
            for t in range(T):
                pe.wait_ge(S["o_norm"], t + 1)
                turn4(6 + t, lambda i: od[:, t, i * P:(i + 1) * P], S["od_tr"])
            out_half(G_OOUT, 1, o_hi, o_lo)
            pe.wait_ge(S["od_lo"], T)
            out_half(G_OOUT, 2, o_hi, o_lo)
            out_half(G_OOUT, 3, o_hi, o_lo, lambda: norm_turn(3, (0, 1)))
            pe.wait_ge(n_full[3], 2)
            keep_warm(2, 4)
            norm_turn(3, (2, 3))
            pe.wait_ge(S["router_in"], 16)
            for b, (h, t) in enumerate(BLOCKS):
                pe.wait_ge(n_full[3], b + 1)
                for k in range(4):
                    last = pe.matmul(ps[:, t, 0:N_EXP], m_full[:, b, k * P:(k + 1) * P], router[:, 4 * h + k, :],
                                     start=h == 0 and k == 0, stop=h == 1 and k == 3)
            last.then_inc(S["r_mm"], 1)
            pe.wait_ge(S["sel_s"], 1)
            lexc = cst[:, K_LEXC:K_LEXC + P]
            pe.matmul(ps[:, 2, 0:N_EXP], lexc, sel[:, 0, :], start=True, stop=True)
            pe.matmul(ps[:, 3, 0:N_EXP], ones, sel[:, 0, :], start=True, stop=False)
            pe.matmul(ps[:, 3, 0:N_EXP], lexc, sel[:, 1, :], start=False, stop=True)
            pe.matmul(ps[:, 4, 0:N_EXP], ones, sel[:, 0, :], start=True, stop=False)
            pe.matmul(ps[:, 4, 0:N_EXP], ones, sel[:, 1, :], start=False, stop=True).then_inc(S["cnt_mm"], 1)

            def gather(i, n):
                pe.wait_ge(S["pk"], i + 1)
                for r in range(4):
                    if n == 2 and r >= 2:
                        pe.wait_ge(S["ga_lo"], 4 * i + (r - 1))
                    c0 = 0 if n == 2 else r // 2 * SEQ
                    for c in range(2):
                        for t in range(T):
                            last = pe.matmul(ps[:, 2 + r % 2, c0 + c * n * P:c0 + (c + 1) * n * P],
                                             h_all[:, t, (2 * r + c) * P:(2 * r + c + 1) * P], pick[:, t, 0:n * P],
                                             start=t == 0, stop=t == T - 1)
                    last.then_inc(S["ga_mm"], 1)

            def halves(j, us, n, packed):
                rows = [slice(t * P, (t + 1) * P) for t in range(n)]
                for u in us:
                    g, r = gm(j, u), (G_MOE + u) % RING
                    c, up = u // 4, u // 2 % 2
                    if u < 4 * EC:
                        if u % 4 == 0 and c:
                            pe.wait_ge(S["e_silu"], EC * j + c)
                        if u % 4 == 2 and c:
                            pe.wait_ge(S["e_ufree"], EC * j + c)
                        half_cols(g, r, g_hi, g_lo, u % 2 * 4, 4, (2 * up, 2 * up + 1), C, u % 2 == 0, u % 2 == 1,
                                  rows, packed)
                    else:
                        v = u - 4 * EC
                        pe.wait_ge(S["e_lo"], EC * j + (max(v // 2 + 1, EC - 1) if v == 0 else v // 2 + 1))
                        half_rows(g, r, ea_hi, ea_lo, 2 * v, ((6, 7), (4, 5)), v == 0, v == 2 * EC - 1, rows, packed)
                    if u == 3:
                        pe.wait_ge(S["sc_add"], 8 * j + 1)
                        for n_ in range(2):
                            for t in range(T):
                                last = pe.transpose(ps[:, 6, (n_ * T + t) * P:(n_ * T + t + 1) * P],
                                                    pick[:, t, n_ * P:(n_ + 1) * P], ident)
                        last.then_inc(S["pt_mm"], 1)
                    if u % 4 == 1 and (4 < u < 4 * EC or u == 4 * EC + 1):
                        c = min(c, EC)
                        pe.wait_ge(S["e_ufree"], EC * j + c)
                        if c > 1:
                            pe.wait_ge(S["e_lo"], EC * j + (c - 1))
                        for t in range(n):
                            for i in range(4):
                                dst = ps[:, (0 if c == EC else 4) + t, i * P:(i + 1) * P]
                                block_in = e_a[:, t, i * P:(i + 1) * P]
                                if packed and t:
                                    last = pe.matmul(dst, block_in, kept[:, K_FOLD:K_FOLD + P], start=True, stop=True)
                                else:
                                    last = pe.transpose(dst, block_in, ident)
                        last.then_inc(S["e_tr"], 1)

            def scatter(j, n):
                pe.wait_ge(S["pt_ev"], j + 1)
                for r in range(4):
                    tile, c0, wd = TILE_OF(n, r), COL_OF(n, r), WIDE(n)
                    bank, b0 = place(n, r)
                    pe.wait_ge(S["y_lo_s"], 4 * j + (4 if n == 2 or r >= 2 else r + 1))
                    if n == 2 and r == 3:
                        pe.wait_ge(S["sc_add"], 8 * j + 5)
                    for t in range(T):
                        dst, put = ps[:, bank + t, b0:b0 + wd], put_r[:, tile, t, :]
                        pe.matmul(dst, put, out_piece(Y_HI, n, r), start=True, stop=False)
                        pe.matmul(dst, put, out_piece(Y_LO, n, r), start=False, stop=True).then_inc(S["sc_mm"], 1)
                if n == 2:
                    pe.wait_ge(S["sc_add"], 8 * j + 3)

            keep_warm(2, 5)
            pe.wait_ge(S["h_full"], T)
            pe.wait_ge(S["route"], 1)
            many = many_of(pe, 0)
            by_tiles(pe, many, lambda n: gather(0, n))
            keep_warm(2, 5)
            pe.wait_ge(S["ga_lo"], 4)
            by_form(pe, many, lambda n, packed: halves(0, range(LEAD), n, packed))

            def expert(j, last):
                many = many_of(pe, j)
                by_form(pe, many, lambda n, packed: halves(j, range(LEAD, MID), n, packed))
                if not last:
                    many2 = many_of(pe, j + 1)
                    pe.wait_ge(S["e_ufree"], EC * j + EC)
                    by_tiles(pe, many2, lambda n: gather(j + 1, n))
                by_form(pe, many, lambda n, packed: halves(j, range(MID, JOB), n, packed))
                if not last:
                    pe.wait_ge(S["ga_lo"], 4 * j + 8)
                    by_form(pe, many2, lambda n, packed: halves(j + 1, range(LEAD), n, packed))
                by_tiles(pe, many, lambda n: scatter(j, n))

            each_expert(pe, expert)


_INS = ['x', 'ev_norm_mix', 'ev_w_in', 'ev_lambda_q1', 'ev_lambda_k1', 'ev_lambda_q2', 'ev_lambda_k2',
        'ev_subln', 'ev_w_out', 'ev_norm_ffn', 'ev_ffn_gate', 'ev_ffn_up', 'ev_ffn_down',
        'od_norm_mix', 'od_w_in', 'od_conv_w', 'od_conv_b', 'od_conv_ln_g', 'od_conv_ln_b', 'od_rel_bias',
        'od_w_out', 'od_norm_ffn', 'od_router', 'od_exp_gate', 'od_exp_up', 'od_exp_down', 'final_norm']


def kernel(**inputs):
    import numpy as _np
    import concourse.bacc as _bacc
    from concourse import mybir as _mybir
    from concourse.bass_utils import run_bass_kernel_spmd as _run

    nc = _bacc.Bacc("TRN2", target_bir_lowering=False, num_devices=1)
    arrays, aps = {}, {}
    for name in _INS + ["cst"]:
        a = constants() if name == "cst" else _np.ascontiguousarray(inputs[name])
        arrays[f"in_{name}_dram"] = a
        aps[name] = nc.dram_tensor(f"in_{name}_dram", a.shape, _mybir.dt.from_np(a.dtype), kind="ExternalInput").ap()
    out = nc.dram_tensor("out_0_dram", (1, SEQ, D), _mybir.dt.float32, kind="ExternalOutput").ap()
    trunk(nc, aps, out)
    r = _run(nc, [arrays], core_ids=[0])
    return r.results[0]["out_0_dram"]
```
